# Optimizing a Trainium2 kernel written in Bass

```python
import math
import jax, jax.numpy as jnp
from jax import lax
import numpy as np

D_MODEL = 2048
BATCH = 1
SEQ = 256
DEPTH = 2

N_MIXERS = 2
POOL_WINDOWS = (2, 4, 8, 16)
N_POOL_GROUPS = 4
POOL_GROUP_DIM = D_MODEL // N_POOL_GROUPS
ATTN_PATTERNS = ((128, 1), (512, 4), (2048, 16))
N_ATTN_GROUPS = 3
HEAD_DIM = 128
N_SLOTS = 8
GROUP_WIDTH = N_SLOTS * HEAD_DIM
QKV_WIDTH = 3 * N_ATTN_GROUPS * GROUP_WIDTH
BLOCK = 128
N_TOTAL_HEADS = N_ATTN_GROUPS * N_SLOTS
D_FF = 4 * D_MODEL
LN_EPS = 1e-5
DEEPNORM_ALPHA = (2 * DEPTH) ** 0.25
DEEPNORM_BETA = (8 * DEPTH) ** -0.25
N_POOL_LAYERS = (DEPTH + 1) // 2
N_ATTN_LAYERS = DEPTH // 2


def layer_norm(x, g, b):
    xf = x.astype(jnp.float32)
    mu = jnp.mean(xf, axis=-1, keepdims=True)
    xc = xf - mu
    var = jnp.mean(xc * xc, axis=-1, keepdims=True)
    y = xc * lax.rsqrt(var + LN_EPS) * g.astype(jnp.float32) + b.astype(jnp.float32)
    return y.astype(x.dtype)

def alibi_slopes():
    n = N_TOTAL_HEADS
    return jnp.exp2(-8.0 * jnp.arange(1, n + 1, dtype=jnp.float32) / n).reshape(N_ATTN_GROUPS, N_SLOTS)

def pool_mixer(x, w_in, w_group, scale, w_out):
    B, S, D = x.shape
    u = (x @ w_in).reshape(B, S, N_POOL_GROUPS, POOL_GROUP_DIM)
    uf = u.astype(jnp.float32)
    cs = jnp.cumsum(uf, axis=1)
    t = jnp.arange(S)
    outs = []
    for g, w in enumerate(POOL_WINDOWS):
        c = cs[:, :, g]
        lagged = jnp.pad(c, ((0, 0), (w, 0), (0, 0)))[:, :S]
        cnt = jnp.minimum(t + 1, w).astype(jnp.float32)[:, None]
        outs.append((c - lagged) / cnt - uf[:, :, g])
    p = jnp.stack(outs, axis=2).astype(x.dtype)
    y = jnp.einsum('bsgc,gcd->bsgd', p, w_group).reshape(B, S, D) * scale
    return y @ w_out

def strided_window_attention(q, k, v, dil, n_back, slopes):
    B, S, H, E = q.shape
    L = S // dil
    nb = -(-L // BLOCK)
    Lp = nb * BLOCK
    N = B * dil

    def to_blocks(a):
        a = a.reshape(B, L, dil, H, E).transpose(0, 2, 1, 3, 4).reshape(N, L, H, E)
        a = jnp.pad(a, ((0, 0), (0, Lp - L), (0, 0), (0, 0)))
        return a.reshape(N, nb, BLOCK, H, E)

    def with_prev(a):
        prev = jnp.pad(a, ((0, 0), (1, 0), (0, 0), (0, 0), (0, 0)))[:, :nb]
        return jnp.concatenate([prev, a], axis=2)

    def from_blocks(a):
        rest = a.shape[3:]
        a = a.reshape((B, dil, Lp) + rest)[:, :, :L]
        a = jnp.moveaxis(a, 1, 2)
        return a.reshape((B, S) + rest)

    qb = to_blocks(q)
    kw = with_prev(to_blocks(k))
    vw = with_prev(to_blocks(v))
    s = jnp.einsum('nbqhe,nbkhe->nbhqk', qb, kw, preferred_element_type=jnp.float32)
    s = s * (1.0 / math.sqrt(E))
    qi = jnp.arange(BLOCK)[:, None]
    ki = jnp.arange(2 * BLOCK)[None, :]
    dist = qi + BLOCK - ki
    blk = jnp.arange(nb)[:, None, None]
    valid = ((dist >= 0) & (dist <= n_back))[None] & ((blk > 0) | (ki[None] >= BLOCK))
    bias = -slopes[:, None, None] * (dist * dil).astype(jnp.float32)[None]
    s = s + bias[None, None]
    s = jnp.where(valid[None, :, None], s, -jnp.inf)
    m = jnp.max(s, axis=-1, keepdims=True)
    e = jnp.exp(s - m)
    den = jnp.sum(e, axis=-1, keepdims=True)
    p = e / den
    lse = (m + jnp.log(den))[..., 0]
    o = jnp.einsum('nbhqk,nbkhe->nbqhe', p.astype(v.dtype), vw,
                   preferred_element_type=jnp.float32)
    return from_blocks(o), from_blocks(jnp.swapaxes(lse, 2, 3))

def dilated_attention(x, w_qkv, w_out):
    B, S, D = x.shape
    qkv = (x @ w_qkv).reshape(B, S, 3, N_ATTN_GROUPS, N_SLOTS, HEAD_DIM)
    slopes = alibi_slopes()
    outs, lses = [], []
    for g, (w, d) in enumerate(ATTN_PATTERNS):
        o, lse = strided_window_attention(qkv[:, :, 0, g], qkv[:, :, 1, g], qkv[:, :, 2, g],
                                          d, w // d, slopes[g])
        outs.append(o)
        lses.append(lse)
    wts = jax.nn.softmax(jnp.stack(lses, axis=0), axis=0)
    merged = jnp.einsum('gbsh,gbshe->bshe', wts, jnp.stack(outs, axis=0)).astype(x.dtype)
    return merged.reshape(B, S, GROUP_WIDTH) @ w_out

def sqrelu_mlp(x, w_up, w_down):
    h = jax.nn.relu(x @ w_up)
    return (h * h) @ w_down

def first_inputs(seed: int = 0) -> dict:
    key = jax.random.key(seed)
    ks = jax.random.split(key, 14)
    f32 = jnp.float32
    nrm = lambda k, shape, s: jax.random.normal(k, shape, f32) * s
    x = jax.random.normal(ks[0], (BATCH, SEQ, D_MODEL), f32)
    pool_w_in = nrm(ks[1], (N_POOL_LAYERS, D_MODEL, D_MODEL), D_MODEL ** -0.5)
    pool_w_group = nrm(ks[2], (N_POOL_LAYERS, N_POOL_GROUPS, POOL_GROUP_DIM, POOL_GROUP_DIM), POOL_GROUP_DIM ** -0.5)
    pool_scale = 1.0 + nrm(ks[3], (N_POOL_LAYERS, D_MODEL), 0.1)
    pool_w_out = nrm(ks[4], (N_POOL_LAYERS, D_MODEL, D_MODEL), DEEPNORM_BETA * D_MODEL ** -0.5)
    attn_w_qkv = nrm(ks[5], (N_ATTN_LAYERS, D_MODEL, QKV_WIDTH), D_MODEL ** -0.5)
    attn_w_out = nrm(ks[6], (N_ATTN_LAYERS, GROUP_WIDTH, D_MODEL), DEEPNORM_BETA * GROUP_WIDTH ** -0.5)
    mlp_w_up = nrm(ks[7], (DEPTH, D_MODEL, D_FF), D_MODEL ** -0.5)
    mlp_w_down = nrm(ks[8], (DEPTH, D_FF, D_MODEL), DEEPNORM_BETA * D_FF ** -0.5)
    ln_mix_g = 1.0 + nrm(ks[9], (DEPTH, D_MODEL), 0.05)
    ln_mix_b = nrm(ks[10], (DEPTH, D_MODEL), 0.02)
    ln_mlp_g = 1.0 + nrm(ks[11], (DEPTH, D_MODEL), 0.05)
    ln_mlp_b = nrm(ks[12], (DEPTH, D_MODEL), 0.02)
    return {"x": x, "pool_w_in": pool_w_in, "pool_w_group": pool_w_group, "pool_scale": pool_scale,
            "pool_w_out": pool_w_out, "attn_w_qkv": attn_w_qkv, "attn_w_out": attn_w_out,
            "mlp_w_up": mlp_w_up, "mlp_w_down": mlp_w_down, "ln_mix_g": ln_mix_g, "ln_mix_b": ln_mix_b,
            "ln_mlp_g": ln_mlp_g, "ln_mlp_b": ln_mlp_b}

def first_block(x, pool_w_in, pool_w_group, pool_scale, pool_w_out, attn_w_qkv, attn_w_out,
              mlp_w_up, mlp_w_down, ln_mix_g, ln_mix_b, ln_mlp_g, ln_mlp_b):
    for i in range(DEPTH):
        j = i // N_MIXERS
        if i % N_MIXERS == 0:
            h = pool_mixer(x, pool_w_in[j], pool_w_group[j], pool_scale[j], pool_w_out[j])
        else:
            h = dilated_attention(x, attn_w_qkv[j], attn_w_out[j])
        x = layer_norm(DEEPNORM_ALPHA * x + h, ln_mix_g[i], ln_mix_b[i])
        x = layer_norm(DEEPNORM_ALPHA * x + sqrelu_mlp(x, mlp_w_up[i], mlp_w_down[i]),
                       ln_mlp_g[i], ln_mlp_b[i])
    return x


DEPTH_2 = 1

MIX_WIDTH = D_MODEL
SSM_WIDTH = MIX_WIDTH // 2
SSM_GROUP = 16
SSM_GROUPS = SSM_WIDTH // SSM_GROUP
SSM_STATE = 64
DT_MIN = 1e-3
DT_MAX = 1e-1
QK_NOPE_DIM = 128
QK_ROPE_DIM = 64
V_HEAD_DIM = 128
MLA_WIDTH = MIX_WIDTH - SSM_WIDTH
MLA_HEADS = MLA_WIDTH // V_HEAD_DIM
Q_LORA_RANK = D_MODEL // 4
KV_LORA_RANK = D_MODEL // 8
ROPE_THETA = 10000.0
Q_BLOCK = 128
IN_WIDTH = SSM_WIDTH + Q_LORA_RANK + KV_LORA_RANK + QK_ROPE_DIM
D_FF_2 = ((8 * D_MODEL // 3 + 255) // 256) * 256
CONV_WIDTH = 3
RMS_EPS = 1e-6


def _rmsnorm(x, w):
    xf = x.astype(jnp.float32)
    y = xf * lax.rsqrt(jnp.mean(xf * xf, axis=-1, keepdims=True) + RMS_EPS)
    return (y * w.astype(jnp.float32)).astype(x.dtype)

def _rope_tables(positions, dtype):
    inv_freq = ROPE_THETA ** (-jnp.arange(0, QK_ROPE_DIM, 2, dtype=jnp.float32) / QK_ROPE_DIM)
    ang = positions.astype(jnp.float32)[..., None] * inv_freq
    return jnp.cos(ang).astype(dtype), jnp.sin(ang).astype(dtype)

def _rope(x, cos, sin):
    x1, x2 = jnp.split(x, 2, axis=-1)
    return jnp.concatenate([x1 * cos - x2 * sin, x1 * sin + x2 * cos], axis=-1)

def _ssm_combine(left, right):
    ar1, ai1, br1, bi1 = left
    ar2, ai2, br2, bi2 = right
    ar = ar2 * ar1 - ai2 * ai1
    ai = ar2 * ai1 + ai2 * ar1
    br = ar2 * br1 - ai2 * bi1 + br2
    bi = ar2 * bi1 + ai2 * br1 + bi2
    return ar, ai, br, bi

def _s5_group(u, lam_re, lam_im, log_dt, b_re, b_im, c_re, c_im, d_skip, w_glu, b_glu):
    bsz, seq, _ = u.shape
    ug = u.astype(jnp.float32).reshape(bsz, seq, SSM_GROUPS, SSM_GROUP)
    lr = lam_re.astype(jnp.float32)
    li = lam_im.astype(jnp.float32)
    dt = jnp.exp(log_dt.astype(jnp.float32))[:, None]
    mag = jnp.exp(lr * dt)
    abar_re = mag * jnp.cos(li * dt)
    abar_im = mag * jnp.sin(li * dt)
    nr, ni = abar_re - 1.0, abar_im
    den = lr * lr + li * li
    zr = (nr * lr + ni * li) / den
    zi = (ni * lr - nr * li) / den
    bre = b_re.astype(jnp.float32)
    bim = b_im.astype(jnp.float32)
    bbar_re = zr[..., None] * bre - zi[..., None] * bim
    bbar_im = zr[..., None] * bim + zi[..., None] * bre
    bu_re = jnp.einsum('blgh,gph->lbgp', ug, bbar_re)
    bu_im = jnp.einsum('blgh,gph->lbgp', ug, bbar_im)
    a_re = jnp.broadcast_to(abar_re, (seq, 1, SSM_GROUPS, SSM_STATE))
    a_im = jnp.broadcast_to(abar_im, (seq, 1, SSM_GROUPS, SSM_STATE))
    _, _, s_re, s_im = lax.associative_scan(_ssm_combine, (a_re, a_im, bu_re, bu_im), axis=0)
    y = (jnp.einsum('lbgp,ghp->blgh', s_re, c_re.astype(jnp.float32))
         - jnp.einsum('lbgp,ghp->blgh', s_im, c_im.astype(jnp.float32))
         + d_skip.astype(jnp.float32).reshape(SSM_GROUPS, SSM_GROUP) * ug)
    y = jax.nn.gelu(y.reshape(bsz, seq, SSM_WIDTH)).astype(u.dtype)
    return y * jax.nn.sigmoid(y @ w_glu + b_glu)

def _mla_group(c_q, c_kv, k_pe, positions, q_norm_w, w_uq, kv_norm_w, w_ukv):
    bsz, seq, _ = c_q.shape
    q = (_rmsnorm(c_q, q_norm_w) @ w_uq).reshape(bsz, seq, MLA_HEADS, QK_NOPE_DIM + QK_ROPE_DIM)
    q_nope, q_pe = q[..., :QK_NOPE_DIM], q[..., QK_NOPE_DIM:]
    kv = (_rmsnorm(c_kv, kv_norm_w) @ w_ukv).reshape(bsz, seq, MLA_HEADS, QK_NOPE_DIM + V_HEAD_DIM)
    k_nope, v = kv[..., :QK_NOPE_DIM], kv[..., QK_NOPE_DIM:]
    cos, sin = _rope_tables(positions, q.dtype)
    q_pe = _rope(q_pe, cos[:, :, None, :], sin[:, :, None, :])
    k_pe = _rope(k_pe, cos, sin)
    scale = (QK_NOPE_DIM + QK_ROPE_DIM) ** -0.5
    neg = jnp.finfo(jnp.float32).min
    outs = []
    for blk in range(seq // Q_BLOCK):
        q0 = blk * Q_BLOCK
        kend = q0 + Q_BLOCK
        s = (jnp.einsum('bqhd,bkhd->bhqk', q_nope[:, q0:kend], k_nope[:, :kend])
             + jnp.einsum('bqhr,bkr->bhqk', q_pe[:, q0:kend], k_pe[:, :kend]))
        s = s.astype(jnp.float32) * scale
        causal = jnp.arange(kend)[None, :] <= (q0 + jnp.arange(Q_BLOCK))[:, None]
        s = jnp.where(causal, s, neg)
        p = jax.nn.softmax(s, axis=-1).astype(v.dtype)
        outs.append(jnp.einsum('bhqk,bkhd->bqhd', p, v[:, :kend]))
    o = jnp.concatenate(outs, axis=1)
    return o.reshape(bsz, seq, MLA_WIDTH)

def _conv_ffn(h, w_up, conv_w, conv_b, w_down):
    a = h @ w_up
    a = lax.conv_general_dilated(a, conv_w[:, None, :], window_strides=(1,),
                                 padding=[(CONV_WIDTH - 1, 0)],
                                 dimension_numbers=('NWC', 'WIO', 'NWC'),
                                 feature_group_count=2 * D_FF_2) + conv_b
    gate, val = jnp.split(a, 2, axis=-1)
    return (jax.nn.silu(gate) * val) @ w_down

def second_inputs(seed: int = 0) -> dict:
    key = jax.random.key(seed)
    ks = jax.random.split(key, 32)
    f32 = jnp.float32

    def nrm(k, shape, scale):
        return jax.random.normal(k, (DEPTH_2,) + shape, f32) * scale

    def gain(k, n):
        return 1.0 + 0.02 * jax.random.normal(k, (DEPTH_2, n), f32)

    x = jax.random.normal(ks[0], (BATCH, SEQ, D_MODEL), f32)
    offs = jax.random.randint(ks[1], (BATCH, 1), 0, 1024, dtype=jnp.int32)
    positions = offs + jnp.arange(SEQ, dtype=jnp.int32)[None, :]
    lam_re = -0.5 + 0.01 * jax.random.normal(ks[4], (DEPTH_2, SSM_GROUPS, SSM_STATE), f32)
    lam_im = (math.pi * jnp.arange(SSM_STATE, dtype=f32))[None, None, :] + 0.01 * jax.random.normal(ks[5], (DEPTH_2, SSM_GROUPS, SSM_STATE), f32)
    log_dt = jax.random.uniform(ks[6], (DEPTH_2, SSM_GROUPS), f32, math.log(DT_MIN), math.log(DT_MAX))
    return {
        'x': x,
        'positions': positions,
        'attn_norm_w': gain(ks[2], D_MODEL),
        'w_in': nrm(ks[3], (D_MODEL, IN_WIDTH), D_MODEL ** -0.5),
        'ssm_lambda_re': lam_re,
        'ssm_lambda_im': lam_im,
        'ssm_log_dt': log_dt,
        'ssm_b_re': nrm(ks[7], (SSM_GROUPS, SSM_STATE, SSM_GROUP), (2 * SSM_GROUP) ** -0.5),
        'ssm_b_im': nrm(ks[8], (SSM_GROUPS, SSM_STATE, SSM_GROUP), (2 * SSM_GROUP) ** -0.5),
        'ssm_c_re': nrm(ks[9], (SSM_GROUPS, SSM_GROUP, SSM_STATE), (2 * SSM_STATE) ** -0.5),
        'ssm_c_im': nrm(ks[10], (SSM_GROUPS, SSM_GROUP, SSM_STATE), (2 * SSM_STATE) ** -0.5),
        'ssm_d': nrm(ks[11], (SSM_WIDTH,), 1.0),
        'ssm_w_glu': nrm(ks[12], (SSM_WIDTH, SSM_WIDTH), SSM_WIDTH ** -0.5),
        'ssm_b_glu': nrm(ks[13], (SSM_WIDTH,), 0.01),
        'mla_q_norm_w': gain(ks[14], Q_LORA_RANK),
        'mla_w_uq': nrm(ks[15], (Q_LORA_RANK, MLA_HEADS * (QK_NOPE_DIM + QK_ROPE_DIM)), Q_LORA_RANK ** -0.5),
        'mla_kv_norm_w': gain(ks[16], KV_LORA_RANK),
        'mla_w_ukv': nrm(ks[17], (KV_LORA_RANK, MLA_HEADS * (QK_NOPE_DIM + V_HEAD_DIM)), KV_LORA_RANK ** -0.5),
        'ssm_out_norm_w': gain(ks[18], SSM_WIDTH),
        'mla_out_norm_w': gain(ks[19], MLA_WIDTH),
        'w_out': nrm(ks[20], (MIX_WIDTH, D_MODEL), MIX_WIDTH ** -0.5),
        'ffn_norm_w': gain(ks[21], D_MODEL),
        'ffn_w_up': nrm(ks[22], (D_MODEL, 2 * D_FF_2), D_MODEL ** -0.5),
        'ffn_conv_w': nrm(ks[23], (CONV_WIDTH, 2 * D_FF_2), CONV_WIDTH ** -0.5),
        'ffn_conv_b': nrm(ks[24], (2 * D_FF_2,), 0.01),
        'ffn_w_down': nrm(ks[25], (D_FF_2, D_MODEL), D_FF_2 ** -0.5),
        'final_norm_w': 1.0 + 0.02 * jax.random.normal(ks[26], (D_MODEL,), f32),
    }

def second_block(x, positions, attn_norm_w, w_in, ssm_lambda_re, ssm_lambda_im, ssm_log_dt,
              ssm_b_re, ssm_b_im, ssm_c_re, ssm_c_im, ssm_d, ssm_w_glu, ssm_b_glu,
              mla_q_norm_w, mla_w_uq, mla_kv_norm_w, mla_w_ukv, ssm_out_norm_w,
              mla_out_norm_w, w_out, ffn_norm_w, ffn_w_up, ffn_conv_w, ffn_conv_b,
              ffn_w_down, final_norm_w):
    split_at = [SSM_WIDTH, SSM_WIDTH + Q_LORA_RANK, SSM_WIDTH + Q_LORA_RANK + KV_LORA_RANK]
    h = x
    for l in range(DEPTH_2):
        hn = _rmsnorm(h, attn_norm_w[l])
        proj = hn @ w_in[l]
        u, c_q, c_kv, k_pe = jnp.split(proj, split_at, axis=-1)
        y_ssm = _s5_group(u, ssm_lambda_re[l], ssm_lambda_im[l], ssm_log_dt[l],
                          ssm_b_re[l], ssm_b_im[l], ssm_c_re[l], ssm_c_im[l],
                          ssm_d[l], ssm_w_glu[l], ssm_b_glu[l])
        y_mla = _mla_group(c_q, c_kv, k_pe, positions, mla_q_norm_w[l], mla_w_uq[l],
                           mla_kv_norm_w[l], mla_w_ukv[l])
        y = jnp.concatenate([_rmsnorm(y_ssm, ssm_out_norm_w[l]),
                             _rmsnorm(y_mla, mla_out_norm_w[l])], axis=-1)
        h = h + y @ w_out[l]
        h = h + _conv_ffn(_rmsnorm(h, ffn_norm_w[l]), ffn_w_up[l], ffn_conv_w[l],
                          ffn_conv_b[l], ffn_w_down[l])
    return _rmsnorm(h, final_norm_w)


_first_inputs = second_inputs


def second_inputs(seed=0):
    import zlib

    import numpy as np

    out = dict(_first_inputs(seed))
    spreads = {}
    factors = {}
    for name, (base, spread) in spreads.items():
        noise = np.random.default_rng([zlib.crc32(name.encode()), seed]).standard_normal(out[name].shape)
        drawn = base * np.exp(spread * noise) if base else spread * noise
        out[name] = __import__('jax').numpy.asarray(drawn.astype(out[name].dtype))
    for name, factor in factors.items():
        out[name] = (out[name] * factor).astype(out[name].dtype)
    return out


_narrow_inputs = second_inputs


def second_inputs(seed=0):
    out = dict(_narrow_inputs(seed))
    wider = {'ssm_lambda_re': 12.0,
     'ssm_b_glu': 12.0,
     'mla_q_norm_w': 6.74,
     'mla_kv_norm_w': 4.09,
     'ssm_out_norm_w': 5.84,
     'mla_out_norm_w': 5.93,
     'ffn_norm_w': 5.41,
     'ffn_conv_b': 11.22,
     'final_norm_w': 3.27}
    for name, times in wider.items():
        mean = out[name].mean()
        out[name] = (mean + times * (out[name] - mean)).astype(out[name].dtype)
    return out


def setup_inputs(seed=0):
    out = dict(first_inputs(seed))
    for name, value in second_inputs(seed + 1).items():
        if name != "x":
            out[name + "_2"] = value
    return out


def reference(
    x, pool_w_in, pool_w_group, pool_scale, pool_w_out, attn_w_qkv, attn_w_out, mlp_w_up,
    mlp_w_down, ln_mix_g, ln_mix_b, ln_mlp_g, ln_mlp_b, positions_2, attn_norm_w_2, w_in_2,
    ssm_lambda_re_2, ssm_lambda_im_2, ssm_log_dt_2, ssm_b_re_2, ssm_b_im_2, ssm_c_re_2,
    ssm_c_im_2, ssm_d_2, ssm_w_glu_2, ssm_b_glu_2, mla_q_norm_w_2, mla_w_uq_2, mla_kv_norm_w_2,
    mla_w_ukv_2, ssm_out_norm_w_2, mla_out_norm_w_2, w_out_2, ffn_norm_w_2, ffn_w_up_2,
    ffn_conv_w_2, ffn_conv_b_2, ffn_w_down_2, final_norm_w_2,
):
    x = first_block(
        x, pool_w_in, pool_w_group, pool_scale, pool_w_out, attn_w_qkv, attn_w_out, mlp_w_up,
        mlp_w_down, ln_mix_g, ln_mix_b, ln_mlp_g, ln_mlp_b,
    )
    return second_block(
        x, positions_2, attn_norm_w_2, w_in_2, ssm_lambda_re_2, ssm_lambda_im_2, ssm_log_dt_2,
        ssm_b_re_2, ssm_b_im_2, ssm_c_re_2, ssm_c_im_2, ssm_d_2, ssm_w_glu_2, ssm_b_glu_2,
        mla_q_norm_w_2, mla_w_uq_2, mla_kv_norm_w_2, mla_w_ukv_2, ssm_out_norm_w_2,
        mla_out_norm_w_2, w_out_2, ffn_norm_w_2, ffn_w_up_2, ffn_conv_w_2, ffn_conv_b_2,
        ffn_w_down_2, final_norm_w_2,
    )


_drawn_inputs = setup_inputs


def setup_inputs(seed=0):
    import zlib

    import numpy as np

    out = dict(_drawn_inputs(seed))
    spreads = {}
    factors = {'attn_norm_w_2': 3.322,
     'ssm_lambda_re_2': 200.0,
     'ssm_lambda_im_2': 32.088,
     'ssm_log_dt_2': 35.856,
     'ssm_b_re_2': 44.576,
     'ssm_b_im_2': 45.088,
     'ssm_c_re_2': 44.448,
     'ssm_c_im_2': 44.68,
     'ssm_b_glu_2': 3.357}
    for name, (base, spread) in spreads.items():
        noise = np.random.default_rng([zlib.crc32(name.encode()), seed]).standard_normal(out[name].shape)
        drawn = base * np.exp(spread * noise) if base else spread * noise
        out[name] = __import__('jax').numpy.asarray(drawn.astype(out[name].dtype))
    for name, factor in factors.items():
        out[name] = (out[name] * factor).astype(out[name].dtype)
    return out
```

```python
from contextlib import ExitStack

import concourse.bass as bass
from concourse import mybir

F32 = mybir.dt.float32
F32R = mybir.dt.float32r
I32 = mybir.dt.int32
ALU = mybir.AluOpType
ACT = mybir.ActivationFunctionType
AX = mybir.AxisListType

P = 128
T = 256
D = 2048
DT = D // P
FF = 4 * D
FF2 = 5632
HID = 512
SLOTS = 4
CW = 2048
N_HEADS = 8
N_GROUPS = 3
HD = 128
ROPE = 64
ALPHA = 4.0 ** 0.25
LN_EPS = 1e-5
RMS_EPS = 1e-6
ATTN_SCALE = HD ** -0.5
MLA_SCALE = (HD + ROPE) ** -0.5
POOL_WINDOWS = (2, 4, 8, 16)
PAD = 16
SCAN = 16

STAGES = (("pool_in", 4), ("pool_group", 1), ("pool_out", 4), ("mlp0", 32), ("attn", 24), ("attn_out", 2),
          ("mlp1", 32), ("proj", 4), ("glu", 1), ("mla", 2), ("out2", 4), ("ffn", 33))
QUAD, N_QUADS = {}, 0
for _name, _n in STAGES:
    QUAD[_name] = N_QUADS
    N_QUADS += _n

BLOCK, _b = {}, 0
for _name, _n in (("pool_in", 4), ("pool_group", 4), ("pool_out", 4), ("mlp0", 16), ("attn_out", 4), ("mlp1", 16),
                  ("proj", 4), ("glu", 2), ("out2", 4), ("ffn", 22)):
    BLOCK[_name] = _b
    _b += _n
HIDDEN = {"mlp0": 0, "mlp1": FF // HID, "ffn": 2 * FF // HID}

FEATURES = (("pool_scale", DT), ("ln_mix_g", 2 * DT), ("ln_mix_b", 2 * DT), ("ln_mlp_g", 2 * DT), ("ln_mlp_b", 2 * DT),
            ("attn_norm_w_2", DT), ("ffn_norm_w_2", DT), ("final_norm_w_2", DT), ("ssm_d_2", 8), ("ssm_b_glu_2", 8),
            ("mla_q_norm_w_2", 4), ("mla_kv_norm_w_2", 2), ("ssm_out_norm_w_2", 8), ("mla_out_norm_w_2", 8),
            ("ffn_conv_w_2", 3 * 2 * FF2 // P), ("ffn_conv_b_2", 2 * FF2 // P))
FEAT, N_FEAT = {}, 0
for _name, _n in FEATURES:
    FEAT[_name] = N_FEAT
    N_FEAT += _n

CONSTS = (("ident", P), ("dist", 3 * 384), ("causal", 384), ("slope", 24), ("sel", ROPE), ("rot", ROPE),
          ("count", 4 * PAD), ("freq", 1), ("ln_eps", 1), ("rms_eps", 1))
CONST, N_CONST = {}, 0
for _name, _n in CONSTS:
    CONST[_name] = N_CONST
    N_CONST += _n

NORMS = (("mix0", 16, True), ("mlp0", 16, True), ("mix1", 16, True), ("mlp1", 16, True), ("attn2", 16, False),
         ("ssm", 8, False), ("q", 4, False), ("kv", 2, False), ("mla", 8, False), ("ffn2", 16, False), ("final", 16, False))
NORM = {n: i for i, (n, _, _) in enumerate(NORMS)}
NORM_TILES = {n: t for n, t, _ in NORMS}
PIECES = [max(1, t // 4) for _, t, _ in NORMS]
PIECE0 = [sum(PIECES[:i]) for i in range(len(PIECES))]
LO0 = [sum(p for (n, _, _), p in zip(NORMS[:i], PIECES) if n not in ("mlp1", "final")) for i in range(len(NORMS))]
ATTN_WIDTHS = (CW, CW, CW, 16)


class Steps:

    def __init__(self, eng, sem):
        self.eng, self.sem, self.n, self.it, self.per = eng, sem, 0, None, 0

    def __call__(self, ins):
        ins.then_inc(self.sem, 1)
        self.n += 1

    def settle(self):
        if self.it is None:
            self.eng.wait_ge(self.sem, self.n)
        else:
            self.eng.wait_ge(self.sem, self.it * self.per + self.n)

    def enter(self, it, per):
        self.it, self.per, self.start = it, per, self.n

    def leave(self, times):
        assert self.n - self.start == self.per, (self.n - self.start, self.per)
        self.it = None
        self.n = self.start + self.per * times


def build(nc, x_t, weights, ssm_blocks, features, consts, ssm_lam, positions, out):
    with ExitStack() as ctx:
        def sem(name):
            return ctx.enter_context(nc.semaphore(name))

        def sb(name, shape, dt=F32, scope=ctx):
            return scope.enter_context(nc.sbuf_tensor(name, shape, dt))

        raw = sb("raw", [P, SLOTS, CW])
        whi = sb("whi", [P, SLOTS, CW], F32R)
        wlo = sb("wlo", [P, SLOTS, CW], F32R)
        resid = sb("resid", [P, DT, T])
        feat = sb("feat", [P, N_FEAT])
        const = sb("const", [P, N_CONST])
        ones = sb("ones", [P, P])
        ones_mean = sb("ones_mean", [P, P])
        std = sb("std", [P, T])
        rstd = sb("rstd", [P, T])

        with ExitStack() as s:
            xhi = sb("xhi", [P, DT, T], F32R, s)
            xlo = sb("xlo", [P, DT, T], F32R, s)
        state = sb("state", [P, 2, 16, T])

        with ExitStack() as s:
            pool_hi = sb("pool_hi", [P, 2, 4, T], F32R, s)
            pool_lo = sb("pool_lo", [P, 2, 4, T], F32R, s)
        with ExitStack() as s:
            heads_hi = sb("heads_hi", [P, N_HEADS, T], F32R, s)
            heads_lo = sb("heads_lo", [P, N_HEADS, T], F32R, s)
        with ExitStack() as s:
            blocks = sb("blocks", [P, 4, 1024], F32, s)
        scratch = sb("scratch", [P, DT, T])

        with ExitStack() as s:
            u_pad = sb("u_pad", [P, 4, 4, PAD + T], F32, s)
            win_a = sb("win_a", [P, 4, PAD + T], F32, s)
            win_b = sb("win_b", [P, 4, PAD + T], F32, s)
        with ExitStack() as s:
            hid = sb("hid", [P, 4, T], F32, s)
            hid_hi = sb("hid_hi", [P, 4, T], F32R, s)
            hid_lo = sb("hid_lo", [P, 4, T], F32R, s)
            conv = sb("conv", [P, 8, T], F32, s)
            gate_sig = sb("gate_sig", [P, 4, T], F32, s)
        with ExitStack() as s:
            qk = sb("qk", [P, N_GROUPS, 2, T], F32, s)
            v_new = sb("v_new", [P, N_GROUPS, 2, HD], F32, s)
            v_cur = sb("v_cur", [P, N_GROUPS, 2, HD], F32, s)
            score = sb("score", [P, N_GROUPS, 384], F32, s)
            prob_t = sb("prob_t", [P, N_GROUPS, 384], F32, s)
            row_max = sb("row_max", [P, 2], F32, s)
            row_den = sb("row_den", [P, 2], F32, s)
        with ExitStack() as s:
            proj = sb("proj", [P, 15, T], F32, s)
            rope_cos = sb("rope_cos", [ROPE, T], F32, s)
            rope_sin = sb("rope_sin", [ROPE, T], F32, s)
            with ExitStack() as s2:
                lam = sb("lam", [P, 3, 32], F32, s2)
                par = sb("par", [P, 13, 32], F32, s2)
                pow_re = sb("pow_re", [P, 32, SCAN], F32, s2)
                pow_im = sb("pow_im", [P, 32, SCAN], F32, s2)
                scan_a = sb("scan_a", [P, 2, 16, 16], F32, s2)
                scan_b = sb("scan_b", [P, 2, 16, 16], F32, s2)
                bu_tmp = sb("bu_tmp", [P, 4, 2, T], F32, s2)
            pos_i = rope_cos[:].bitcast(I32)
            with ExitStack() as s2:
                cq_hi = sb("cq_hi", [P, 4, T], F32R, s2)
                cq_lo = sb("cq_lo", [P, 4, T], F32R, s2)
                ckv_hi = sb("ckv_hi", [P, 2, T], F32R, s2)
                ckv_lo = sb("ckv_lo", [P, 2, T], F32R, s2)
                k_rope = sb("k_rope", [ROPE, T], F32, s2)
                rope_a = sb("rope_a", [ROPE, T], F32, s2)
                m_max = sb("m_max", [P, 2], F32, s2)
                m_den = sb("m_den", [P, 2], F32, s2)

        ps = ctx.enter_context(nc.psum_tensor("ps", [P, 8, 512], F32))

        def half(bank, h):
            return ps[:, bank, h * T:(h + 1) * T]

        def block_ps(b):
            return ps[:, 2 * b:2 * b + 2, :].rearrange("p b (h t) -> p (b h) t", t=T)

        def wait_used(eng, q, s=SLOTS - 1):
            eng.wait_ge(chunk_used, q * SLOTS + (SLOTS + s + 1))

        def up_quad(q0, g, per):
            return q0 if isinstance(g, int) and g == 0 else g * per + (q0 - 1)

        def scratch_gelu(hf):
            return bu_tmp[:].rearrange("p a b t -> p (a b) t")[:, 0:4, :]

        def fcol(name, i):
            return feat[:, bass.ds(FEAT[name] + i, 1)]

        def ccol(name, a=0, n=None, rows=P):
            n = dict(CONSTS)[name] - a if n is None else n
            return const[0:rows, CONST[name] + a:CONST[name] + a + n]

        landed = [sem(f"landed{i}") for i in range(SLOTS)]
        hi_ready, lo_ready, chunk_used = sem("hi_ready"), sem("lo_ready"), sem("chunk_used")
        x_landed, table_landed, lam_landed, out_landed = sem("x_landed"), sem("table_landed"), sem("lam_landed"), sem("out_landed")
        ones_ready = sem("ones_ready")
        x_hi_ready, x_lo_ready, resid_ready = sem("x_hi_ready"), sem("x_lo_ready"), sem("resid_ready")
        block_free = sem("block_free")
        down_free = sem("down_free")
        hidden_ready, hidden_hi, hidden_lo = sem("hidden_ready"), sem("hidden_hi"), sem("hidden_lo")
        conv_start, conv_done, sig_ready = sem("conv_start"), sem("conv_done"), sem("sig_ready")
        u_ready, pad_ready, pooled, pooled_hi, pooled_lo = (sem(n) for n in ("u_ready", "pad_ready", "pooled", "pooled_hi", "pooled_lo"))
        y_scaled, y_hi, y_lo = sem("y_scaled"), sem("y_hi"), sem("y_lo")
        norm_src, norm_mean, norm_xc, norm_sq, norm_var, norm_std, norm_y, norm_hi, norm_lo = (
            sem(n) for n in ("norm_src", "norm_mean", "norm_xc", "norm_sq", "norm_var", "norm_std", "norm_y", "norm_hi", "norm_lo"))
        qkv_copied, v_ready = sem("qkv_copied"), sem("v_ready")
        scores_done, shift_ready, exp_done, prob_ready = sem("scores_done"), sem("shift_ready"), sem("exp_done"), sem("prob_ready")
        turned, turned_copied, head_done, head_hi, head_lo = (sem(n) for n in ("turned", "turned_copied", "head_done", "head_hi", "head_lo"))
        blocks_landed = [sem(f"blocks_landed{i}") for i in range(4)]
        angles_ready, trig_ready, table_ready = sem("angles_ready"), sem("trig_ready"), sem("table_ready")
        proj_copied, bu_done, bu_part, bu_ready, scan_done, y_done, y_ready = (
            sem(n) for n in ("proj_copied", "bu_done", "bu_part", "bu_ready", "scan_done", "y_done", "y_ready"))
        gelu_sq, gelu_arg, gelu_sig, gelu_ready, gelu_hi, gelu_lo, glu_sig = (
            sem(n) for n in ("gelu_sq", "gelu_arg", "gelu_sig", "gelu_ready", "gelu_hi", "gelu_lo", "glu_sig"))
        m_copied, rope_done, rope_ready, m_score, m_shift, m_exp, m_prob, m_turned, m_pt, m_out, m_out_copied = (
            sem(n) for n in ("m_copied", "rope_done", "rope_ready", "m_score", "m_shift", "m_exp", "m_prob",
                             "m_turned", "m_pt", "m_out", "m_out_copied"))
        act_steps, dve_steps, pool_steps = sem("act_steps"), sem("dve_steps"), sem("pool_steps")

        block = ctx.enter_context(nc.Block())

        @block.sync
        def _(sp):
            def load(q, s, width=CW):
                sp.wait_ge(lo_ready, q * SLOTS + (s + 1))
                sp.dma_start(raw[:, s, 0:width],
                             weights[bass.ds(q * SLOTS + s, 1), :, 0:width].rearrange("a p c -> p (a c)")).then_inc(landed[s], 16)

            with sp.Fori(0, QUAD["attn"]) as q:
                for s in range(SLOTS):
                    load(q, s)
            with sp.Fori(QUAD["attn"], QUAD["attn_out"]) as q:
                for s in range(SLOTS):
                    load(q, s, CW if s < 3 else 16)
            with sp.Fori(QUAD["attn_out"], N_QUADS) as q:
                for s in range(SLOTS):
                    load(q, s)
            for p in range(4):
                sp.wait_ge(norm_y, PIECE0[NORM["final"]] + p + 1)
                sp.dma_start(out.rearrange("(n p) t -> p n t", p=P)[:, 4 * p:4 * p + 4, :],
                             scratch[:, 4 * p:4 * p + 4, :]).then_inc(out_landed, 16)
            sp.wait_ge(out_landed, 64)

        @block.scalar
        def _(act):
            step = Steps(act, act_steps)

            def hi1(q, s, width=CW):
                act.wait_ge(landed[s], q * 16 + 16)
                act.wait_ge(chunk_used, q * SLOTS + (s + 1))
                act.activation(whi[:, s, 0:width], raw[:, s, 0:width], ACT.Copy).then_inc(hi_ready, 1)

            def hi4(q, widths=(CW,) * 4):
                for s in range(SLOTS):
                    hi1(q, s, widths[s])

            def norm(name, src, dst_hi=None, scale_resid=False):
                k = NORM[name]
                n, mean, t0 = NORMS[k][1], NORMS[k][2], PIECE0[k]
                w = min(4, n)
                off = DT - n
                if LO0[k]:
                    act.wait_ge(norm_lo, LO0[k])
                if not mean:
                    act.wait_ge(norm_src, k + 1)
                for p in range(PIECES[k]):
                    if mean:
                        act.wait_ge(norm_xc, t0 + p + 1)
                    act.activation(scratch[:, off + p * w:off + p * w + w, :], src[:, p * w:p * w + w, :],
                                   ACT.Square).then_inc(norm_sq, 1)
                act.wait_ge(norm_var, k + 1)
                act.activation(std[:], half(6, 0), ACT.Sqrt, scale=1.0 / (n * P),
                               bias=ccol("ln_eps" if mean else "rms_eps")).then_inc(norm_std, 1)
                if dst_hi is None:
                    return
                y = src if mean else scratch[:, off:DT, :]
                for p in range(PIECES[k]):
                    act.wait_ge(norm_y, t0 + p + 1)
                    act.activation(dst_hi[:, p * w:p * w + w, :], y[:, p * w:p * w + w, :], ACT.Copy).then_inc(norm_hi, 1)
                if scale_resid:
                    for p in range(PIECES[k]):
                        act.wait_ge(norm_lo, LO0[k] + p + 1)
                        act.mul(resid[:, 4 * p:4 * p + 4, :], resid[:, 4 * p:4 * p + 4, :], ALPHA).then_inc(resid_ready, 1)

            def mlp(name, next_quad, next_widths=(CW,) * 4):
                q0, b0, h0 = QUAD[name], BLOCK[name], HIDDEN[name]
                n = FF // HID

                def activate(g):
                    wait_used(act, up_quad(q0, g, 2))
                    if not (isinstance(g, int) and g + h0 == 0):
                        act.wait_ge(hidden_lo, g + h0)
                    act.activation(hid[:], block_ps(0), ACT.Relu).then_inc(block_free, 1)
                    act.wait_ge(block_free, g + (b0 + 3))
                    act.activation(hid[:], hid[:], ACT.Square).then_inc(hidden_ready, 1)

                def split(g):
                    act.wait_ge(hidden_ready, g + (h0 + 1))
                    if not (isinstance(g, int) and g == 0):
                        wait_used(act, g * 2 + q0)
                    act.activation(hid_hi[:], hid[:], ACT.Copy).then_inc(hidden_hi, 1)

                hi4(q0 + 1)
                activate(0)
                split(0)
                with act.Fori(0, n - 2) as g:
                    hi4(g * 2 + (q0 + 2))
                    activate(g + 1)
                    hi4(g * 2 + (q0 + 3))
                    split(g + 1)
                hi4(q0 + 2 * n - 2)
                activate(n - 1)
                hi4(q0 + 2 * n - 1)
                split(n - 1)
                hi4(next_quad, next_widths)

            act.dma_start(const[:], consts).then_inc(table_landed, 16)
            act.dma_start(feat[:], features).then_inc(table_landed, 16)
            xv = x_t.rearrange("(n p) t -> p n t", p=P)
            for p in range(4):
                act.dma_start(resid[:, 4 * p:4 * p + 4, :], xv[:, 4 * p:4 * p + 4, :]).then_inc(x_landed, 16)
            act.wait_ge(x_landed, 64)
            for p in range(4):
                act.activation(xhi[:, 4 * p:4 * p + 4, :], resid[:, 4 * p:4 * p + 4, :], ACT.Copy).then_inc(x_hi_ready, 1)
            hi4(0)
            for p in range(4):
                act.wait_ge(x_lo_ready, p + 1)
                act.mul(resid[:, 4 * p:4 * p + 4, :], resid[:, 4 * p:4 * p + 4, :], ALPHA).then_inc(resid_ready, 1)

            act.wait_ge(pad_ready, 1)

            def copy_u(b):
                wait_used(act, b)
                act.activation(u_pad[:, bass.ds(b, 1), :, PAD:PAD + T].rearrange("p a n t -> p (a n) t"),
                               block_ps(b % 2), ACT.Copy).then_inc(block_free, 1)
            for b in range(4):
                hi4(b + 1)
                copy_u(b)
            for g in range(4):
                act.wait_ge(pooled, g + 1)
                if g >= 2:
                    wait_used(act, QUAD["pool_group"], g - 2)
                act.activation(pool_hi[:, g % 2], win_a[:, :, PAD:PAD + T] if (4 - g) % 2 else win_b[:, :, PAD:PAD + T],
                               ACT.Copy).then_inc(pooled_hi, 1)
            for g in range(4):
                grp = 3 - g
                act.wait_ge(y_scaled, g + 1)
                act.activation(xhi[:, 4 * grp:4 * grp + 4, :], u_pad[:, g, :, PAD:PAD + T], ACT.Copy).then_inc(y_hi, 1)
            for b in range(4):
                hi4(QUAD["pool_out"] + b)
            hi4(QUAD["mlp0"])
            act.wait_ge(table_landed, 32)
            norm("mix0", resid, xhi, True)
            mlp("mlp0", QUAD["attn"], ATTN_WIDTHS)
            norm("mlp0", resid, xhi, True)

            def copy_qkv(n, g):
                wait_used(act, n + QUAD["attn"])
                ab = 2 * (g % 2)
                act.activation(qk[:, g], ps[:, ab, :].rearrange("p (a t) -> p a t", a=2), ACT.Copy)
                act.activation(v_new[:, g], ps[:, ab + 1, 0:2 * HD].rearrange("p (a t) -> p a t", a=2),
                               ACT.Copy).then_inc(qkv_copied, 1)

            def copy_turned(h):
                act.wait_ge(turned, h + 1)
                act.activation(prob_t[:], ps[:, 4:7, 0:384], ACT.Copy).then_inc(turned_copied, 1)

            def copy_head(h):
                act.wait_ge(head_done, h + 1)
                act.activation(heads_hi[:, bass.ds(h, 1), :].rearrange("p a t -> p (a t)"), half(7, 0), ACT.Copy).then_inc(head_hi, 1)

            def exps(h):
                act.activation(v_cur[:], v_new[:], ACT.Copy).then_inc(v_ready, 1)
                act.wait_ge(shift_ready, h + 1)
                act.activation(score[:, :, 0:128], score[:, :, 0:128], ACT.Exp, bias=row_max[:, 0:1], scale=ATTN_SCALE,
                               accum_out=row_den[:, 0:1])
                act.activation(score[:, :, 128:384], score[:, :, 128:384], ACT.Exp, bias=row_max[:, 1:2], scale=ATTN_SCALE,
                               accum_out=row_den[:, 1:2]).then_inc(exp_done, 1)

            def attn_head(h, first, last):
                q = h * 3 + QUAD["attn"]
                hi4(q + 1, ATTN_WIDTHS)
                if not first:
                    act.wait_ge(v_ready, h)
                copy_qkv(h * 3, 0)
                if not first:
                    copy_turned(h - 1)
                hi4(q + 2, ATTN_WIDTHS)
                copy_qkv(h * 3 + 1, 1)
                if not first:
                    copy_head(h - 1)
                hi4(q + 3, (CW,) * 4 if last else ATTN_WIDTHS)
                copy_qkv(h * 3 + 2, 2)
                act.wait_ge(qkv_copied, h * 3 + 3)
                exps(h)
            attn_head(0, True, False)
            with act.Fori(1, N_HEADS - 1) as h:
                attn_head(h, False, False)
            attn_head(N_HEADS - 1, False, True)
            copy_turned(N_HEADS - 1)
            copy_head(N_HEADS - 1)
            hi4(QUAD["attn_out"] + 1)
            hi4(QUAD["mlp1"])
            norm("mix1", resid, xhi, True)
            mlp("mlp1", QUAD["proj"])
            norm("mlp1", resid)
            norm("attn2", resid, xhi)

            hi4(QUAD["proj"] + 1)
            act.dma_start(lam[:], ssm_lam).then_inc(lam_landed, 16)
            act.dma_start(pos_i, positions.partition_broadcast(ROPE)).then_inc(lam_landed, 16)
            act.wait_ge(angles_ready, 1)
            act.activation(par[:, 0, :], lam[:, 2, :], ACT.Exp).then_inc(trig_ready, 1)
            act.wait_ge(angles_ready, 2)
            act.activation(par[:, 1, :], par[:, 1, :], ACT.Exp).then_inc(trig_ready, 1)
            act.wait_ge(angles_ready, 4)
            act.activation(par[:, 2, :], par[:, 2, :], ACT.Sin)
            act.activation(par[:, 3, :], par[:, 3, :], ACT.Sin).then_inc(trig_ready, 1)
            act.wait_ge(angles_ready, 6)
            act.activation(rope_sin[:], rope_sin[:], ACT.Sin)
            act.activation(rope_cos[:], rope_cos[:], ACT.Sin).then_inc(trig_ready, 1)
            for b in range(4):
                if b:
                    hi4(QUAD["proj"] + b + 1)
                wait_used(act, QUAD["proj"] + b)
                n = min(4, 15 - 4 * b)
                act.activation(proj[:, 4 * b:4 * b + n, :], block_ps(b % 2)[:, 0:n, :], ACT.Copy).then_inc(block_free, 1)

            for hf in range(2):
                for ci in range(4):
                    c = 4 * hf + ci
                    act.wait_ge(bu_done, c + 1)
                    if c == 0:
                        act.wait_ge(table_ready, 1)
                    if c == 4:
                        act.wait_ge(gelu_ready, 1)
                    if c >= 1:
                        act.wait_ge(bu_ready, c)
                    for st in range(4):
                        tile = 4 * c + st
                        src = ps[:, 4 * (ci % 2) + st, :].rearrange("p (r t) -> p r t", r=2)
                        act.activation(bu_tmp[:, st, 0, :], src[:, 1, :], ACT.Copy, scale=par[:, 9, tile:tile + 1])
                        act.activation(bu_tmp[:, st, 1, :], src[:, 0, :], ACT.Copy, scale=par[:, 8, tile:tile + 1]).then_inc(bu_part, 1)
                u = proj[:, 4 * hf:4 * hf + 4, :]
                act.wait_ge(y_ready, hf + 1)
                act.activation(scratch_gelu(hf), u, ACT.Square).then_inc(gelu_sq, 1)
                act.wait_ge(gelu_arg, hf + 1)
                act.activation(scratch_gelu(hf), scratch_gelu(hf), ACT.Sigmoid).then_inc(gelu_sig, 1)
            for hf in range(2):
                act.wait_ge(gelu_ready, 2)
                act.activation(xhi[:, 4 * hf:4 * hf + 4, :], proj[:, 4 * hf:4 * hf + 4, :], ACT.Copy).then_inc(gelu_hi, 1)
            for b in range(2):
                wait_used(act, QUAD["glu"], 2 * b + 1)
                for nt in range(4):
                    ins = act.activation(scratch[:, 4 * b + nt, :], block_ps(b)[:, nt, :], ACT.Sigmoid,
                                         bias=fcol("ssm_b_glu_2", 4 * b + nt))
                ins.then_inc(glu_sig, 1)
            hi4(QUAD["mla"])
            norm("ssm", proj[:, 0:8, :], xhi)
            norm("q", proj[:, 8:12, :], cq_hi)
            norm("kv", proj[:, 12:14, :], ckv_hi)

            def mla_head(h, q, s_slot):
                wait_used(act, q - 1, s_slot)
                act.activation(proj[:, 0:2, :], ps[:, 0, :].rearrange("p (a t) -> p a t", a=2), ACT.Copy)
                act.activation(proj[:, 2:4, :], ps[:, 1, :].rearrange("p (a t) -> p a t", a=2), ACT.Copy).then_inc(m_copied, 1)
                hi1(q, s_slot)
                act.wait_ge(m_shift, h + 1)
                s = proj[:, 5:7, :].rearrange("p a t -> p (a t)")
                act.activation(s[:, 0:128], s[:, 0:128], ACT.Exp, bias=m_max[:, 0:1], scale=MLA_SCALE, accum_out=m_den[:, 0:1])
                act.activation(s[:, 128:384], s[:, 128:384], ACT.Exp, bias=m_max[:, 1:2], scale=MLA_SCALE,
                               accum_out=m_den[:, 1:2]).then_inc(m_exp, 1)
                act.wait_ge(m_turned, h + 1)
                act.activation(proj[:, 7:9, :].rearrange("p a t -> p (a t)")[:, 0:384], ps[:, 4, 0:384], ACT.Copy).then_inc(m_pt, 1)
                act.wait_ge(m_out, h + 1)
                act.activation(scratch[:, bass.ds(h, 1), :].rearrange("p a t -> p (a t)"), half(5, 0), ACT.Copy).then_inc(m_out_copied, 1)
            with act.Fori(0, 2) as i:
                for s in range(SLOTS):
                    mla_head(i * 4 + s, i + (QUAD["mla"] + 1), s)
            act.wait_ge(m_out_copied, N_HEADS)
            act.sem_inc(norm_src, 1)
            norm("mla", scratch[:, 0:8, :], xhi[:, 8:16, :])
            for b in range(1, 4):
                hi4(QUAD["out2"] + b)
            hi4(QUAD["ffn"])
            norm("ffn2", resid, xhi)

            q0, b0, h0, n = QUAD["ffn"], BLOCK["ffn"], HIDDEN["ffn"], FF2 // HID

            def conv_first(g):
                for half_ in range(2):
                    wait_used(act, up_quad(q0, g, 3) + half_)
                    if not (isinstance(g, int) and g == 0):
                        act.wait_ge(hidden_ready, g + h0)
                    for nt in range(4):
                        i = g * 4 + (half_ * (FF2 // P) + nt)
                        ins = act.activation(conv[:, 4 * half_ + nt, :], block_ps(half_)[:, nt, :], ACT.Identity,
                                             scale=fcol("ffn_conv_w_2", i + 2 * (2 * FF2 // P)), bias=fcol("ffn_conv_b_2", i))
                    ins.then_inc(conv_start, 1)

            def gate(g):
                act.wait_ge(conv_done, g * 2 + 1)
                act.activation(gate_sig[:], conv[:, 0:4, :], ACT.Sigmoid).then_inc(sig_ready, 1)

            def ffn_split(g):
                act.wait_ge(hidden_ready, g + (h0 + 1))
                if not (isinstance(g, int) and g == 0):
                    wait_used(act, g * 3 + (q0 + 1))
                act.activation(hid_hi[:], hid[:], ACT.Copy).then_inc(hidden_hi, 1)
            hi4(q0 + 1)
            hi4(q0 + 2)
            conv_first(0)
            gate(0)
            hi4(q0 + 3)
            ffn_split(0)
            with act.Fori(0, n - 2) as g:
                hi4(g * 3 + (q0 + 4))
                conv_first(g + 1)
                gate(g + 1)
                hi4(g * 3 + (q0 + 5))
                ffn_split(g + 1)
                hi4(g * 3 + (q0 + 6))
            g = n - 2
            hi4(g * 3 + (q0 + 4))
            conv_first(g + 1)
            gate(g + 1)
            hi4(g * 3 + (q0 + 5))
            ffn_split(g + 1)
            norm("final", resid)

        @block.vector
        def _(dve):
            step = Steps(dve, dve_steps)

            def lo1(q, s, width=CW):
                dve.wait_ge(hi_ready, q * SLOTS + (s + 1))
                dve.tensor_tensor(wlo[:, s, 0:width], raw[:, s, 0:width], whi[:, s, 0:width].bitcast(F32),
                                  ALU.subtract).then_inc(lo_ready, 1)

            def lo4(q, widths=(CW,) * 4):
                for s in range(SLOTS):
                    lo1(q, s, widths[s])

            def lo4_add(q, q_down, widths=(CW,) * 4):
                for s in range(SLOTS):
                    lo1(q, s, widths[s])
                    add_down(q_down, s)

            def norm(name, src, gain, bias=None, dst_hi=None, dst_lo=None, next_src=False):
                k = NORM[name]
                n, mean, t0 = NORMS[k][1], NORMS[k][2], PIECE0[k]
                w = min(4, n)
                off = DT - n
                pieces = range(PIECES[k])
                y = src if mean else scratch[:, off:DT, :]
                if mean:
                    dve.wait_ge(norm_mean, k + 1)
                    for p in pieces:
                        s = src[:, p * w:p * w + w, :]
                        dve.tensor_tensor(s, s, half(7, 0).unsqueeze(1).to_broadcast([P, w, T]), ALU.subtract).then_inc(norm_xc, 1)
                dve.wait_ge(norm_std, k + 1)
                step(dve.reciprocal(rstd[:], std[:]))
                step.settle()

                def lo(p):
                    dve.wait_ge(norm_hi, LO0[k] + p + 1)
                    a = slice(p * w, p * w + w)
                    dve.tensor_tensor(dst_lo[:, a, :], y[:, a, :], dst_hi[:, a, :].bitcast(F32), ALU.subtract).then_inc(norm_lo, 1)
                for p in pieces:
                    if mean:
                        s = src[:, p * w:p * w + w, :]
                        step(dve.tensor_tensor(s, s, rstd[:].unsqueeze(1).to_broadcast([P, w, T]), ALU.mult))
                        step.settle()
                    for i in range(p * w, p * w + w):
                        if mean:
                            ins = dve.tensor_scalar(y[:, i, :], src[:, i, :], fcol(gain[0], gain[1] + i), fcol(bias[0], bias[1] + i),
                                                    ALU.mult, ALU.add)
                        else:
                            ins = dve.scalar_tensor_tensor(out=y[:, i, :], in0=src[:, i, :], scalar=fcol(gain[0], gain[1] + i),
                                                           in1=rstd[:], op0=ALU.mult, op1=ALU.mult)
                    ins.then_inc(norm_y, 1)
                    if dst_lo is not None and p >= 1:
                        lo(p - 1)
                if dst_lo is not None:
                    lo(PIECES[k] - 1)
                if next_src:
                    dve.wait_ge(norm_y, t0 + PIECES[k])
                    dve.sem_inc(norm_src, 1)

            def add_down(q, nb):
                wait_used(dve, q, nb)
                r = resid[:, 4 * nb:4 * nb + 4, :]
                return dve.tensor_tensor(r, r, block_ps(2 + nb % 2), ALU.add).then_inc(down_free, 1)

            def mlp(name, next_quad, next_widths=(CW,) * 4):
                q0, h0 = QUAD[name], HIDDEN[name]
                n = FF // HID

                def split(g):
                    dve.wait_ge(hidden_hi, g + (h0 + 1))
                    dve.tensor_tensor(hid_lo[:], hid[:], hid_hi[:].bitcast(F32), ALU.subtract).then_inc(hidden_lo, 1)

                lo4(q0 + 1)
                split(0)
                with dve.Fori(0, n - 2) as g:
                    lo4(g * 2 + (q0 + 2))
                    lo4_add(g * 2 + (q0 + 3), g * 2 + (q0 + 2))
                    split(g + 1)
                lo4(q0 + 2 * n - 2)
                lo4_add(q0 + 2 * n - 1, q0 + 2 * n - 2)
                split(n - 1)
                lo4_add(next_quad, q0 + 2 * n - 1, next_widths)
                dve.wait_ge(down_free, 4 * (h0 + n) + 2)
                dve.sem_inc(norm_src, 1)

            def add_block(b, nb, q, s=SLOTS - 1):
                wait_used(dve, q, s)
                r = resid[:, 4 * nb:4 * nb + 4, :]
                dve.tensor_tensor(r, r, block_ps(b % 2), ALU.add).then_inc(block_free, 1)

            dve.sem_inc(lo_ready, SLOTS)
            dve.memset(ones[:], 1.0)
            dve.memset(ones_mean[:], 1.0 / D).then_inc(ones_ready, 1)
            dve.memset(win_a[:, :, 0:PAD], 0.0)
            dve.memset(win_b[:, :, 0:PAD], 0.0)
            dve.memset(u_pad[:, :, :, 0:PAD].rearrange("p a n t -> p (a n) t"), 0.0).then_inc(pad_ready, 1)
            for p in range(4):
                a = slice(4 * p, 4 * p + 4)
                dve.wait_ge(x_hi_ready, p + 1)
                dve.tensor_tensor(xlo[:, a, :], resid[:, a, :], xhi[:, a, :].bitcast(F32), ALU.subtract).then_inc(x_lo_ready, 1)

            for q in range(QUAD["pool_out"]):
                lo4(q)
            for g in range(4):
                dve.wait_ge(pooled_hi, g + 1)
                res = win_a if (4 - g) % 2 else win_b
                dve.tensor_tensor(pool_lo[:, g % 2], res[:, :, PAD:PAD + T], pool_hi[:, g % 2].bitcast(F32),
                                  ALU.subtract).then_inc(pooled_lo, 1)
            dve.wait_ge(table_landed, 32)
            for g in range(4):
                grp = 3 - g
                b = BLOCK["pool_group"] + g
                wait_used(dve, QUAD["pool_group"], g)
                for nt in range(4):
                    ins = dve.tensor_scalar(u_pad[:, g, nt, PAD:PAD + T], block_ps(b % 2)[:, nt, :],
                                            fcol("pool_scale", 4 * grp + nt), None, ALU.mult)
                    if nt == 3:
                        ins.then_inc(y_scaled, 1)
                dve.wait_ge(y_hi, g + 1)
                dve.tensor_tensor(xlo[:, 4 * grp:4 * grp + 4, :], u_pad[:, g, :, PAD:PAD + T],
                                  xhi[:, 4 * grp:4 * grp + 4, :].bitcast(F32), ALU.subtract).then_inc(y_lo, 1)
                dve.sem_inc(block_free, 1)
            dve.wait_ge(resid_ready, 4)
            lo4(QUAD["pool_out"])
            for b in range(4):
                lo4(QUAD["pool_out"] + b + 1)
                add_block(BLOCK["pool_out"] + b, b, QUAD["pool_out"] + b)
            dve.wait_ge(block_free, 2 + BLOCK["mlp0"])
            dve.sem_inc(norm_src, 1)
            norm("mix0", resid, ("ln_mix_g", 0), ("ln_mix_b", 0), xhi, xlo)
            dve.wait_ge(resid_ready, 8)
            mlp("mlp0", QUAD["attn"], ATTN_WIDTHS)
            norm("mlp0", resid, ("ln_mlp_g", 0), ("ln_mlp_b", 0), xhi, xlo)

            def shift(h):
                dve.wait_ge(scores_done, h + 1)
                for g in range(N_GROUPS):
                    step(dve.scalar_tensor_tensor(
                        out=score[:, g, :], in0=ccol("dist", 384 * g, 384),
                        scalar=const[:, bass.ds(h + (CONST["slope"] + g * N_HEADS), 1)],
                        in1=ps[:, 4 + g, 0:384], op0=ALU.mult, op1=ALU.add))
                step.settle()
                step(dve.tensor_reduce(row_max[:, 0:1], score[:, :, 0:128], AX.XY, ALU.max))
                step(dve.tensor_reduce(row_max[:, 1:2], score[:, :, 128:384], AX.XY, ALU.max))
                step.settle()
                dve.tensor_scalar(row_max[:], row_max[:], -ATTN_SCALE, None, ALU.mult).then_inc(shift_ready, 1)
                dve.wait_ge(exp_done, h + 1)
                step(dve.reciprocal(row_den[:], row_den[:]))
                step.settle()
                dve.tensor_scalar(score[:, :, 0:128], score[:, :, 0:128], row_den[:, 0:1], None, ALU.mult)
                dve.tensor_scalar(score[:, :, 128:384], score[:, :, 128:384], row_den[:, 1:2], None, ALU.mult).then_inc(prob_ready, 1)

            def head_low(h):
                dve.wait_ge(head_hi, h + 1)
                dve.tensor_tensor(heads_lo[:, bass.ds(h, 1), :].rearrange("p a t -> p (a t)"), half(7, 0),
                                  heads_hi[:, bass.ds(h, 1), :].rearrange("p a t -> p (a t)").bitcast(F32), ALU.subtract).then_inc(head_lo, 1)

            def attn_head(h, first, last):
                q = h * 3 + QUAD["attn"]
                lo4(q + 1, ATTN_WIDTHS)
                lo4(q + 2, ATTN_WIDTHS)
                if not first:
                    head_low(h - 1)
                lo4(q + 3, (CW,) * 4 if last else ATTN_WIDTHS)
                shift(h)
            attn_head(0, True, False)
            with dve.Fori(0, N_HEADS - 2) as h:
                step.enter(h, 6)
                attn_head(h + 1, False, False)
                step.leave(N_HEADS - 2)
            attn_head(N_HEADS - 1, False, True)
            head_low(N_HEADS - 1)
            lo4(QUAD["attn_out"] + 1)
            dve.wait_ge(resid_ready, 12)
            b = BLOCK["attn_out"]
            add_block(b, 0, QUAD["attn_out"], 1)
            add_block(b + 1, 1, QUAD["attn_out"], 3)
            lo4(QUAD["mlp1"])
            add_block(b + 2, 2, QUAD["attn_out"] + 1, 1)
            add_block(b + 3, 3, QUAD["attn_out"] + 1, 3)
            dve.wait_ge(block_free, 2 + b + 4)
            dve.sem_inc(norm_src, 1)
            norm("mix1", resid, ("ln_mix_g", DT), ("ln_mix_b", DT), xhi, xlo)
            dve.wait_ge(resid_ready, 16)
            mlp("mlp1", QUAD["proj"])
            norm("mlp1", resid, ("ln_mlp_g", DT), ("ln_mlp_b", DT), next_src=True)
            norm("attn2", resid, ("attn_norm_w_2", 0), None, xhi, xlo)

            def op(out_, a, b_, o):
                step(dve.tensor_tensor(out_, a, b_, o))
                step.settle()

            def reduce_angle(out_, angle, tmp, quarter):
                def ts(o, a, s1, s2, o1, o2=ALU.bypass):
                    step(dve.tensor_scalar(o, a, s1, s2, o1, o2) if s2 is not None else dve.tensor_scalar(o, a, s1, None, o1))
                    step.settle()
                two_pi = 6.283185307179586
                c1 = 6.28125
                c2 = 0.0019350051879882812
                c3 = two_pi - c1 - c2
                magic = 12582912.0
                ts(tmp, angle, 1.0 / two_pi, 0.25 if quarter else 0.0, ALU.mult, ALU.add)
                ts(tmp, tmp, magic, None, ALU.add)
                ts(tmp, tmp, magic, None, ALU.subtract)
                for n, c in enumerate((c1, c2, c3)):
                    step(dve.scalar_tensor_tensor(out=out_, in0=tmp, scalar=-c, in1=angle if n == 0 else out_, op0=ALU.mult, op1=ALU.add))
                    step.settle()
                ts(out_, out_, two_pi / 4 if quarter else 0.0, 3.1415925, ALU.add, ALU.min)
                ts(out_, out_, -3.1415925, None, ALU.max)

            lo4(QUAD["proj"] + 1)
            dve.wait_ge(lam_landed, 32)
            dve.sem_inc(angles_ready, 1)
            lr, li = lam[:, 0, :], lam[:, 1, :]
            dve.wait_ge(trig_ready, 1)
            dt = par[:, 0, :]
            op(par[:, 1, :], lr, dt, ALU.mult)
            dve.sem_inc(angles_ready, 1)
            op(par[:, 4, :], li, dt, ALU.mult)
            reduce_angle(par[:, 2, :], par[:, 4, :], par[:, 5, :], False)
            dve.sem_inc(angles_ready, 1)
            reduce_angle(par[:, 3, :], par[:, 4, :], par[:, 5, :], True)
            dve.sem_inc(angles_ready, 1)
            rope_tmp, rope_angle = scan_a[0:ROPE, 0], scan_b[0:ROPE, 0]
            rope_tmp = rope_tmp.rearrange("p a b -> p (a b)")
            rope_angle = rope_angle.rearrange("p a b -> p (a b)")
            step(dve.tensor_copy(rope_angle, pos_i))
            step.settle()
            step(dve.tensor_scalar(rope_angle, rope_angle, ccol("freq", rows=ROPE), None, ALU.mult))
            step.settle()
            reduce_angle(rope_sin[:], rope_angle, rope_tmp, False)
            dve.sem_inc(angles_ready, 1)
            reduce_angle(rope_cos[:], rope_angle, rope_tmp, True)
            dve.sem_inc(angles_ready, 1)
            dve.wait_ge(trig_ready, 3)
            a_re, a_im, n_re, den, z_re, z_im, nz_im, na_im = (par[:, i, :] for i in (4, 5, 6, 10, 7, 8, 9, 11))
            tmp = par[:, 12, :]
            op(a_re, par[:, 1, :], par[:, 3, :], ALU.mult)
            op(a_im, par[:, 1, :], par[:, 2, :], ALU.mult)
            step(dve.tensor_scalar(n_re, a_re, 1.0, None, ALU.subtract))
            step.settle()
            op(den, lr, lr, ALU.mult)
            op(tmp, li, li, ALU.mult)
            op(den, den, tmp, ALU.add)
            op(z_re, n_re, lr, ALU.mult)
            op(tmp, a_im, li, ALU.mult)
            op(z_re, z_re, tmp, ALU.add)
            op(z_im, a_im, lr, ALU.mult)
            op(tmp, n_re, li, ALU.mult)
            op(z_im, z_im, tmp, ALU.subtract)
            step(dve.reciprocal(den, den))
            step.settle()
            op(z_re, z_re, den, ALU.mult)
            op(z_im, z_im, den, ALU.mult)
            step(dve.tensor_scalar(nz_im, z_im, -1.0, None, ALU.mult))
            step(dve.tensor_scalar(na_im, a_im, -1.0, None, ALU.mult))
            step(dve.tensor_copy(pow_re[:, :, 0], a_re))
            step(dve.tensor_copy(pow_im[:, :, 0], a_im))
            step.settle()
            for j in range(1, SCAN):
                op(pow_re[:, :, j], pow_re[:, :, j - 1], a_re, ALU.mult)
                op(tmp, pow_im[:, :, j - 1], a_im, ALU.mult)
                op(pow_re[:, :, j], pow_re[:, :, j], tmp, ALU.subtract)
                op(pow_im[:, :, j], pow_im[:, :, j - 1], a_re, ALU.mult)
                op(tmp, pow_re[:, :, j - 1], a_im, ALU.mult)
                op(pow_im[:, :, j], pow_im[:, :, j], tmp, ALU.add)
            dve.sem_inc(table_ready, 1)
            for b in range(1, 4):
                lo4(QUAD["proj"] + b + 1)

            sv = state[:].rearrange("p r s (b j) -> p r s b j", j=SCAN)
            for hf in range(2):
                for ci in range(4):
                    c = 4 * hf + ci
                    for st in range(4):
                        tile = 4 * c + st
                        dve.wait_ge(bu_part, 4 * c + st + 1)
                        src = ps[:, 4 * (ci % 2) + st, :].rearrange("p (r t) -> p r t", r=2)
                        zr = par[:, 7, tile:tile + 1]
                        dve.scalar_tensor_tensor(out=state[:, 0, 4 * ci + st, :], in0=src[:, 0, :], scalar=zr,
                                                 in1=bu_tmp[:, st, 0, :], op0=ALU.mult, op1=ALU.add)
                        ins = dve.scalar_tensor_tensor(out=state[:, 1, 4 * ci + st, :], in0=src[:, 1, :], scalar=zr,
                                                       in1=bu_tmp[:, st, 1, :], op0=ALU.mult, op1=ALU.add)
                    ins.then_inc(bu_ready, 1)
                dve.wait_ge(bu_ready, 4 * hf + 4)
                t16 = slice(16 * hf, 16 * hf + 16)

                def along(ap, n):
                    return ap.unsqueeze(2).to_broadcast([P, 16, n])
                ar2 = a_re[:, t16].unsqueeze(1).unsqueeze(3).to_broadcast([P, 2, 16, 16])
                with dve.Fori(0, SCAN - 1) as j:
                    step.enter(j, 5)
                    cur = sv[:, :, :, :, bass.ds(j + 1, 1)].rearrange("p r s b a -> p r s (b a)")
                    prev = sv[:, :, :, :, bass.ds(j, 1)].rearrange("p r s b a -> p r s (b a)")
                    step(dve.tensor_tensor(scan_a[:], prev, ar2, ALU.mult))
                    step(dve.tensor_tensor(scan_b[:, 0], prev[:, 1], along(na_im[:, t16], 16), ALU.mult))
                    step(dve.tensor_tensor(scan_b[:, 1], prev[:, 0], along(a_im[:, t16], 16), ALU.mult))
                    step.settle()
                    step(dve.tensor_tensor(scan_a[:], scan_a[:], scan_b[:], ALU.add))
                    step.settle()
                    step(dve.tensor_tensor(cur, cur, scan_a[:], ALU.add))
                    step.settle()
                    step.leave(SCAN - 1)
                pr16, pi16 = pow_re[:, t16, SCAN - 1], pow_im[:, t16, SCAN - 1]
                ends = sv[:, :, :, :, SCAN - 1]
                with dve.Fori(0, SCAN - 1) as b:
                    step.enter(b, 8)
                    cur = ends[:, :, :, bass.ds(b + 1, 1)].rearrange("p r s a -> p r (s a)")
                    prev = ends[:, :, :, bass.ds(b, 1)].rearrange("p r s a -> p r (s a)")
                    step(dve.tensor_tensor(scan_a[:, 0, 0], prev[:, 0], pr16, ALU.mult))
                    step(dve.tensor_tensor(scan_a[:, 0, 1], prev[:, 1], pi16, ALU.mult))
                    step(dve.tensor_tensor(scan_a[:, 0, 2], prev[:, 0], pi16, ALU.mult))
                    step(dve.tensor_tensor(scan_a[:, 0, 3], prev[:, 1], pr16, ALU.mult))
                    step.settle()
                    step(dve.tensor_tensor(scan_b[:, 0, 0], scan_a[:, 0, 0], scan_a[:, 0, 1], ALU.subtract))
                    step(dve.tensor_tensor(scan_b[:, 0, 1], scan_a[:, 0, 2], scan_a[:, 0, 3], ALU.add))
                    step.settle()
                    step(dve.tensor_tensor(cur[:, 0], cur[:, 0], scan_b[:, 0, 0], ALU.add))
                    step(dve.tensor_tensor(cur[:, 1], cur[:, 1], scan_b[:, 0, 1], ALU.add))
                    step.settle()
                    step.leave(SCAN - 1)
                f = bu_tmp[:].rearrange("p a b t -> p (a b t)")[:, 0:4 * 15 * 15].rearrange("p (s b j) -> p s b j", b=15, j=15)
                f2 = bu_tmp[:].rearrange("p a b t -> p (a b t)")[:, 1024:1024 + 900].rearrange("p (s b j) -> p s b j", b=15, j=15)
                for ci in range(4):
                    ss = slice(4 * ci, 4 * ci + 4)
                    tt = slice(16 * hf + 4 * ci, 16 * hf + 4 * ci + 4)

                    def powb(ap):
                        return ap[:, tt, 0:15].unsqueeze(2).to_broadcast([P, 4, 15, 15])

                    def carry(r):
                        return ends[:, r, ss, 0:15].unsqueeze(3).to_broadcast([P, 4, 15, 15])
                    for r, (pa, pb, o) in enumerate(((pow_re, pow_im, ALU.subtract), (pow_im, pow_re, ALU.add))):
                        tgt = sv[:, r, ss, 1:16, 0:15]
                        step(dve.tensor_tensor(f, powb(pa), carry(0), ALU.mult))
                        step(dve.tensor_tensor(f2, powb(pb), carry(1), ALU.mult))
                        step.settle()
                        step(dve.tensor_tensor(tgt, tgt, f, ALU.add))
                        step.settle()
                        step(dve.tensor_tensor(tgt, tgt, f2, o))
                        step.settle()
                    dve.sem_inc(scan_done, 1)
                for ci in range(4):
                    c = 4 * hf + ci
                    dve.wait_ge(y_done, c + 1)
                    step(dve.scalar_tensor_tensor(out=proj[:, c, :], in0=proj[:, c, :], scalar=fcol("ssm_d_2", c),
                                                  in1=half(ci, 0), op0=ALU.mult, op1=ALU.add))
                    step.settle()
                    step(dve.tensor_tensor(proj[:, c, :], proj[:, c, :], half(ci, 1), ALU.subtract))
                step.settle()
                dve.sem_inc(y_ready, 1)
                k = 2.0 * (2.0 / 3.141592653589793) ** 0.5
                u = proj[:, 4 * hf:4 * hf + 4, :]
                dve.wait_ge(gelu_sq, hf + 1)
                step(dve.tensor_scalar(scratch_gelu(hf), scratch_gelu(hf), 0.044715 * k, k, ALU.mult, ALU.add))
                step.settle()
                dve.tensor_tensor(scratch_gelu(hf), scratch_gelu(hf), u, ALU.mult).then_inc(gelu_arg, 1)
                dve.wait_ge(gelu_sig, hf + 1)
                dve.tensor_tensor(u, u, scratch_gelu(hf), ALU.mult).then_inc(gelu_ready, 1)
            for hf in range(2):
                a = slice(4 * hf, 4 * hf + 4)
                dve.wait_ge(gelu_hi, hf + 1)
                dve.tensor_tensor(xlo[:, a, :], proj[:, a, :], xhi[:, a, :].bitcast(F32), ALU.subtract).then_inc(gelu_lo, 1)
            lo4(QUAD["mla"])
            for b in range(2):
                a = slice(4 * b, 4 * b + 4)
                dve.wait_ge(glu_sig, b + 1)
                dve.tensor_tensor(proj[:, a, :], proj[:, a, :], scratch[:, a, :], ALU.mult).then_inc(block_free, 1)
            dve.wait_ge(block_free, 2 + BLOCK["out2"])
            dve.sem_inc(norm_src, 3)
            norm("ssm", proj[:, 0:8, :], ("ssm_out_norm_w_2", 0), None, xhi, xlo)
            norm("q", proj[:, 8:12, :], ("mla_q_norm_w_2", 0), None, cq_hi, cq_lo)
            norm("kv", proj[:, 12:14, :], ("mla_kv_norm_w_2", 0), None, ckv_hi, ckv_lo)

            def rope(n, dst):
                dve.wait_ge(rope_done, n + 1)
                step(dve.tensor_tensor(rope_a[:], ps[0:ROPE, 2, 0:T], rope_cos[:], ALU.mult))
                step(dve.tensor_tensor(dst, ps[0:ROPE, 2, T:2 * T], rope_sin[:], ALU.mult))
                step.settle()
                dve.tensor_tensor(dst, dst, rope_a[:], ALU.add).then_inc(rope_ready, 1)

            def mla_head(h, q, s_slot):
                lo1(q, s_slot)
                rope(h + 1, proj[0:ROPE, 4, :])
                s = proj[:, 5:7, :].rearrange("p a t -> p (a t)")
                dve.wait_ge(m_score, h + 1)
                step(dve.tensor_tensor(s[:, 0:384], ps[:, 3, 0:384], ccol("causal"), ALU.add))
                step.settle()
                step(dve.tensor_reduce(m_max[:, 0:1], s[:, 0:128], AX.X, ALU.max))
                step(dve.tensor_reduce(m_max[:, 1:2], s[:, 128:384], AX.X, ALU.max))
                step.settle()
                dve.tensor_scalar(m_max[:], m_max[:], -MLA_SCALE, None, ALU.mult).then_inc(m_shift, 1)
                dve.wait_ge(m_exp, h + 1)
                step(dve.reciprocal(m_den[:], m_den[:]))
                step.settle()
                dve.tensor_scalar(s[:, 0:128], s[:, 0:128], m_den[:, 0:1], None, ALU.mult)
                dve.tensor_scalar(s[:, 128:384], s[:, 128:384], m_den[:, 1:2], None, ALU.mult).then_inc(m_prob, 1)
            dve.wait_ge(trig_ready, 4)
            rope(0, k_rope[:])
            with dve.Fori(0, 2) as i:
                step.enter(i, SLOTS * 6)
                for s in range(SLOTS):
                    mla_head(i * 4 + s, i + (QUAD["mla"] + 1), s)
                step.leave(2)
            norm("mla", scratch[:, 0:8, :], ("mla_out_norm_w_2", 0), None, xhi[:, 8:16, :], xlo[:, 8:16, :])
            for b in range(4):
                lo4(QUAD["out2"] + b + 1)
                add_block(BLOCK["out2"] + b, b, QUAD["out2"] + b)
            dve.wait_ge(block_free, 2 + BLOCK["ffn"])
            dve.sem_inc(norm_src, 1)
            norm("ffn2", resid, ("ffn_norm_w_2", 0), None, xhi, xlo)

            q0, h0, n = QUAD["ffn"], HIDDEN["ffn"], FF2 // HID

            def conv_rest(g):
                for half_ in range(2):
                    dve.wait_ge(conv_start, g * 2 + (half_ + 1))
                    for lag, tap in ((1, 1), (2, 0)):
                        for nt in range(4):
                            i = g * 4 + (half_ * (FF2 // P) + nt)
                            o = conv[:, 4 * half_ + nt, lag:T]
                            ins = dve.scalar_tensor_tensor(out=o, in0=block_ps(half_)[:, nt, 0:T - lag],
                                                           scalar=fcol("ffn_conv_w_2", i + tap * (2 * FF2 // P)), in1=o,
                                                           op0=ALU.mult, op1=ALU.add)
                            if lag == 1:
                                step(ins)
                        if lag == 1:
                            step.settle()
                    ins.then_inc(conv_done, 1)
                    dve.wait_ge(conv_done, g * 2 + (half_ + 1))
                    dve.sem_inc(block_free, 1)

            def gate(g):
                dve.wait_ge(sig_ready, g + 1)
                if not (isinstance(g, int) and g == 0):
                    dve.wait_ge(hidden_lo, g + h0)
                step(dve.tensor_tensor(hid[:], conv[:, 0:4, :], gate_sig[:], ALU.mult))
                step.settle()
                dve.tensor_tensor(hid[:], hid[:], conv[:, 4:8, :], ALU.mult).then_inc(hidden_ready, 1)

            def ffn_split(g):
                dve.wait_ge(hidden_hi, g + (h0 + 1))
                dve.tensor_tensor(hid_lo[:], hid[:], hid_hi[:].bitcast(F32), ALU.subtract).then_inc(hidden_lo, 1)
            lo4(q0 + 1)
            lo4(q0 + 2)
            conv_rest(0)
            gate(0)
            lo4(q0 + 3)
            ffn_split(0)
            with dve.Fori(0, n - 2) as g:
                step.enter(g, 9)
                lo4(g * 3 + (q0 + 4))
                conv_rest(g + 1)
                gate(g + 1)
                lo4_add(g * 3 + (q0 + 5), g * 3 + (q0 + 4))
                ffn_split(g + 1)
                lo4(g * 3 + (q0 + 6))
                step.leave(n - 2)
            g = n - 2
            lo4(g * 3 + (q0 + 4))
            conv_rest(g + 1)
            gate(g + 1)
            lo4_add(g * 3 + (q0 + 5), g * 3 + (q0 + 4))
            ffn_split(g + 1)
            for nb in range(4):
                add_down(q0 + 3 * n - 1, nb)
            dve.wait_ge(down_free, 2 + 4 * (h0 + n))
            dve.sem_inc(norm_src, 1)
            norm("final", resid, ("final_norm_w_2", 0))

        @block.gpsimd
        def _(pool):
            step = Steps(pool, pool_steps)
            pool.wait_ge(pad_ready, 1)
            pool.wait_ge(table_landed, 32)
            for g in range(4):
                grp = 3 - g
                w = POOL_WINDOWS[grp]
                pool.wait_ge(block_free, 2 + g + 1)
                src, shift = u_pad[:, g], 1
                bufs = (win_a, win_b)
                if g >= 1:
                    pool.wait_ge(pooled_lo, g)
                n = 0
                while shift < w:
                    dst = bufs[n % 2]
                    step(pool.tensor_tensor(dst[:, :, PAD:PAD + T], src[:, :, PAD:PAD + T],
                                            src[:, :, PAD - shift:PAD - shift + T], ALU.add))
                    step.settle()
                    src, shift, n = dst, shift * 2, n + 1
                head, tail = src[:, :, PAD:2 * PAD], src[:, :, 2 * PAD:PAD + T]
                step(pool.tensor_tensor(head, head, ccol("count", PAD * grp, PAD).unsqueeze(1).to_broadcast([P, 4, PAD]), ALU.mult))
                step(pool.tensor_scalar(tail, tail, 1.0 / w, None, ALU.mult))
                step.settle()
                assert (src is win_a) == ((4 - g) % 2 == 1)
                pool.tensor_tensor(src[:, :, PAD:PAD + T], src[:, :, PAD:PAD + T], u_pad[:, g, :, PAD:PAD + T],
                                   ALU.subtract).then_inc(pooled, 1)
            for n in range(16):
                hf, kind, ci = n // 8, (n // 4) % 2, n % 4
                if n == 0:
                    pool.wait_ge(norm_lo, LO0[NORM["attn2"]] + 4)
                elif kind == 1:
                    pool.wait_ge(bu_done, 4 * hf + ci + 1)
                elif n >= 8:
                    pool.wait_ge(y_done, ci + 1)
                pool.dma_start(blocks[:, ci, :], ssm_blocks[n]).then_inc(blocks_landed[ci], 16)

        @block.tensor
        def _(pe):
            pe.sem_inc(chunk_used, SLOTS)
            pe.sem_inc(block_free, 2)
            pe.sem_inc(down_free, 2)
            pe.sem_inc(head_lo, 1)

            def chunk(q, s):
                pe.wait_ge(lo_ready, q * SLOTS + (SLOTS + s + 1))

            def three(o, w_hi, w_lo, x_hi, x_lo, first, last):
                pe.matmul(o, w_hi, x_hi, start=first, stop=False)
                pe.matmul(o, w_hi, x_lo, start=False, stop=False)
                return pe.matmul(o, w_lo, x_hi, start=False, stop=last)

            def tile(o, s, off, stride, kts, xh, xl):
                for k in range(kts):
                    c = slice(off + k * stride, off + k * stride + P)
                    ins = three(o, whi[:, s, c], wlo[:, s, c], xh[:, k, :], xl[:, k, :], k == 0, k == kts - 1)
                return ins

            def quad_block(q, set_, free, x_ready=None, tiles=4):
                pe.wait_ge(block_free, free)
                for s in range(tiles):
                    chunk(q, s if s < tiles - 1 else SLOTS - 1)
                    o = block_ps(set_)[:, s, :]
                    for k in range(DT):
                        if s == 0 and x_ready is not None and k % 4 == 0:
                            pe.wait_ge(x_ready[0], x_ready[1] + k // 4 + 1)
                        c = slice(k * P, k * P + P)
                        ins = three(o, whi[:, s, c], wlo[:, s, c], xhi[:, k, :], xlo[:, k, :], k == 0, k == DT - 1)
                    if s < tiles - 1:
                        ins.then_inc(chunk_used, 1)
                ins.then_inc(chunk_used, 1 + SLOTS - tiles)

            def norm(name, src):
                k = NORM[name]
                n, mean, t0 = NORMS[k][1], NORMS[k][2], PIECE0[k]
                w = min(4, n)
                off = DT - n
                if mean:
                    pe.wait_ge(norm_src, k + 1)
                    for i in range(n):
                        ins = pe.matmul(half(7, 0), ones_mean[:], src[:, i, :], start=i == 0, stop=i == n - 1)
                    ins.then_inc(norm_mean, 1)
                for p in range(PIECES[k]):
                    pe.wait_ge(norm_sq, t0 + p + 1)
                    for i in range(p * w, p * w + w):
                        ins = pe.matmul(half(6, 0), ones[:], scratch[:, off + i, :], start=i == 0, stop=i == n - 1)
                ins.then_inc(norm_var, 1)

            def down(q, m, hidden):
                pe.wait_ge(hidden_lo, hidden)
                for s in range(SLOTS):
                    chunk(q, s)
                    pe.wait_ge(down_free, m + (s + 1))
                    for nt in range(4):
                        ins = tile(block_ps(2 + s % 2)[:, nt, :], s, nt * P, 512, 4, hid_hi, hid_lo)
                    ins.then_inc(chunk_used, 1)

            def mlp(name):
                q0, b0, h0, n = QUAD[name], BLOCK[name], HIDDEN[name], FF // HID

                def up(g, x_ready=None):
                    quad_block(q0 if isinstance(g, int) else g * 2 + (q0 - 1), 0, g + (b0 + 2), x_ready)
                up(0, (norm_lo, LO0[NORM["mix" + name[-1]]]))
                with pe.Fori(0, n - 1) as g:
                    up(g + 1)
                    down(g * 2 + (q0 + 2), g * 4 + 4 * h0, g + (h0 + 1))
                down(q0 + 2 * n - 1, 4 * (h0 + n - 1), h0 + n)

            pe.wait_ge(ones_ready, 1)
            pe.wait_ge(table_landed, 32)
            for b in range(4):
                quad_block(b, b % 2, b + 1, (x_lo_ready, 0) if b == 0 else None)
            for g in range(4):
                b = BLOCK["pool_group"] + g
                pe.wait_ge(pooled_lo, g + 1)
                pe.wait_ge(block_free, b + 1)
                chunk(QUAD["pool_group"], g)
                for nt in range(4):
                    ins = tile(block_ps(b % 2)[:, nt, :], g, nt * P, 512, 4, pool_hi[:, g % 2], pool_lo[:, g % 2])
                ins.then_inc(chunk_used, 1)
            pe.wait_ge(y_lo, 4)
            for b in range(4):
                n = BLOCK["pool_out"] + b
                quad_block(QUAD["pool_out"] + b, n % 2, n + 1)
            norm("mix0", resid)
            mlp("mlp0")
            norm("mlp0", resid)

            pe.wait_ge(norm_lo, LO0[NORM["mlp0"]] + 4)

            def qkv(h, g):
                n = h * 3 + g
                q = n + QUAD["attn"]
                ab = 2 * (g % 2)
                if g == 0 and not isinstance(h, int):
                    pe.wait_ge(qkv_copied, n)
                if g == 2:
                    pe.wait_ge(qkv_copied, n - 1)
                for s in range(2):
                    chunk(q, s)
                    tile(half(ab, s), s, 0, P, DT, xhi, xlo).then_inc(chunk_used, 1)
                chunk(q, 3)
                for tt in range(2):
                    o = ps[:, ab + 1, tt * HD:(tt + 1) * HD]
                    for k in range(DT):
                        c, t = slice(k * P, k * P + P), slice(tt * P, tt * P + P)
                        pe.matmul(o, xhi[:, k, t], whi[:, 2, c], start=k == 0, stop=False)
                        pe.matmul(o, xhi[:, k, t], wlo[:, 2, c], start=False, stop=False)
                        ins = pe.matmul(o, xlo[:, k, t], whi[:, 2, c], start=False, stop=k == DT - 1)
                ins.then_inc(chunk_used, 2)

            def scores(h):
                pe.wait_ge(qkv_copied, h * 3 + 3)
                for g in range(N_GROUPS):
                    pe.matmul(ps[:, 4 + g, 0:128], qk[:, g, 0, 0:128], qk[:, g, 1, 0:128], start=True, stop=True)
                    ins = pe.matmul(ps[:, 4 + g, 128:384], qk[:, g, 0, 128:256], qk[:, g, 1, :], start=True, stop=True)
                ins.then_inc(scores_done, 1)

            def turn(h):
                pe.wait_ge(prob_ready, h + 1)
                for g in range(N_GROUPS):
                    for b in range(3):
                        ins = pe.transpose(ps[:, 4 + g, b * P:(b + 1) * P], score[:, g, b * P:(b + 1) * P], ccol("ident"))
                ins.then_inc(turned, 1)

            def mix(h):
                pe.wait_ge(turned_copied, h + 1)
                pe.wait_ge(v_ready, h + 1)
                pe.wait_ge(head_lo, h + 1)
                for g in range(N_GROUPS):
                    pe.matmul(ps[:, 7, 0:128], v_cur[:, g, 0], prob_t[:, g, 0:128], start=g == 0, stop=g == 2)
                for g in range(N_GROUPS):
                    for kt in range(2):
                        ins = pe.matmul(ps[:, 7, 128:256], v_cur[:, g, kt], prob_t[:, g, 128 + 128 * kt:256 + 128 * kt],
                                        start=g + kt == 0, stop=g + kt == 3)
                ins.then_inc(head_done, 1)
            qkv(0, 0)
            qkv(0, 1)
            qkv(0, 2)
            scores(0)
            with pe.Fori(0, N_HEADS - 1) as hh:
                qkv(hh + 1, 0)
                turn(hh)
                qkv(hh + 1, 1)
                mix(hh)
                qkv(hh + 1, 2)
                scores(hh + 1)
            turn(N_HEADS - 1)
            mix(N_HEADS - 1)
            pe.wait_ge(head_lo, 1 + N_HEADS)
            for b in range(4):
                n = BLOCK["attn_out"] + b
                q = QUAD["attn_out"] + b // 2
                pe.wait_ge(block_free, n + 1)
                for s2 in range(2):
                    s = 2 * (b % 2) + s2
                    chunk(q, s)
                    for j in range(2):
                        ins = tile(block_ps(n % 2)[:, 2 * s2 + j, :], s, j * P, 256, 8, heads_hi, heads_lo)
                    ins.then_inc(chunk_used, 1)
            norm("mix1", resid)
            mlp("mlp1")
            norm("mlp1", resid)
            norm("attn2", resid)

            for b in range(4):
                n = BLOCK["proj"] + b
                quad_block(QUAD["proj"] + b, n % 2, n + 1, (norm_lo, LO0[NORM["attn2"]]) if b == 0 else None, 3 if b == 3 else 4)
            for hf in range(2):
                pe.wait_ge(block_free, 2 + BLOCK["proj"] + 4)
                for ci in range(4):
                    c = 4 * hf + ci
                    pe.wait_ge(blocks_landed[ci], 32 * hf + 16)
                    if ci >= 2:
                        pe.wait_ge(bu_ready, c - 1)
                    elif hf:
                        pe.wait_ge(y_ready, 1)
                    for st in range(4):
                        for r in range(2):
                            ins = pe.matmul(half(4 * (ci % 2) + st, r), blocks[:, ci, r * 512 + st * P:r * 512 + st * P + P],
                                            proj[:, c, :], start=True, stop=True)
                    ins.then_inc(bu_done, 1)
                for ci in range(4):
                    pe.wait_ge(blocks_landed[ci], 32 * hf + 32)
                    pe.wait_ge(scan_done, 4 * hf + ci + 1)
                    for r in range(2):
                        for st in range(4):
                            ins = pe.matmul(half(ci, r), blocks[:, ci, r * 512 + st * P:r * 512 + st * P + P],
                                            state[:, r, 4 * ci + st, :], start=st == 0, stop=st == 3)
                    ins.then_inc(y_done, 1)
            pe.wait_ge(gelu_lo, 2)
            for b in range(2):
                for s2 in range(2):
                    s = 2 * b + s2
                    chunk(QUAD["glu"], s)
                    for j in range(2):
                        ins = tile(block_ps(b)[:, 2 * s2 + j, :], s, j * P, 256, 8, xhi, xlo)
                    ins.then_inc(chunk_used, 1)
            norm("ssm", proj[:, 0:8, :])
            norm("q", proj[:, 8:12, :])
            norm("kv", proj[:, 12:14, :])

            def rope(src):
                pe.matmul(ps[0:ROPE, 2, 0:T], ccol("sel"), src, start=True, stop=True)
                pe.matmul(ps[0:ROPE, 2, T:2 * T], ccol("rot"), src, start=True, stop=True).then_inc(rope_done, 1)
            rope(proj[:, 14, :])
            pe.wait_ge(norm_lo, LO0[NORM["kv"]] + 1)
            pe.wait_ge(rope_ready, 1)
            with pe.Fori(0, 2) as i:
                for s in range(SLOTS):
                    h = i * 4 + s
                    chunk(i + QUAD["mla"], s)
                    for j in range(2):
                        tile(half(0, j), s, j * ROPE, 192, 4, cq_hi, cq_lo)
                    tile(half(1, 0), s, 768, 256, 2, ckv_hi, ckv_lo)
                    for tt in range(2):
                        o = ps[:, 1, T + tt * HD:T + (tt + 1) * HD]
                        for k in range(2):
                            c, t = slice(768 + k * 256 + P, 768 + k * 256 + 256), slice(tt * P, tt * P + P)
                            pe.matmul(o, ckv_hi[:, k, t], whi[:, s, c], start=k == 0, stop=False)
                            pe.matmul(o, ckv_hi[:, k, t], wlo[:, s, c], start=False, stop=False)
                            ins = pe.matmul(o, ckv_lo[:, k, t], whi[:, s, c], start=False, stop=k == 1)
                    ins.then_inc(chunk_used, 1)
                    pe.wait_ge(m_copied, h + 1)
                    rope(proj[:, 1, :])
                    pe.wait_ge(rope_ready, h + 2)
                    for qt in range(2):
                        o = ps[:, 3, 128 * qt:128 + 256 * qt]
                        t, keys = slice(qt * P, qt * P + P), slice(0, P + P * qt)
                        pe.matmul(o, proj[:, 0, t], proj[:, 2, keys], start=True, stop=False)
                        ins = pe.matmul(o, proj[0:ROPE, 4, t], k_rope[:, keys], start=False, stop=True)
                    ins.then_inc(m_score, 1)
                    pe.wait_ge(m_prob, h + 1)
                    sc = proj[:, 5:7, :].rearrange("p a t -> p (a t)")
                    for b in range(3):
                        ins = pe.transpose(ps[:, 4, b * P:(b + 1) * P], sc[:, b * P:(b + 1) * P], ccol("ident"))
                    ins.then_inc(m_turned, 1)
                    pe.wait_ge(m_pt, h + 1)
                    pt = proj[:, 7:9, :].rearrange("p a t -> p (a t)")
                    pe.matmul(ps[:, 5, 0:128], proj[:, 3, 0:HD], pt[:, 0:128], start=True, stop=True)
                    pe.matmul(ps[:, 5, 128:256], proj[:, 3, 0:HD], pt[:, 128:256], start=True, stop=False)
                    pe.matmul(ps[:, 5, 128:256], proj[:, 3, HD:2 * HD], pt[:, 256:384], start=False, stop=True).then_inc(m_out, 1)
            norm("mla", scratch[:, 0:8, :])
            pe.wait_ge(norm_lo, LO0[NORM["mla"]] + 2)
            for b in range(4):
                n = BLOCK["out2"] + b
                quad_block(QUAD["out2"] + b, n % 2, n + 1)
            norm("ffn2", resid)

            q0, b0, h0, n = QUAD["ffn"], BLOCK["ffn"], HIDDEN["ffn"], FF2 // HID

            def up(g, quad, x_ready=None):
                for i in range(2):
                    quad_block(quad + i, i, g * 2 + (b0 + i + 1), x_ready if i == 0 else None)
            up(0, q0, (norm_lo, LO0[NORM["ffn2"]]))
            with pe.Fori(0, n - 1) as g:
                up(g + 1, g * 3 + (q0 + 2))
                down(g * 3 + (q0 + 4), g * 4 + 4 * h0, g + (h0 + 1))
            down(q0 + 3 * n - 1, 4 * (h0 + n - 1), h0 + n)
            norm("final", resid)


def shape_constants():
    import numpy as np
    t = np.zeros((P, N_CONST), np.float32)

    def put(name, a):
        t[:a.shape[0], CONST[name]:CONST[name] + a.shape[1]] = a
    put("ident", np.eye(P))
    far = 1e37
    lag = np.arange(T)[:, None] - np.arange(T)[None, :]
    for g, (window, dil) in enumerate(((128, 1), (512, 4), (2048, 16))):
        ok = (lag >= 0) & (lag <= window) & (lag % dil == 0)
        d = np.where(ok, lag, far)
        t[:, CONST["dist"] + 384 * g:CONST["dist"] + 384 * g + 128] = d[:P, :P]
        t[:, CONST["dist"] + 384 * g + 128:CONST["dist"] + 384 * g + 384] = d[P:, :]
    c = np.where(lag >= 0, 0.0, -far)
    put("causal", np.concatenate([c[:P, :P], c[P:, :]], axis=1))
    n = N_GROUPS * N_HEADS
    put("slope", np.broadcast_to(-np.exp2(-8.0 * np.arange(1, n + 1) / n) / ATTN_SCALE, (P, n)))
    sel, rot, h = np.zeros((P, ROPE)), np.zeros((P, ROPE)), ROPE // 2
    for i in range(ROPE):
        sel[ROPE + i, i] = 1.0
    for i in range(h):
        rot[ROPE + h + i, i] = -1.0
        rot[ROPE + i, h + i] = 1.0
    put("sel", sel)
    put("rot", rot)
    put("count", np.broadcast_to(np.concatenate([1.0 / np.minimum(np.arange(1, PAD + 1), w) for w in POOL_WINDOWS]), (P, 4 * PAD)))
    f = 10000.0 ** (-np.arange(0, ROPE, 2) / ROPE)
    put("freq", np.concatenate([f, f])[:, None])
    t[:, CONST["ln_eps"]] = LN_EPS
    t[:, CONST["rms_eps"]] = RMS_EPS
    return t


def pack_weights(i):
    import numpy as np

    def columns(w, kts=DT):
        n = CW // kts
        return w.reshape(kts, P, -1, n).transpose(2, 1, 0, 3).reshape(-1, P, CW)

    def rows(w):
        return w.reshape(-1, 4, P, w.shape[1] // 512, 512).transpose(0, 3, 2, 1, 4).reshape(-1, P, CW)

    def mlp(up, down):
        u, d = columns(up).reshape(-1, 4, P, CW), rows(down).reshape(-1, 4, P, CW)
        parts = [u[0]]
        for g in range(len(u) - 1):
            parts += [u[g + 1], d[g]]
        return np.concatenate(parts + [d[-1]])

    def ffn(up, down):
        u, d = columns(up).reshape(2, -1, 4, P, CW), rows(down).reshape(-1, 4, P, CW)
        n = len(d)
        parts = [u[0, 0], u[1, 0]]
        for g in range(n - 1):
            parts += [u[0, g + 1], u[1, g + 1], d[g]]
        return np.concatenate(parts + [d[-1]])
    parts = [columns(i["pool_w_in"][0]).reshape(4, 4, P, CW)[::-1].reshape(-1, P, CW),
             np.concatenate([rows(i["pool_w_group"][0, 3 - g]) for g in range(4)]),
             columns(i["pool_w_out"][0]), mlp(i["mlp_w_up"][0], i["mlp_w_down"][0])]
    qkv = columns(i["attn_w_qkv"][0]).reshape(3, N_GROUPS, N_HEADS, P, CW).transpose(2, 1, 0, 3, 4)
    attn = np.zeros((N_HEADS, N_GROUPS, 4, P, CW), np.float32)
    attn[:, :, 0:3] = qkv
    parts += [attn.reshape(-1, P, CW), columns(i["attn_w_out"][0], 8), mlp(i["mlp_w_up"][1], i["mlp_w_down"][1])]
    w = i["w_in_2"][0]
    parts += [columns(w[:, 0:1792]), columns(w[:, 1728:1856]), np.zeros((1, P, CW), np.float32), columns(i["ssm_w_glu_2"][0], 8)]
    mla = np.zeros((N_HEADS, P, CW), np.float32)
    mla[:, :, 0:768] = i["mla_w_uq_2"][0].reshape(4, P, N_HEADS, 192).transpose(2, 1, 0, 3).reshape(N_HEADS, P, 768)
    mla[:, :, 768:1280] = i["mla_w_ukv_2"][0].reshape(2, P, N_HEADS, 256).transpose(2, 1, 0, 3).reshape(N_HEADS, P, 512)
    parts += [mla, columns(i["w_out_2"][0]), ffn(i["ffn_w_up_2"][0], i["ffn_w_down_2"][0])]
    return np.concatenate(parts)


def pack_ssm(i):
    import numpy as np
    t = np.zeros((2, 2, 4, P, 2, 4, P), np.float32)
    for r, part in enumerate(("re", "im")):
        b, c = i[f"ssm_b_{part}_2"][0], i[f"ssm_c_{part}_2"][0]
        for g in range(64):
            hf, ci, st, h = g // 32, (g // 8) % 4, (g // 2) % 4, g % 2
            ch, state = slice(g % 8 * 16, g % 8 * 16 + 16), slice(64 * h, 64 * h + 64)
            t[hf, 0, ci, ch, r, st, state] = b[g].T
            t[hf, 1, ci, state, r, st, ch] = c[g].T
    return t.reshape(16, P, 1024)


def kernel(**inputs):
    import numpy as np
    import concourse.bacc as bacc
    from concourse.bass_utils import run_bass_kernel_spmd as run

    i = {k: np.asarray(v) for k, v in inputs.items()}
    lam = np.stack([i["ssm_lambda_re_2"].reshape(32, P), i["ssm_lambda_im_2"].reshape(32, P),
                    np.repeat(i["ssm_log_dt_2"].reshape(64), 64).reshape(32, P)])
    arrays = {
        "x_t": i["x"][0].T,
        "weights": pack_weights(i),
        "ssm_blocks": pack_ssm(i),
        "features": np.concatenate([i[n].reshape(-1, P) for n, _ in FEATURES]).T,
        "consts": shape_constants(),
        "ssm_lam": lam.transpose(2, 0, 1),
        "positions": i["positions_2"].reshape(T),
    }
    arrays = {k: np.ascontiguousarray(v) for k, v in arrays.items()}
    nc = bacc.Bacc("TRN2", target_bir_lowering=False, num_devices=1)
    args = [nc.dram_tensor(k, v.shape, mybir.dt.from_np(v.dtype), kind="ExternalInput").ap() for k, v in arrays.items()]
    out = nc.dram_tensor("out", (D, T), F32, kind="ExternalOutput").ap()
    build(nc, *args, out)
    r = run(nc, [arrays], core_ids=[0])
    return np.ascontiguousarray(r.results[0]["out"].T)[None]
```

```python
from contextlib import ExitStack

import concourse.bass as bass
from concourse import mybir

F32 = mybir.dt.float32
F32R = mybir.dt.float32r
I32 = mybir.dt.int32
ALU = mybir.AluOpType
ACT = mybir.ActivationFunctionType
AX = mybir.AxisListType

P = 128
T = 256
D = 2048
DT = D // P
FF = 4 * D
FF2 = 5632
HID = 512
SLOTS = 4
CW = 2048
N_HEADS = 8
N_GROUPS = 3
HD = 128
ROPE = 64
ALPHA = 4.0 ** 0.25
LN_EPS = 1e-5
RMS_EPS = 1e-6
ATTN_SCALE = HD ** -0.5
MLA_SCALE = (HD + ROPE) ** -0.5
POOL_WINDOWS = (2, 4, 8, 16)
PAD = 16
SCAN = 16

STAGES = (("pool_in", 4), ("pool_group", 1), ("pool_out", 4), ("mlp0", 32), ("attn", 24), ("attn_out", 2),
          ("mlp1", 32), ("proj", 4), ("glu", 1), ("mla", 2), ("out2", 4), ("ffn", 33))
QUAD, N_QUADS = {}, 0
for _name, _n in STAGES:
    QUAD[_name] = N_QUADS
    N_QUADS += _n

BLOCK, _b = {}, 0
for _name, _n in (("pool_in", 4), ("pool_group", 4), ("pool_out", 4), ("mlp0", 16), ("attn_out", 4), ("mlp1", 16),
                  ("proj", 4), ("glu", 2), ("out2", 4), ("ffn", 22)):
    BLOCK[_name] = _b
    _b += _n
HIDDEN = {"mlp0": 0, "mlp1": FF // HID, "ffn": 2 * FF // HID}

FEATURES = (("pool_scale", DT), ("ln_mix_g", 2 * DT), ("ln_mix_b", 2 * DT), ("ln_mlp_g", 2 * DT), ("ln_mlp_b", 2 * DT),
            ("attn_norm_w_2", DT), ("ffn_norm_w_2", DT), ("final_norm_w_2", DT), ("ssm_d_2", 8), ("ssm_b_glu_2", 8),
            ("mla_q_norm_w_2", 4), ("mla_kv_norm_w_2", 2), ("ssm_out_norm_w_2", 8), ("mla_out_norm_w_2", 8),
            ("ffn_conv_w_2", 3 * 2 * FF2 // P), ("ffn_conv_b_2", 2 * FF2 // P))
FEAT, N_FEAT = {}, 0
for _name, _n in FEATURES:
    FEAT[_name] = N_FEAT
    N_FEAT += _n

CONSTS = (("ident", P), ("dist", 3 * 384), ("causal", 384), ("slope", 24), ("sel", ROPE), ("rot", ROPE),
          ("count", 4 * PAD), ("freq", 1), ("ln_eps", 1), ("rms_eps", 1))
CONST, N_CONST = {}, 0
for _name, _n in CONSTS:
    CONST[_name] = N_CONST
    N_CONST += _n

NORMS = (("mix0", 16, True), ("mlp0", 16, True), ("mix1", 16, True), ("mlp1", 16, True), ("attn2", 16, False),
         ("ssm", 8, False), ("q", 4, False), ("kv", 2, False), ("mla", 8, False), ("ffn2", 16, False), ("final", 16, False))
NORM = {n: i for i, (n, _, _) in enumerate(NORMS)}
NORM_TILES = {n: t for n, t, _ in NORMS}
PIECES = [max(1, t // 4) for _, t, _ in NORMS]
PIECE0 = [sum(PIECES[:i]) for i in range(len(PIECES))]
LO0 = [sum(p for (n, _, _), p in zip(NORMS[:i], PIECES) if n not in ("mlp1", "final")) for i in range(len(NORMS))]
ATTN_WIDTHS = (CW, CW, CW, 16)


class Steps:

    def __init__(self, eng, sem):
        self.eng, self.sem, self.n, self.it, self.per = eng, sem, 0, None, 0

    def __call__(self, ins):
        ins.then_inc(self.sem, 1)
        self.n += 1

    def settle(self):
        if self.it is None:
            self.eng.wait_ge(self.sem, self.n)
        else:
            self.eng.wait_ge(self.sem, self.it * self.per + self.n)

    def enter(self, it, per):
        self.it, self.per, self.start = it, per, self.n

    def leave(self, times):
        assert self.n - self.start == self.per, (self.n - self.start, self.per)
        self.it = None
        self.n = self.start + self.per * times


def build(nc, x_t, weights, ssm_blocks, features, consts, ssm_lam, positions, out):
    with ExitStack() as ctx:
        def sem(name):
            return ctx.enter_context(nc.semaphore(name))

        def sb(name, shape, dt=F32, scope=ctx):
            return scope.enter_context(nc.sbuf_tensor(name, shape, dt))

        raw = sb("raw", [P, SLOTS, CW])
        whi = sb("whi", [P, SLOTS, CW], F32R)
        wlo = sb("wlo", [P, SLOTS, CW], F32R)
        resid = sb("resid", [P, DT, T])
        feat = sb("feat", [P, N_FEAT])
        const = sb("const", [P, N_CONST])
        ones = sb("ones", [P, P])
        ones_mean = sb("ones_mean", [P, P])
        std = sb("std", [P, T])
        rstd = sb("rstd", [P, T])
        rope_a, k_rope = std[0:ROPE, :], rstd[0:ROPE, :]
        lam = sb("lam", [P, 3, 32])
        par = sb("par", [P, 13, 32])
        pow_re = sb("pow_re", [P, 32, SCAN])
        pow_im = sb("pow_im", [P, 32, SCAN])
        rope_cos = sb("rope_cos", [ROPE, T])
        rope_sin = sb("rope_sin", [ROPE, T])
        pos_i = rope_cos[:].bitcast(I32)

        with ExitStack() as s:
            xhi = sb("xhi", [P, DT, T], F32R, s)
            xlo = sb("xlo", [P, DT, T], F32R, s)
        state = sb("state", [P, 2, 16, T])

        with ExitStack() as s:
            pool_hi = sb("pool_hi", [P, 2, 4, T], F32R, s)
            pool_lo = sb("pool_lo", [P, 2, 4, T], F32R, s)
        with ExitStack() as s:
            heads_hi = sb("heads_hi", [P, N_HEADS, T], F32R, s)
            heads_lo = sb("heads_lo", [P, N_HEADS, T], F32R, s)
        with ExitStack() as s:
            blocks = sb("blocks", [P, 4, 1024], F32, s)
        scratch = sb("scratch", [P, DT, T])

        with ExitStack() as s:
            u_pad = sb("u_pad", [P, 4, 4, PAD + T], F32, s)
            win_a = sb("win_a", [P, 4, PAD + T], F32, s)
            win_b = sb("win_b", [P, 4, PAD + T], F32, s)
        with ExitStack() as s:
            hid = sb("hid", [P, 4, T], F32, s)
            hid_hi = sb("hid_hi", [P, 4, T], F32R, s)
            hid_lo = sb("hid_lo", [P, 4, T], F32R, s)
            conv = sb("conv", [P, 8, T], F32, s)
            gate_sig = sb("gate_sig", [P, 4, T], F32, s)
        with ExitStack() as s:
            qkv_t = sb("qkv_t", [P, N_GROUPS, 3, T], F32, s)
            v_rows = sb("v_rows", [P, 2, N_GROUPS, 2, HD], F32, s)
            score = sb("score", [P, N_GROUPS, 384], F32, s)
            prob_t = sb("prob_t", [P, N_GROUPS, 384], F32, s)
            row_max = sb("row_max", [P, 2], F32, s)
            row_den = sb("row_den", [P, 2], F32, s)
        with ExitStack() as s:
            proj = sb("proj", [P, 15, T], F32, s)
            with ExitStack() as s2:
                scan_a = sb("scan_a", [P, 2, 16, 16], F32, s2)
                scan_b = sb("scan_b", [P, 2, 16, 16], F32, s2)
                bu_tmp = sb("bu_tmp", [P, 4, 2, T], F32, s2)
            with ExitStack() as s2:
                cq_hi = sb("cq_hi", [P, 4, T], F32R, s2)
                cq_lo = sb("cq_lo", [P, 4, T], F32R, s2)
                ckv_hi = sb("ckv_hi", [P, 2, T], F32R, s2)
                ckv_lo = sb("ckv_lo", [P, 2, T], F32R, s2)
                m_max = sb("m_max", [P, 2], F32, s2)
                m_den = sb("m_den", [P, 2], F32, s2)

        ps = ctx.enter_context(nc.psum_tensor("ps", [P, 8, 512], F32))

        def half(bank, h):
            return ps[:, bank, h * T:(h + 1) * T]

        def block_ps(b):
            return ps[:, 2 * b:2 * b + 2, :].rearrange("p b (h t) -> p (b h) t", t=T)

        def wait_used(eng, q, s=SLOTS - 1):
            eng.wait_ge(chunk_used, q * SLOTS + (SLOTS + s + 1))

        def up_quad(q0, g, per):
            return q0 if isinstance(g, int) and g == 0 else g * per + (q0 - 1)

        def scratch_gelu(hf):
            return bu_tmp[:].rearrange("p a b t -> p (a b) t")[:, 0:4, :]

        def fcol(name, i):
            return feat[:, bass.ds(FEAT[name] + i, 1)]

        def ccol(name, a=0, n=None, rows=P):
            n = dict(CONSTS)[name] - a if n is None else n
            return const[0:rows, CONST[name] + a:CONST[name] + a + n]

        landed = [sem(f"landed{i}") for i in range(SLOTS)]
        hi_ready, lo_ready, chunk_used = sem("hi_ready"), sem("lo_ready"), sem("chunk_used")
        x_landed = [sem(f"x_landed{i}") for i in range(4)]
        table_landed, lam_landed, out_landed = sem("table_landed"), sem("lam_landed"), sem("out_landed")
        ones_ready = sem("ones_ready")
        x_hi_ready, x_lo_ready, resid_ready = sem("x_hi_ready"), sem("x_lo_ready"), sem("resid_ready")
        block_free = sem("block_free")
        down_free = sem("down_free")
        hidden_ready, hidden_hi, hidden_lo = sem("hidden_ready"), sem("hidden_hi"), sem("hidden_lo")
        conv_start, conv_done, sig_ready = sem("conv_start"), sem("conv_done"), sem("sig_ready")
        u_ready, pad_ready, pooled, pooled_hi, pooled_lo = (sem(n) for n in ("u_ready", "pad_ready", "pooled", "pooled_hi", "pooled_lo"))
        y_scaled, y_hi, y_lo = sem("y_scaled"), sem("y_hi"), sem("y_lo")
        norm_src, norm_mean, norm_xc, norm_sq, norm_var, norm_std, norm_y, norm_hi, norm_lo = (
            sem(n) for n in ("norm_src", "norm_mean", "norm_xc", "norm_sq", "norm_var", "norm_std", "norm_y", "norm_hi", "norm_lo"))
        qkv_copied, v_turned, v_ready = sem("qkv_copied"), sem("v_turned"), sem("v_ready")
        scores_done, shift_ready, exp_done, prob_ready = sem("scores_done"), sem("shift_ready"), sem("exp_done"), sem("prob_ready")
        turned, turned_copied, head_done, head_hi, head_lo = (sem(n) for n in ("turned", "turned_copied", "head_done", "head_hi", "head_lo"))
        blocks_landed = [sem(f"blocks_landed{i}") for i in range(4)]
        angles_ready, trig_ready, table_ready = sem("angles_ready"), sem("trig_ready"), sem("table_ready")
        proj_copied, bu_done, bu_part, bu_ready, scan_done, y_done, y_ready = (
            sem(n) for n in ("proj_copied", "bu_done", "bu_part", "bu_ready", "scan_done", "y_done", "y_ready"))
        gelu_sq, gelu_arg, gelu_sig, gelu_ready, gelu_hi, gelu_lo, glu_sig = (
            sem(n) for n in ("gelu_sq", "gelu_arg", "gelu_sig", "gelu_ready", "gelu_hi", "gelu_lo", "glu_sig"))
        m_copied, rope_done, rope_ready, m_score, m_shift, m_exp, m_prob, m_turned, m_pt, m_out, m_out_copied = (
            sem(n) for n in ("m_copied", "rope_done", "rope_ready", "m_score", "m_shift", "m_exp", "m_prob",
                             "m_turned", "m_pt", "m_out", "m_out_copied"))
        act_steps, dve_steps, pool_steps = sem("act_steps"), sem("dve_steps"), sem("pool_steps")

        block = ctx.enter_context(nc.Block())

        @block.sync
        def _(sp):
            def load(q, s, width=CW):
                sp.wait_ge(lo_ready, q * SLOTS + (s + 1))
                sp.dma_start(raw[:, s, 0:width],
                             weights[bass.ds(q * SLOTS + s, 1), :, 0:width].rearrange("a p c -> p (a c)")).then_inc(landed[s], 16)

            xv = x_t.rearrange("(n p) t -> p n t", p=P)
            for p in range(4):
                sp.dma_start(resid[:, 4 * p:4 * p + 4, :], xv[:, 4 * p:4 * p + 4, :]).then_inc(x_landed[p], 16)
            with sp.Fori(0, QUAD["attn"]) as q:
                for s in range(SLOTS):
                    load(q, s)
            with sp.Fori(QUAD["attn"], QUAD["attn_out"]) as q:
                for s in range(SLOTS):
                    load(q, s, CW if s < 3 else 16)
            with sp.Fori(QUAD["attn_out"], N_QUADS) as q:
                for s in range(SLOTS):
                    load(q, s)
            for p in range(4):
                sp.wait_ge(norm_y, PIECE0[NORM["final"]] + p + 1)
                sp.dma_start(out.rearrange("(n p) t -> p n t", p=P)[:, 4 * p:4 * p + 4, :],
                             scratch[:, 4 * p:4 * p + 4, :]).then_inc(out_landed, 16)
            sp.wait_ge(out_landed, 64)

        @block.scalar
        def _(act):
            step = Steps(act, act_steps)

            def hi1(q, s, width=CW):
                act.wait_ge(landed[s], q * 16 + 16)
                act.wait_ge(chunk_used, q * SLOTS + (s + 1))
                act.activation(whi[:, s, 0:width], raw[:, s, 0:width], ACT.Copy).then_inc(hi_ready, 1)

            def hi4(q, widths=(CW,) * 4):
                for s in range(SLOTS):
                    hi1(q, s, widths[s])

            def norm(name, src, dst_hi=None, scale_resid=False):
                k = NORM[name]
                n, mean, t0 = NORMS[k][1], NORMS[k][2], PIECE0[k]
                w = min(4, n)
                off = DT - n
                if LO0[k]:
                    act.wait_ge(norm_lo, LO0[k])
                if not mean:
                    act.wait_ge(norm_src, k + 1)
                for p in range(PIECES[k]):
                    if mean:
                        act.wait_ge(norm_xc, t0 + p + 1)
                    act.activation(scratch[:, off + p * w:off + p * w + w, :], src[:, p * w:p * w + w, :],
                                   ACT.Square).then_inc(norm_sq, 1)
                act.wait_ge(norm_var, k + 1)
                act.activation(std[:], half(6, 0), ACT.Sqrt, scale=1.0 / (n * P),
                               bias=ccol("ln_eps" if mean else "rms_eps")).then_inc(norm_std, 1)
                if dst_hi is None:
                    return
                y = src if mean else scratch[:, off:DT, :]
                for p in range(PIECES[k]):
                    act.wait_ge(norm_y, t0 + p + 1)
                    act.activation(dst_hi[:, p * w:p * w + w, :], y[:, p * w:p * w + w, :], ACT.Copy).then_inc(norm_hi, 1)
                if scale_resid:
                    for p in range(PIECES[k]):
                        act.wait_ge(norm_lo, LO0[k] + p + 1)
                        act.mul(resid[:, 4 * p:4 * p + 4, :], resid[:, 4 * p:4 * p + 4, :], ALPHA).then_inc(resid_ready, 1)

            def mlp(name, next_quad, next_widths=(CW,) * 4):
                q0, b0, h0 = QUAD[name], BLOCK[name], HIDDEN[name]
                n = FF // HID

                def activate(g):
                    wait_used(act, up_quad(q0, g, 2))
                    if not (isinstance(g, int) and g + h0 == 0):
                        act.wait_ge(hidden_lo, g + h0)
                    act.activation(hid[:], block_ps(0), ACT.Relu).then_inc(block_free, 1)
                    act.wait_ge(block_free, g + (b0 + 3))
                    act.activation(hid[:], hid[:], ACT.Square).then_inc(hidden_ready, 1)

                def split(g):
                    act.wait_ge(hidden_ready, g + (h0 + 1))
                    if not (isinstance(g, int) and g == 0):
                        wait_used(act, g * 2 + q0)
                    act.activation(hid_hi[:], hid[:], ACT.Copy).then_inc(hidden_hi, 1)

                hi4(q0 + 1)
                activate(0)
                split(0)
                with act.Fori(0, n - 2) as g:
                    hi4(g * 2 + (q0 + 2))
                    activate(g + 1)
                    hi4(g * 2 + (q0 + 3))
                    split(g + 1)
                hi4(q0 + 2 * n - 2)
                activate(n - 1)
                hi4(q0 + 2 * n - 1)
                split(n - 1)
                hi4(next_quad, next_widths)

            act.dma_start(lam[:], ssm_lam).then_inc(lam_landed, 16)
            act.dma_start(pos_i, positions.partition_broadcast(ROPE)).then_inc(lam_landed, 16)
            act.wait_ge(lam_landed, 32)
            act.activation(par[:, 0, :], lam[:, 2, :], ACT.Exp).then_inc(trig_ready, 1)
            act.wait_ge(angles_ready, 1)
            act.activation(par[:, 1, :], par[:, 1, :], ACT.Exp).then_inc(trig_ready, 1)
            act.wait_ge(angles_ready, 3)
            act.activation(par[:, 2, :], par[:, 2, :], ACT.Sin)
            act.activation(par[:, 3, :], par[:, 3, :], ACT.Sin).then_inc(trig_ready, 1)
            for p in range(4):
                act.wait_ge(x_landed[p], 16)
                act.activation(xhi[:, 4 * p:4 * p + 4, :], resid[:, 4 * p:4 * p + 4, :], ACT.Copy).then_inc(x_hi_ready, 1)
            act.dma_start(const[:], consts).then_inc(table_landed, 16)
            act.dma_start(feat[:], features).then_inc(table_landed, 16)
            hi4(0)
            for p in range(4):
                act.wait_ge(x_lo_ready, p + 1)
                act.mul(resid[:, 4 * p:4 * p + 4, :], resid[:, 4 * p:4 * p + 4, :], ALPHA).then_inc(resid_ready, 1)

            act.wait_ge(pad_ready, 1)

            def copy_u(b):
                wait_used(act, b)
                act.activation(u_pad[:, bass.ds(b, 1), :, PAD:PAD + T].rearrange("p a n t -> p (a n) t"),
                               block_ps(b % 2), ACT.Copy).then_inc(block_free, 1)

            def pooled_high(g):
                act.wait_ge(pooled, g + 1)
                if g >= 2:
                    wait_used(act, QUAD["pool_group"], g - 2)
                act.activation(pool_hi[:, g % 2], win_a[:, :, PAD:PAD + T] if (4 - g) % 2 else win_b[:, :, PAD:PAD + T],
                               ACT.Copy).then_inc(pooled_hi, 1)

            def mixed_high(g):
                grp = 3 - g
                act.wait_ge(y_scaled, g + 1)
                act.activation(xhi[:, 4 * grp:4 * grp + 4, :], u_pad[:, g, :, PAD:PAD + T], ACT.Copy).then_inc(y_hi, 1)
                hi1(QUAD["pool_out"], g)
            hi4(1)
            copy_u(0)
            hi4(2)
            copy_u(1)
            act.wait_ge(angles_ready, 5)
            act.activation(rope_sin[:], rope_sin[:], ACT.Sin)
            act.activation(rope_cos[:], rope_cos[:], ACT.Sin).then_inc(trig_ready, 1)
            hi4(3)
            pooled_high(0)
            copy_u(2)
            hi4(QUAD["pool_group"])
            pooled_high(1)
            copy_u(3)
            mixed_high(0)
            pooled_high(2)
            mixed_high(1)
            pooled_high(3)
            mixed_high(2)
            mixed_high(3)
            for b in range(1, 4):
                hi4(QUAD["pool_out"] + b)
            hi4(QUAD["mlp0"])
            act.wait_ge(table_landed, 32)
            norm("mix0", resid, xhi, True)
            mlp("mlp0", QUAD["attn"], ATTN_WIDTHS)
            norm("mlp0", resid, xhi, True)

            def copy_qkv(h, odd, g):
                wait_used(act, h * 3 + (g + QUAD["attn"]))
                b = 2 * ((odd + g) % 2)
                act.activation(qkv_t[:, g].rearrange("p a t -> p (a t)"),
                               ps[:, b:b + 2, :].rearrange("p b c -> p (b c)")[:, 0:3 * T], ACT.Copy).then_inc(qkv_copied, 1)

            def copy_v(h, odd, g):
                act.wait_ge(v_turned, h * 3 + (g + 1))
                act.activation(v_rows[:, odd, g].rearrange("p a t -> p (a t)"), half(2 * ((odd + g) % 2) + 1, 1),
                               ACT.Copy).then_inc(v_ready, 1)

            def copy_turned(h):
                act.wait_ge(turned, h + 1)
                act.activation(prob_t[:], ps[:, 4:7, 0:384], ACT.Copy).then_inc(turned_copied, 1)

            def copy_head(h):
                act.wait_ge(head_done, h + 1)
                act.activation(heads_hi[:, bass.ds(h, 1), :].rearrange("p a t -> p (a t)"), half(7, 0), ACT.Copy).then_inc(head_hi, 1)

            def exps(h):
                act.wait_ge(shift_ready, h + 1)
                act.activation(score[:, :, 0:128], score[:, :, 0:128], ACT.Exp, bias=row_max[:, 0:1], scale=ATTN_SCALE,
                               accum_out=row_den[:, 0:1])
                act.activation(score[:, :, 128:384], score[:, :, 128:384], ACT.Exp, bias=row_max[:, 1:2], scale=ATTN_SCALE,
                               accum_out=row_den[:, 1:2]).then_inc(exp_done, 1)

            def attn_head(h, odd, first, last):
                q = h * 3 + QUAD["attn"]
                hi1(q + 1, 0)
                if not first:
                    copy_v(h - 1, 1 - odd, 2)
                hi1(q + 1, 1)
                if not first:
                    exps(h - 1)
                copy_qkv(h, odd, 0)
                hi1(q + 1, 2)
                hi1(q + 1, 3, ATTN_WIDTHS[3])
                hi1(q + 2, 0)
                copy_v(h, odd, 0)
                if not first:
                    copy_turned(h - 1)
                hi1(q + 2, 1)
                copy_qkv(h, odd, 1)
                hi1(q + 2, 2)
                hi1(q + 2, 3, ATTN_WIDTHS[3])
                hi1(q + 3, 0)
                if not first:
                    copy_head(h - 1)
                copy_v(h, odd, 1)
                hi1(q + 3, 1)
                copy_qkv(h, odd, 2)
                hi1(q + 3, 2)
                hi1(q + 3, 3, CW if last else ATTN_WIDTHS[3])
            attn_head(0, 0, True, False)
            with act.Fori(0, N_HEADS // 2 - 1) as i:
                attn_head(i * 2 + 1, 1, False, False)
                attn_head(i * 2 + 2, 0, False, False)
            attn_head(N_HEADS - 1, 1, False, True)
            copy_v(N_HEADS - 1, 1, 2)
            exps(N_HEADS - 1)
            copy_turned(N_HEADS - 1)
            copy_head(N_HEADS - 1)
            hi4(QUAD["attn_out"] + 1)
            hi4(QUAD["mlp1"])
            norm("mix1", resid, xhi, True)
            mlp("mlp1", QUAD["proj"])
            norm("mlp1", resid)
            norm("attn2", resid, xhi)

            hi4(QUAD["proj"] + 1)
            for b in range(4):
                if b:
                    hi4(QUAD["proj"] + b + 1)
                wait_used(act, QUAD["proj"] + b)
                n = min(4, 15 - 4 * b)
                act.activation(proj[:, 4 * b:4 * b + n, :], block_ps(b % 2)[:, 0:n, :], ACT.Copy).then_inc(block_free, 1)

            for hf in range(2):
                for ci in range(4):
                    c = 4 * hf + ci
                    act.wait_ge(bu_done, c + 1)
                    if c == 0:
                        act.wait_ge(table_ready, 1)
                    if c == 4:
                        act.wait_ge(gelu_ready, 1)
                    if c >= 1:
                        act.wait_ge(bu_ready, c)
                    for st in range(4):
                        tile = 4 * c + st
                        src = ps[:, 4 * (ci % 2) + st, :].rearrange("p (r t) -> p r t", r=2)
                        act.activation(bu_tmp[:, st, 0, :], src[:, 1, :], ACT.Copy, scale=par[:, 9, tile:tile + 1])
                        act.activation(bu_tmp[:, st, 1, :], src[:, 0, :], ACT.Copy, scale=par[:, 8, tile:tile + 1]).then_inc(bu_part, 1)
                u = proj[:, 4 * hf:4 * hf + 4, :]
                act.wait_ge(y_ready, hf + 1)
                act.activation(scratch_gelu(hf), u, ACT.Square).then_inc(gelu_sq, 1)
                act.wait_ge(gelu_arg, hf + 1)
                act.activation(scratch_gelu(hf), scratch_gelu(hf), ACT.Sigmoid).then_inc(gelu_sig, 1)
            for hf in range(2):
                act.wait_ge(gelu_ready, 2)
                act.activation(xhi[:, 4 * hf:4 * hf + 4, :], proj[:, 4 * hf:4 * hf + 4, :], ACT.Copy).then_inc(gelu_hi, 1)
            for b in range(2):
                wait_used(act, QUAD["glu"], 2 * b + 1)
                for nt in range(4):
                    ins = act.activation(scratch[:, 4 * b + nt, :], block_ps(b)[:, nt, :], ACT.Sigmoid,
                                         bias=fcol("ssm_b_glu_2", 4 * b + nt))
                ins.then_inc(glu_sig, 1)
            hi4(QUAD["mla"])
            norm("ssm", proj[:, 0:8, :], xhi)
            norm("q", proj[:, 8:12, :], cq_hi)
            norm("kv", proj[:, 12:14, :], ckv_hi)

            def mla_head(h, q, s_slot):
                wait_used(act, q - 1, s_slot)
                act.activation(proj[:, 0:2, :], ps[:, 0, :].rearrange("p (a t) -> p a t", a=2), ACT.Copy)
                act.activation(proj[:, 2:4, :], ps[:, 1, :].rearrange("p (a t) -> p a t", a=2), ACT.Copy).then_inc(m_copied, 1)
                hi1(q, s_slot)
                act.wait_ge(m_shift, h + 1)
                s = proj[:, 5:7, :].rearrange("p a t -> p (a t)")
                act.activation(s[:, 0:128], s[:, 0:128], ACT.Exp, bias=m_max[:, 0:1], scale=MLA_SCALE, accum_out=m_den[:, 0:1])
                act.activation(s[:, 128:384], s[:, 128:384], ACT.Exp, bias=m_max[:, 1:2], scale=MLA_SCALE,
                               accum_out=m_den[:, 1:2]).then_inc(m_exp, 1)
                act.wait_ge(m_turned, h + 1)
                act.activation(proj[:, 7:9, :].rearrange("p a t -> p (a t)")[:, 0:384], ps[:, 4, 0:384], ACT.Copy).then_inc(m_pt, 1)
                act.wait_ge(m_out, h + 1)
                act.activation(scratch[:, bass.ds(h, 1), :].rearrange("p a t -> p (a t)"), half(5, 0), ACT.Copy).then_inc(m_out_copied, 1)
            with act.Fori(0, 2) as i:
                for s in range(SLOTS):
                    mla_head(i * 4 + s, i + (QUAD["mla"] + 1), s)
            act.wait_ge(m_out_copied, N_HEADS)
            act.sem_inc(norm_src, 1)
            norm("mla", scratch[:, 0:8, :], xhi[:, 8:16, :])
            for b in range(1, 4):
                hi4(QUAD["out2"] + b)
            hi4(QUAD["ffn"])
            norm("ffn2", resid, xhi)

            q0, b0, h0, n = QUAD["ffn"], BLOCK["ffn"], HIDDEN["ffn"], FF2 // HID

            def conv_first(g, half_):
                wait_used(act, up_quad(q0, g, 3) + half_)
                if not (isinstance(g, int) and g == 0):
                    act.wait_ge(hidden_ready, g + h0)
                for nt in range(4):
                    i = g * 4 + (half_ * (FF2 // P) + nt)
                    ins = act.activation(conv[:, 4 * half_ + nt, :], block_ps(half_)[:, nt, :], ACT.Identity,
                                         scale=fcol("ffn_conv_w_2", i + 2 * (2 * FF2 // P)), bias=fcol("ffn_conv_b_2", i))
                ins.then_inc(conv_start, 1)

            def gate(g):
                act.wait_ge(conv_done, g * 2 + 1)
                act.activation(gate_sig[:], conv[:, 0:4, :], ACT.Sigmoid).then_inc(sig_ready, 1)

            def ffn_split(g):
                act.wait_ge(hidden_ready, g + (h0 + 1))
                if not (isinstance(g, int) and g == 0):
                    wait_used(act, g * 3 + (q0 + 1))
                act.activation(hid_hi[:], hid[:], ACT.Copy).then_inc(hidden_hi, 1)

            def group(g, q):
                conv_first(g, 0)
                hi1(q, 0)
                gate(g)
                for s in range(1, SLOTS):
                    hi1(q, s)
                conv_first(g, 1)
                hi4(q + 1)
                ffn_split(g)
            hi4(q0 + 1)
            group(0, q0 + 2)
            with act.Fori(0, n - 2) as g:
                group(g + 1, g * 3 + (q0 + 4))
                hi4(g * 3 + (q0 + 6))
            group(n - 1, q0 + 3 * n - 2)
            norm("final", resid)

        @block.vector
        def _(dve):
            step = Steps(dve, dve_steps)

            def lo1(q, s, width=CW):
                dve.wait_ge(hi_ready, q * SLOTS + (s + 1))
                dve.tensor_tensor(wlo[:, s, 0:width], raw[:, s, 0:width], whi[:, s, 0:width].bitcast(F32),
                                  ALU.subtract).then_inc(lo_ready, 1)

            def lo4(q, widths=(CW,) * 4):
                for s in range(SLOTS):
                    lo1(q, s, widths[s])

            def lo4_add(q, q_down, widths=(CW,) * 4):
                for s in range(SLOTS):
                    lo1(q, s, widths[s])
                    add_down(q_down, s)

            def norm(name, src, gain, bias=None, dst_hi=None, dst_lo=None, next_src=False):
                k = NORM[name]
                n, mean, t0 = NORMS[k][1], NORMS[k][2], PIECE0[k]
                w = min(4, n)
                off = DT - n
                pieces = range(PIECES[k])
                y = src if mean else scratch[:, off:DT, :]
                if mean:
                    dve.wait_ge(norm_mean, k + 1)
                    for p in pieces:
                        s = src[:, p * w:p * w + w, :]
                        dve.tensor_tensor(s, s, half(7, 0).unsqueeze(1).to_broadcast([P, w, T]), ALU.subtract).then_inc(norm_xc, 1)
                dve.wait_ge(norm_std, k + 1)
                step(dve.reciprocal(rstd[:], std[:]))
                step.settle()

                def lo(p):
                    dve.wait_ge(norm_hi, LO0[k] + p + 1)
                    a = slice(p * w, p * w + w)
                    dve.tensor_tensor(dst_lo[:, a, :], y[:, a, :], dst_hi[:, a, :].bitcast(F32), ALU.subtract).then_inc(norm_lo, 1)
                for p in pieces:
                    if mean:
                        s = src[:, p * w:p * w + w, :]
                        step(dve.tensor_tensor(s, s, rstd[:].unsqueeze(1).to_broadcast([P, w, T]), ALU.mult))
                        step.settle()
                    for i in range(p * w, p * w + w):
                        if mean:
                            ins = dve.tensor_scalar(y[:, i, :], src[:, i, :], fcol(gain[0], gain[1] + i), fcol(bias[0], bias[1] + i),
                                                    ALU.mult, ALU.add)
                        else:
                            ins = dve.scalar_tensor_tensor(out=y[:, i, :], in0=src[:, i, :], scalar=fcol(gain[0], gain[1] + i),
                                                           in1=rstd[:], op0=ALU.mult, op1=ALU.mult)
                    ins.then_inc(norm_y, 1)
                    if dst_lo is not None and p >= 1:
                        lo(p - 1)
                if dst_lo is not None:
                    lo(PIECES[k] - 1)
                if next_src:
                    dve.wait_ge(norm_y, t0 + PIECES[k])
                    dve.sem_inc(norm_src, 1)

            def add_down(q, nb):
                wait_used(dve, q, nb)
                r = resid[:, 4 * nb:4 * nb + 4, :]
                return dve.tensor_tensor(r, r, block_ps(2 + nb % 2), ALU.add).then_inc(down_free, 1)

            def mlp(name, next_quad, next_widths=(CW,) * 4):
                q0, h0 = QUAD[name], HIDDEN[name]
                n = FF // HID

                def split(g):
                    dve.wait_ge(hidden_hi, g + (h0 + 1))
                    dve.tensor_tensor(hid_lo[:], hid[:], hid_hi[:].bitcast(F32), ALU.subtract).then_inc(hidden_lo, 1)

                lo4(q0 + 1)
                split(0)
                with dve.Fori(0, n - 2) as g:
                    lo4(g * 2 + (q0 + 2))
                    lo4_add(g * 2 + (q0 + 3), g * 2 + (q0 + 2))
                    split(g + 1)
                lo4(q0 + 2 * n - 2)
                lo4_add(q0 + 2 * n - 1, q0 + 2 * n - 2)
                split(n - 1)
                lo4_add(next_quad, q0 + 2 * n - 1, next_widths)
                dve.wait_ge(down_free, 4 * (h0 + n) + 2)
                dve.sem_inc(norm_src, 1)

            def add_block(b, nb, q, s=SLOTS - 1):
                wait_used(dve, q, s)
                r = resid[:, 4 * nb:4 * nb + 4, :]
                dve.tensor_tensor(r, r, block_ps(b % 2), ALU.add).then_inc(block_free, 1)

            dve.sem_inc(lo_ready, SLOTS)
            dve.memset(ones[:], 1.0)
            dve.memset(ones_mean[:], 1.0 / D).then_inc(ones_ready, 1)
            dve.memset(win_a[:, :, 0:PAD], 0.0)
            dve.memset(win_b[:, :, 0:PAD], 0.0)
            dve.memset(u_pad[:, :, :, 0:PAD].rearrange("p a n t -> p (a n) t"), 0.0).then_inc(pad_ready, 1)
            def op(out_, a, b_, o):
                step(dve.tensor_tensor(out_, a, b_, o))
                step.settle()

            def reduce_angle(out_, angle, tmp, quarter):
                def ts(o, a, s1, s2, o1, o2=ALU.bypass):
                    step(dve.tensor_scalar(o, a, s1, s2, o1, o2) if s2 is not None else dve.tensor_scalar(o, a, s1, None, o1))
                    step.settle()
                two_pi = 6.283185307179586
                c1 = 6.28125
                c2 = 0.0019350051879882812
                c3 = two_pi - c1 - c2
                magic = 12582912.0
                ts(tmp, angle, 1.0 / two_pi, 0.25 if quarter else 0.0, ALU.mult, ALU.add)
                ts(tmp, tmp, magic, None, ALU.add)
                ts(tmp, tmp, magic, None, ALU.subtract)
                for n, c in enumerate((c1, c2, c3)):
                    step(dve.scalar_tensor_tensor(out=out_, in0=tmp, scalar=-c, in1=angle if n == 0 else out_, op0=ALU.mult, op1=ALU.add))
                    step.settle()
                ts(out_, out_, two_pi / 4 if quarter else 0.0, 3.1415925, ALU.add, ALU.min)
                ts(out_, out_, -3.1415925, None, ALU.max)

            dve.wait_ge(lam_landed, 32)
            lr, li = lam[:, 0, :], lam[:, 1, :]
            dve.wait_ge(trig_ready, 1)
            dt = par[:, 0, :]
            op(par[:, 1, :], lr, dt, ALU.mult)
            dve.sem_inc(angles_ready, 1)
            op(par[:, 4, :], li, dt, ALU.mult)
            reduce_angle(par[:, 2, :], par[:, 4, :], par[:, 5, :], False)
            dve.sem_inc(angles_ready, 1)
            reduce_angle(par[:, 3, :], par[:, 4, :], par[:, 5, :], True)
            dve.sem_inc(angles_ready, 1)
            for p in range(4):
                a = slice(4 * p, 4 * p + 4)
                dve.wait_ge(x_hi_ready, p + 1)
                dve.tensor_tensor(xlo[:, a, :], resid[:, a, :], xhi[:, a, :].bitcast(F32), ALU.subtract).then_inc(x_lo_ready, 1)

            lo4(0)
            dve.wait_ge(trig_ready, 3)
            a_re, a_im, n_re, den, z_re, z_im, nz_im, na_im = (par[:, i, :] for i in (4, 5, 6, 10, 7, 8, 9, 11))
            tmp = par[:, 12, :]
            op(a_re, par[:, 1, :], par[:, 3, :], ALU.mult)
            op(a_im, par[:, 1, :], par[:, 2, :], ALU.mult)
            step(dve.tensor_scalar(n_re, a_re, 1.0, None, ALU.subtract))
            step.settle()
            op(den, lr, lr, ALU.mult)
            op(tmp, li, li, ALU.mult)
            op(den, den, tmp, ALU.add)
            op(z_re, n_re, lr, ALU.mult)
            op(tmp, a_im, li, ALU.mult)
            op(z_re, z_re, tmp, ALU.add)
            op(z_im, a_im, lr, ALU.mult)
            op(tmp, n_re, li, ALU.mult)
            op(z_im, z_im, tmp, ALU.subtract)
            step(dve.reciprocal(den, den))
            step.settle()
            op(z_re, z_re, den, ALU.mult)
            op(z_im, z_im, den, ALU.mult)
            step(dve.tensor_scalar(nz_im, z_im, -1.0, None, ALU.mult))
            step(dve.tensor_scalar(na_im, a_im, -1.0, None, ALU.mult))
            step(dve.tensor_copy(pow_re[:, :, 0], a_re))
            step(dve.tensor_copy(pow_im[:, :, 0], a_im))
            step.settle()

            def rope_tables():
                rope_tmp, rope_angle = rope_a, k_rope
                step(dve.tensor_copy(rope_angle, pos_i))
                step.settle()
                dve.wait_ge(table_landed, 32)
                step(dve.tensor_scalar(rope_angle, rope_angle, ccol("freq", rows=ROPE), None, ALU.mult))
                step.settle()
                reduce_angle(rope_sin[:], rope_angle, rope_tmp, False)
                dve.sem_inc(angles_ready, 1)
                reduce_angle(rope_cos[:], rope_angle, rope_tmp, True)
                dve.sem_inc(angles_ready, 1)

            def powers(j0, j1):
                for j in range(j0, j1):
                    op(pow_re[:, :, j], pow_re[:, :, j - 1], a_re, ALU.mult)
                    op(tmp, pow_im[:, :, j - 1], a_im, ALU.mult)
                    op(pow_re[:, :, j], pow_re[:, :, j], tmp, ALU.subtract)
                    op(pow_im[:, :, j], pow_im[:, :, j - 1], a_re, ALU.mult)
                    op(tmp, pow_re[:, :, j - 1], a_im, ALU.mult)
                    op(pow_im[:, :, j], pow_im[:, :, j], tmp, ALU.add)

            def pooled_low(g):
                dve.wait_ge(pooled_hi, g + 1)
                res = win_a if (4 - g) % 2 else win_b
                dve.tensor_tensor(pool_lo[:, g % 2], res[:, :, PAD:PAD + T], pool_hi[:, g % 2].bitcast(F32),
                                  ALU.subtract).then_inc(pooled_lo, 1)

            def mixed_low(g):
                grp = 3 - g
                b = BLOCK["pool_group"] + g
                wait_used(dve, QUAD["pool_group"], g)
                for nt in range(4):
                    ins = dve.tensor_scalar(u_pad[:, g, nt, PAD:PAD + T], block_ps(b % 2)[:, nt, :],
                                            fcol("pool_scale", 4 * grp + nt), None, ALU.mult)
                    if nt == 3:
                        ins.then_inc(y_scaled, 1)
                dve.wait_ge(y_hi, g + 1)
                dve.tensor_tensor(xlo[:, 4 * grp:4 * grp + 4, :], u_pad[:, g, :, PAD:PAD + T],
                                  xhi[:, 4 * grp:4 * grp + 4, :].bitcast(F32), ALU.subtract).then_inc(y_lo, 1)
                dve.sem_inc(block_free, 1)
                lo1(QUAD["pool_out"], g)
            lo4(1)
            rope_tables()
            powers(1, 6)
            lo4(2)
            powers(6, 11)
            lo4(3)
            pooled_low(0)
            powers(11, SCAN)
            lo4(QUAD["pool_group"])
            dve.sem_inc(table_ready, 1)
            pooled_low(1)
            dve.wait_ge(table_landed, 32)
            mixed_low(0)
            pooled_low(2)
            mixed_low(1)
            pooled_low(3)
            mixed_low(2)
            mixed_low(3)
            dve.wait_ge(resid_ready, 4)
            for b in range(4):
                lo4(QUAD["pool_out"] + b + 1)
                add_block(BLOCK["pool_out"] + b, b, QUAD["pool_out"] + b)
            dve.wait_ge(block_free, 2 + BLOCK["mlp0"])
            dve.sem_inc(norm_src, 1)
            norm("mix0", resid, ("ln_mix_g", 0), ("ln_mix_b", 0), xhi, xlo)
            dve.wait_ge(resid_ready, 8)
            mlp("mlp0", QUAD["attn"], ATTN_WIDTHS)
            norm("mlp0", resid, ("ln_mlp_g", 0), ("ln_mlp_b", 0), xhi, xlo)

            def shift(h):
                dve.wait_ge(scores_done, h + 1)
                for g in range(N_GROUPS):
                    step(dve.scalar_tensor_tensor(
                        out=score[:, g, :], in0=ccol("dist", 384 * g, 384),
                        scalar=const[:, bass.ds(h + (CONST["slope"] + g * N_HEADS), 1)],
                        in1=ps[:, 4 + g, 0:384], op0=ALU.mult, op1=ALU.add))
                step.settle()
                step(dve.tensor_reduce(row_max[:, 0:1], score[:, :, 0:128], AX.XY, ALU.max))
                step(dve.tensor_reduce(row_max[:, 1:2], score[:, :, 128:384], AX.XY, ALU.max))
                step.settle()
                dve.tensor_scalar(row_max[:], row_max[:], -ATTN_SCALE, None, ALU.mult).then_inc(shift_ready, 1)

            def probs(h):
                dve.wait_ge(exp_done, h + 1)
                step(dve.reciprocal(row_den[:], row_den[:]))
                step.settle()
                dve.tensor_scalar(score[:, :, 0:128], score[:, :, 0:128], row_den[:, 0:1], None, ALU.mult)
                dve.tensor_scalar(score[:, :, 128:384], score[:, :, 128:384], row_den[:, 1:2], None, ALU.mult).then_inc(prob_ready, 1)

            def head_low(h):
                dve.wait_ge(head_hi, h + 1)
                dve.tensor_tensor(heads_lo[:, bass.ds(h, 1), :].rearrange("p a t -> p (a t)"), half(7, 0),
                                  heads_hi[:, bass.ds(h, 1), :].rearrange("p a t -> p (a t)").bitcast(F32), ALU.subtract).then_inc(head_lo, 1)

            def attn_head(h, first, last):
                q = h * 3 + QUAD["attn"]
                lo1(q + 1, 0)
                if not first:
                    shift(h - 1)
                lo1(q + 1, 1)
                if not first:
                    probs(h - 1)
                lo1(q + 1, 2)
                lo1(q + 1, 3, ATTN_WIDTHS[3])
                lo4(q + 2, ATTN_WIDTHS)
                lo1(q + 3, 0)
                if not first:
                    head_low(h - 1)
                lo1(q + 3, 1)
                lo1(q + 3, 2)
                lo1(q + 3, 3, CW if last else ATTN_WIDTHS[3])
            attn_head(0, True, False)
            with dve.Fori(0, N_HEADS // 2 - 1) as i:
                step.enter(i, 12)
                attn_head(i * 2 + 1, False, False)
                attn_head(i * 2 + 2, False, False)
                step.leave(N_HEADS // 2 - 1)
            attn_head(N_HEADS - 1, False, True)
            shift(N_HEADS - 1)
            probs(N_HEADS - 1)
            head_low(N_HEADS - 1)
            lo4(QUAD["attn_out"] + 1)
            dve.wait_ge(resid_ready, 12)
            b = BLOCK["attn_out"]
            add_block(b, 0, QUAD["attn_out"], 1)
            add_block(b + 1, 1, QUAD["attn_out"], 3)
            lo4(QUAD["mlp1"])
            add_block(b + 2, 2, QUAD["attn_out"] + 1, 1)
            add_block(b + 3, 3, QUAD["attn_out"] + 1, 3)
            dve.wait_ge(block_free, 2 + b + 4)
            dve.sem_inc(norm_src, 1)
            norm("mix1", resid, ("ln_mix_g", DT), ("ln_mix_b", DT), xhi, xlo)
            dve.wait_ge(resid_ready, 16)
            mlp("mlp1", QUAD["proj"])
            norm("mlp1", resid, ("ln_mlp_g", DT), ("ln_mlp_b", DT), next_src=True)
            norm("attn2", resid, ("attn_norm_w_2", 0), None, xhi, xlo)

            lo4(QUAD["proj"] + 1)
            for b in range(1, 4):
                lo4(QUAD["proj"] + b + 1)
            a_re, a_im, na_im = (par[:, i, :] for i in (4, 5, 11))

            sv = state[:].rearrange("p r s (b j) -> p r s b j", j=SCAN)
            for hf in range(2):
                for ci in range(4):
                    c = 4 * hf + ci
                    for st in range(4):
                        tile = 4 * c + st
                        dve.wait_ge(bu_part, 4 * c + st + 1)
                        src = ps[:, 4 * (ci % 2) + st, :].rearrange("p (r t) -> p r t", r=2)
                        zr = par[:, 7, tile:tile + 1]
                        dve.scalar_tensor_tensor(out=state[:, 0, 4 * ci + st, :], in0=src[:, 0, :], scalar=zr,
                                                 in1=bu_tmp[:, st, 0, :], op0=ALU.mult, op1=ALU.add)
                        ins = dve.scalar_tensor_tensor(out=state[:, 1, 4 * ci + st, :], in0=src[:, 1, :], scalar=zr,
                                                       in1=bu_tmp[:, st, 1, :], op0=ALU.mult, op1=ALU.add)
                    ins.then_inc(bu_ready, 1)
                dve.wait_ge(bu_ready, 4 * hf + 4)
                t16 = slice(16 * hf, 16 * hf + 16)

                def along(ap, n):
                    return ap.unsqueeze(2).to_broadcast([P, 16, n])
                ar2 = a_re[:, t16].unsqueeze(1).unsqueeze(3).to_broadcast([P, 2, 16, 16])
                with dve.Fori(0, SCAN - 1) as j:
                    step.enter(j, 5)
                    cur = sv[:, :, :, :, bass.ds(j + 1, 1)].rearrange("p r s b a -> p r s (b a)")
                    prev = sv[:, :, :, :, bass.ds(j, 1)].rearrange("p r s b a -> p r s (b a)")
                    step(dve.tensor_tensor(scan_a[:], prev, ar2, ALU.mult))
                    step(dve.tensor_tensor(scan_b[:, 0], prev[:, 1], along(na_im[:, t16], 16), ALU.mult))
                    step(dve.tensor_tensor(scan_b[:, 1], prev[:, 0], along(a_im[:, t16], 16), ALU.mult))
                    step.settle()
                    step(dve.tensor_tensor(scan_a[:], scan_a[:], scan_b[:], ALU.add))
                    step.settle()
                    step(dve.tensor_tensor(cur, cur, scan_a[:], ALU.add))
                    step.settle()
                    step.leave(SCAN - 1)
                pr16, pi16 = pow_re[:, t16, SCAN - 1], pow_im[:, t16, SCAN - 1]
                ends = sv[:, :, :, :, SCAN - 1]
                with dve.Fori(0, SCAN - 1) as b:
                    step.enter(b, 8)
                    cur = ends[:, :, :, bass.ds(b + 1, 1)].rearrange("p r s a -> p r (s a)")
                    prev = ends[:, :, :, bass.ds(b, 1)].rearrange("p r s a -> p r (s a)")
                    step(dve.tensor_tensor(scan_a[:, 0, 0], prev[:, 0], pr16, ALU.mult))
                    step(dve.tensor_tensor(scan_a[:, 0, 1], prev[:, 1], pi16, ALU.mult))
                    step(dve.tensor_tensor(scan_a[:, 0, 2], prev[:, 0], pi16, ALU.mult))
                    step(dve.tensor_tensor(scan_a[:, 0, 3], prev[:, 1], pr16, ALU.mult))
                    step.settle()
                    step(dve.tensor_tensor(scan_b[:, 0, 0], scan_a[:, 0, 0], scan_a[:, 0, 1], ALU.subtract))
                    step(dve.tensor_tensor(scan_b[:, 0, 1], scan_a[:, 0, 2], scan_a[:, 0, 3], ALU.add))
                    step.settle()
                    step(dve.tensor_tensor(cur[:, 0], cur[:, 0], scan_b[:, 0, 0], ALU.add))
                    step(dve.tensor_tensor(cur[:, 1], cur[:, 1], scan_b[:, 0, 1], ALU.add))
                    step.settle()
                    step.leave(SCAN - 1)
                f = bu_tmp[:].rearrange("p a b t -> p (a b t)")[:, 0:4 * 15 * 15].rearrange("p (s b j) -> p s b j", b=15, j=15)
                f2 = bu_tmp[:].rearrange("p a b t -> p (a b t)")[:, 1024:1024 + 900].rearrange("p (s b j) -> p s b j", b=15, j=15)
                for ci in range(4):
                    ss = slice(4 * ci, 4 * ci + 4)
                    tt = slice(16 * hf + 4 * ci, 16 * hf + 4 * ci + 4)

                    def powb(ap):
                        return ap[:, tt, 0:15].unsqueeze(2).to_broadcast([P, 4, 15, 15])

                    def carry(r):
                        return ends[:, r, ss, 0:15].unsqueeze(3).to_broadcast([P, 4, 15, 15])
                    for r, (pa, pb, o) in enumerate(((pow_re, pow_im, ALU.subtract), (pow_im, pow_re, ALU.add))):
                        tgt = sv[:, r, ss, 1:16, 0:15]
                        step(dve.tensor_tensor(f, powb(pa), carry(0), ALU.mult))
                        step(dve.tensor_tensor(f2, powb(pb), carry(1), ALU.mult))
                        step.settle()
                        step(dve.tensor_tensor(tgt, tgt, f, ALU.add))
                        step.settle()
                        step(dve.tensor_tensor(tgt, tgt, f2, o))
                        step.settle()
                    dve.sem_inc(scan_done, 1)
                for ci in range(4):
                    c = 4 * hf + ci
                    dve.wait_ge(y_done, c + 1)
                    step(dve.scalar_tensor_tensor(out=proj[:, c, :], in0=proj[:, c, :], scalar=fcol("ssm_d_2", c),
                                                  in1=half(ci, 0), op0=ALU.mult, op1=ALU.add))
                    step.settle()
                    step(dve.tensor_tensor(proj[:, c, :], proj[:, c, :], half(ci, 1), ALU.subtract))
                step.settle()
                dve.sem_inc(y_ready, 1)
                k = 2.0 * (2.0 / 3.141592653589793) ** 0.5
                u = proj[:, 4 * hf:4 * hf + 4, :]
                dve.wait_ge(gelu_sq, hf + 1)
                step(dve.tensor_scalar(scratch_gelu(hf), scratch_gelu(hf), 0.044715 * k, k, ALU.mult, ALU.add))
                step.settle()
                dve.tensor_tensor(scratch_gelu(hf), scratch_gelu(hf), u, ALU.mult).then_inc(gelu_arg, 1)
                dve.wait_ge(gelu_sig, hf + 1)
                dve.tensor_tensor(u, u, scratch_gelu(hf), ALU.mult).then_inc(gelu_ready, 1)
            for hf in range(2):
                a = slice(4 * hf, 4 * hf + 4)
                dve.wait_ge(gelu_hi, hf + 1)
                dve.tensor_tensor(xlo[:, a, :], proj[:, a, :], xhi[:, a, :].bitcast(F32), ALU.subtract).then_inc(gelu_lo, 1)
            lo4(QUAD["mla"])
            for b in range(2):
                a = slice(4 * b, 4 * b + 4)
                dve.wait_ge(glu_sig, b + 1)
                dve.tensor_tensor(proj[:, a, :], proj[:, a, :], scratch[:, a, :], ALU.mult).then_inc(block_free, 1)
            dve.wait_ge(block_free, 2 + BLOCK["out2"])
            dve.sem_inc(norm_src, 3)
            norm("ssm", proj[:, 0:8, :], ("ssm_out_norm_w_2", 0), None, xhi, xlo)
            norm("q", proj[:, 8:12, :], ("mla_q_norm_w_2", 0), None, cq_hi, cq_lo)
            norm("kv", proj[:, 12:14, :], ("mla_kv_norm_w_2", 0), None, ckv_hi, ckv_lo)

            def rope(n, dst):
                dve.wait_ge(rope_done, n + 1)
                step(dve.tensor_tensor(rope_a, ps[0:ROPE, 2, 0:T], rope_cos[:], ALU.mult))
                step(dve.tensor_tensor(dst, ps[0:ROPE, 2, T:2 * T], rope_sin[:], ALU.mult))
                step.settle()
                dve.tensor_tensor(dst, dst, rope_a, ALU.add).then_inc(rope_ready, 1)

            def mla_head(h, q, s_slot):
                lo1(q, s_slot)
                rope(h + 1, proj[0:ROPE, 4, :])
                s = proj[:, 5:7, :].rearrange("p a t -> p (a t)")
                dve.wait_ge(m_score, h + 1)
                step(dve.tensor_tensor(s[:, 0:384], ps[:, 3, 0:384], ccol("causal"), ALU.add))
                step.settle()
                step(dve.tensor_reduce(m_max[:, 0:1], s[:, 0:128], AX.X, ALU.max))
                step(dve.tensor_reduce(m_max[:, 1:2], s[:, 128:384], AX.X, ALU.max))
                step.settle()
                dve.tensor_scalar(m_max[:], m_max[:], -MLA_SCALE, None, ALU.mult).then_inc(m_shift, 1)
                dve.wait_ge(m_exp, h + 1)
                step(dve.reciprocal(m_den[:], m_den[:]))
                step.settle()
                dve.tensor_scalar(s[:, 0:128], s[:, 0:128], m_den[:, 0:1], None, ALU.mult)
                dve.tensor_scalar(s[:, 128:384], s[:, 128:384], m_den[:, 1:2], None, ALU.mult).then_inc(m_prob, 1)
            dve.wait_ge(trig_ready, 4)
            rope(0, k_rope)
            with dve.Fori(0, 2) as i:
                step.enter(i, SLOTS * 6)
                for s in range(SLOTS):
                    mla_head(i * 4 + s, i + (QUAD["mla"] + 1), s)
                step.leave(2)
            norm("mla", scratch[:, 0:8, :], ("mla_out_norm_w_2", 0), None, xhi[:, 8:16, :], xlo[:, 8:16, :])
            for b in range(4):
                lo4(QUAD["out2"] + b + 1)
                add_block(BLOCK["out2"] + b, b, QUAD["out2"] + b)
            dve.wait_ge(block_free, 2 + BLOCK["ffn"])
            dve.sem_inc(norm_src, 1)
            norm("ffn2", resid, ("ffn_norm_w_2", 0), None, xhi, xlo)

            q0, h0, n = QUAD["ffn"], HIDDEN["ffn"], FF2 // HID

            def conv_rest(g, half_):
                dve.wait_ge(conv_start, g * 2 + (half_ + 1))
                for lag, tap in ((1, 1), (2, 0)):
                    for nt in range(4):
                        i = g * 4 + (half_ * (FF2 // P) + nt)
                        o = conv[:, 4 * half_ + nt, lag:T]
                        ins = dve.scalar_tensor_tensor(out=o, in0=block_ps(half_)[:, nt, 0:T - lag],
                                                       scalar=fcol("ffn_conv_w_2", i + tap * (2 * FF2 // P)), in1=o,
                                                       op0=ALU.mult, op1=ALU.add)
                        if lag == 1:
                            step(ins)
                    if lag == 1:
                        step.settle()
                ins.then_inc(conv_done, 1)
                dve.wait_ge(conv_done, g * 2 + (half_ + 1))
                dve.sem_inc(block_free, 1)

            def group(g, q, adds):
                conv_rest(g, 0)
                lo1(q, 0)
                dve.wait_ge(sig_ready, g + 1)
                if not (isinstance(g, int) and g == 0):
                    dve.wait_ge(hidden_lo, g + h0)
                step(dve.tensor_tensor(hid[:], conv[:, 0:4, :], gate_sig[:], ALU.mult))
                for s in range(1, SLOTS):
                    lo1(q, s)
                conv_rest(g, 1)
                for s in range(SLOTS):
                    lo1(q + 1, s)
                    if adds:
                        add_down(q, s)
                    if s == 0:
                        step.settle()
                        dve.tensor_tensor(hid[:], hid[:], conv[:, 4:8, :], ALU.mult).then_inc(hidden_ready, 1)
                dve.wait_ge(hidden_hi, g + (h0 + 1))
                dve.tensor_tensor(hid_lo[:], hid[:], hid_hi[:].bitcast(F32), ALU.subtract).then_inc(hidden_lo, 1)
            lo4(q0 + 1)
            group(0, q0 + 2, False)
            with dve.Fori(0, n - 2) as g:
                step.enter(g, 9)
                group(g + 1, g * 3 + (q0 + 4), True)
                lo4(g * 3 + (q0 + 6))
                step.leave(n - 2)
            group(n - 1, q0 + 3 * n - 2, True)
            for nb in range(4):
                add_down(q0 + 3 * n - 1, nb)
            dve.wait_ge(down_free, 2 + 4 * (h0 + n))
            dve.sem_inc(norm_src, 1)
            norm("final", resid, ("final_norm_w_2", 0))

        @block.gpsimd
        def _(pool):
            step = Steps(pool, pool_steps)
            pool.wait_ge(pad_ready, 1)
            pool.wait_ge(table_landed, 32)
            for g in range(4):
                grp = 3 - g
                w = POOL_WINDOWS[grp]
                pool.wait_ge(block_free, 2 + g + 1)
                src, shift = u_pad[:, g], 1
                bufs = (win_a, win_b)
                if g >= 1:
                    pool.wait_ge(pooled_lo, g)
                n = 0
                while shift < w:
                    dst = bufs[n % 2]
                    step(pool.tensor_tensor(dst[:, :, PAD:PAD + T], src[:, :, PAD:PAD + T],
                                            src[:, :, PAD - shift:PAD - shift + T], ALU.add))
                    step.settle()
                    src, shift, n = dst, shift * 2, n + 1
                head, tail = src[:, :, PAD:2 * PAD], src[:, :, 2 * PAD:PAD + T]
                step(pool.tensor_tensor(head, head, ccol("count", PAD * grp, PAD).unsqueeze(1).to_broadcast([P, 4, PAD]), ALU.mult))
                step(pool.tensor_scalar(tail, tail, 1.0 / w, None, ALU.mult))
                step.settle()
                assert (src is win_a) == ((4 - g) % 2 == 1)
                pool.tensor_tensor(src[:, :, PAD:PAD + T], src[:, :, PAD:PAD + T], u_pad[:, g, :, PAD:PAD + T],
                                   ALU.subtract).then_inc(pooled, 1)
            for n in range(16):
                hf, kind, ci = n // 8, (n // 4) % 2, n % 4
                if n == 0:
                    pool.wait_ge(norm_lo, LO0[NORM["attn2"]] + 4)
                elif kind == 1:
                    pool.wait_ge(bu_done, 4 * hf + ci + 1)
                elif n >= 8:
                    pool.wait_ge(y_done, ci + 1)
                pool.dma_start(blocks[:, ci, :], ssm_blocks[n]).then_inc(blocks_landed[ci], 16)

        @block.tensor
        def _(pe):
            pe.sem_inc(chunk_used, SLOTS)
            pe.sem_inc(block_free, 2)
            pe.sem_inc(down_free, 2)
            pe.sem_inc(head_lo, 1)

            def chunk(q, s):
                pe.wait_ge(lo_ready, q * SLOTS + (SLOTS + s + 1))

            def three(o, w_hi, w_lo, x_hi, x_lo, first, last):
                pe.matmul(o, w_hi, x_hi, start=first, stop=False)
                pe.matmul(o, w_hi, x_lo, start=False, stop=False)
                return pe.matmul(o, w_lo, x_hi, start=False, stop=last)

            def tile(o, s, off, stride, kts, xh, xl):
                for k in range(kts):
                    c = slice(off + k * stride, off + k * stride + P)
                    ins = three(o, whi[:, s, c], wlo[:, s, c], xh[:, k, :], xl[:, k, :], k == 0, k == kts - 1)
                return ins

            def quad_block(q, set_, free, x_ready=None, tiles=4, order=range(DT)):
                pe.wait_ge(block_free, free)
                for s in range(tiles):
                    chunk(q, s if s < tiles - 1 else SLOTS - 1)
                    o = block_ps(set_)[:, s, :]
                    for n, k in enumerate(order):
                        if s == 0 and x_ready is not None and n % 4 == 0:
                            pe.wait_ge(x_ready[0], x_ready[1] + n // 4 + 1)
                        c = slice(k * P, k * P + P)
                        ins = three(o, whi[:, s, c], wlo[:, s, c], xhi[:, k, :], xlo[:, k, :], n == 0, n == DT - 1)
                    if s < tiles - 1:
                        ins.then_inc(chunk_used, 1)
                ins.then_inc(chunk_used, 1 + SLOTS - tiles)

            def norm(name, src):
                k = NORM[name]
                n, mean, t0 = NORMS[k][1], NORMS[k][2], PIECE0[k]
                w = min(4, n)
                off = DT - n
                if mean:
                    pe.wait_ge(norm_src, k + 1)
                    for i in range(n):
                        ins = pe.matmul(half(7, 0), ones_mean[:], src[:, i, :], start=i == 0, stop=i == n - 1)
                    ins.then_inc(norm_mean, 1)
                for p in range(PIECES[k]):
                    pe.wait_ge(norm_sq, t0 + p + 1)
                    for i in range(p * w, p * w + w):
                        ins = pe.matmul(half(6, 0), ones[:], scratch[:, off + i, :], start=i == 0, stop=i == n - 1)
                ins.then_inc(norm_var, 1)

            def down(q, m, hidden):
                pe.wait_ge(hidden_lo, hidden)
                for s in range(SLOTS):
                    chunk(q, s)
                    pe.wait_ge(down_free, m + (s + 1))
                    for nt in range(4):
                        ins = tile(block_ps(2 + s % 2)[:, nt, :], s, nt * P, 512, 4, hid_hi, hid_lo)
                    ins.then_inc(chunk_used, 1)

            def mlp(name):
                q0, b0, h0, n = QUAD[name], BLOCK[name], HIDDEN[name], FF // HID

                def up(g, x_ready=None):
                    quad_block(q0 if isinstance(g, int) else g * 2 + (q0 - 1), 0, g + (b0 + 2), x_ready)
                up(0, (norm_lo, LO0[NORM["mix" + name[-1]]]))
                with pe.Fori(0, n - 1) as g:
                    up(g + 1)
                    down(g * 2 + (q0 + 2), g * 4 + 4 * h0, g + (h0 + 1))
                down(q0 + 2 * n - 1, 4 * (h0 + n - 1), h0 + n)

            pe.wait_ge(ones_ready, 1)
            for b in range(4):
                quad_block(b, b % 2, b + 1, (x_lo_ready, 0) if b == 0 else None)
            for g in range(4):
                b = BLOCK["pool_group"] + g
                pe.wait_ge(pooled_lo, g + 1)
                pe.wait_ge(block_free, b + 1)
                chunk(QUAD["pool_group"], g)
                for nt in range(4):
                    ins = tile(block_ps(b % 2)[:, nt, :], g, nt * P, 512, 4, pool_hi[:, g % 2], pool_lo[:, g % 2])
                ins.then_inc(chunk_used, 1)
            for b in range(4):
                n = BLOCK["pool_out"] + b
                quad_block(QUAD["pool_out"] + b, n % 2, n + 1, (y_lo, 0) if b == 0 else None,
                           order=[4 * grp + i for grp in (3, 2, 1, 0) for i in range(4)])
            norm("mix0", resid)
            mlp("mlp0")
            norm("mlp0", resid)

            pe.wait_ge(norm_lo, LO0[NORM["mlp0"]] + 4)

            pe.wait_ge(table_landed, 32)

            def qkv(h, odd, g, part):
                n = h * 3 + g
                q = n + QUAD["attn"]
                b = 2 * ((odd + g) % 2)
                if part == 0 and not (isinstance(h, int) and n < 2):
                    pe.wait_ge(qkv_copied, n - 1)
                if part == 2 and not (isinstance(h, int) and n < 2):
                    pe.wait_ge(v_ready, n - 1)
                chunk(q, part if part < 2 else 3)
                tile(half(b + part // 2, part % 2), part, 0, P, DT, xhi, xlo).then_inc(chunk_used, 1 if part < 2 else 2)

            def turn_v(h, odd, g):
                pe.wait_ge(qkv_copied, h * 3 + (g + 1))
                b = 2 * ((odd + g) % 2)
                for kt in range(2):
                    ins = pe.transpose(ps[:, b + 1, T + kt * P:T + kt * P + P], qkv_t[:, g, 2, kt * P:kt * P + P], ccol("ident"))
                ins.then_inc(v_turned, 1)

            def scores(h):
                pe.wait_ge(qkv_copied, h * 3 + 3)
                for g in range(N_GROUPS):
                    pe.matmul(ps[:, 4 + g, 0:128], qkv_t[:, g, 0, 0:128], qkv_t[:, g, 1, 0:128], start=True, stop=True)
                    ins = pe.matmul(ps[:, 4 + g, 128:384], qkv_t[:, g, 0, 128:256], qkv_t[:, g, 1, :], start=True, stop=True)
                ins.then_inc(scores_done, 1)

            def turn(h):
                pe.wait_ge(prob_ready, h + 1)
                for g in range(N_GROUPS):
                    for b in range(3):
                        ins = pe.transpose(ps[:, 4 + g, b * P:(b + 1) * P], score[:, g, b * P:(b + 1) * P], ccol("ident"))
                ins.then_inc(turned, 1)

            def mix(h, odd):
                pe.wait_ge(turned_copied, h + 1)
                pe.wait_ge(v_ready, h * 3 + 3)
                pe.wait_ge(head_lo, h + 1)
                for g in range(N_GROUPS):
                    pe.matmul(ps[:, 7, 0:128], v_rows[:, odd, g, 0], prob_t[:, g, 0:128], start=g == 0, stop=g == 2)
                for g in range(N_GROUPS):
                    for kt in range(2):
                        ins = pe.matmul(ps[:, 7, 128:256], v_rows[:, odd, g, kt], prob_t[:, g, 128 + 128 * kt:256 + 128 * kt],
                                        start=g + kt == 0, stop=g + kt == 3)
                ins.then_inc(head_done, 1)

            def attn_head(h, odd, first):
                qkv(h, odd, 0, 0)
                if not first:
                    turn_v(h - 1, 1 - odd, 2)
                    scores(h - 1)
                qkv(h, odd, 0, 1)
                qkv(h, odd, 0, 2)
                qkv(h, odd, 1, 0)
                turn_v(h, odd, 0)
                if not first:
                    turn(h - 1)
                qkv(h, odd, 1, 1)
                qkv(h, odd, 1, 2)
                qkv(h, odd, 2, 0)
                if not first:
                    mix(h - 1, 1 - odd)
                turn_v(h, odd, 1)
                qkv(h, odd, 2, 1)
                qkv(h, odd, 2, 2)
            attn_head(0, 0, True)
            with pe.Fori(0, N_HEADS // 2 - 1) as i:
                attn_head(i * 2 + 1, 1, False)
                attn_head(i * 2 + 2, 0, False)
            attn_head(N_HEADS - 1, 1, False)
            turn_v(N_HEADS - 1, 1, 2)
            scores(N_HEADS - 1)
            turn(N_HEADS - 1)
            mix(N_HEADS - 1, 1)
            pe.wait_ge(head_lo, 1 + N_HEADS)
            for b in range(4):
                n = BLOCK["attn_out"] + b
                q = QUAD["attn_out"] + b // 2
                pe.wait_ge(block_free, n + 1)
                for s2 in range(2):
                    s = 2 * (b % 2) + s2
                    chunk(q, s)
                    for j in range(2):
                        ins = tile(block_ps(n % 2)[:, 2 * s2 + j, :], s, j * P, 256, 8, heads_hi, heads_lo)
                    ins.then_inc(chunk_used, 1)
            norm("mix1", resid)
            mlp("mlp1")
            norm("mlp1", resid)
            norm("attn2", resid)

            for b in range(4):
                n = BLOCK["proj"] + b
                quad_block(QUAD["proj"] + b, n % 2, n + 1, (norm_lo, LO0[NORM["attn2"]]) if b == 0 else None, 3 if b == 3 else 4)
            for hf in range(2):
                pe.wait_ge(block_free, 2 + BLOCK["proj"] + 4)
                for ci in range(4):
                    c = 4 * hf + ci
                    pe.wait_ge(blocks_landed[ci], 32 * hf + 16)
                    if ci >= 2:
                        pe.wait_ge(bu_ready, c - 1)
                    elif hf:
                        pe.wait_ge(y_ready, 1)
                    for st in range(4):
                        for r in range(2):
                            ins = pe.matmul(half(4 * (ci % 2) + st, r), blocks[:, ci, r * 512 + st * P:r * 512 + st * P + P],
                                            proj[:, c, :], start=True, stop=True)
                    ins.then_inc(bu_done, 1)
                for ci in range(4):
                    pe.wait_ge(blocks_landed[ci], 32 * hf + 32)
                    pe.wait_ge(scan_done, 4 * hf + ci + 1)
                    for r in range(2):
                        for st in range(4):
                            ins = pe.matmul(half(ci, r), blocks[:, ci, r * 512 + st * P:r * 512 + st * P + P],
                                            state[:, r, 4 * ci + st, :], start=st == 0, stop=st == 3)
                    ins.then_inc(y_done, 1)
            pe.wait_ge(gelu_lo, 2)
            for b in range(2):
                for s2 in range(2):
                    s = 2 * b + s2
                    chunk(QUAD["glu"], s)
                    for j in range(2):
                        ins = tile(block_ps(b)[:, 2 * s2 + j, :], s, j * P, 256, 8, xhi, xlo)
                    ins.then_inc(chunk_used, 1)
            norm("ssm", proj[:, 0:8, :])
            norm("q", proj[:, 8:12, :])
            norm("kv", proj[:, 12:14, :])

            def rope(src):
                pe.matmul(ps[0:ROPE, 2, 0:T], ccol("sel"), src, start=True, stop=True)
                pe.matmul(ps[0:ROPE, 2, T:2 * T], ccol("rot"), src, start=True, stop=True).then_inc(rope_done, 1)
            rope(proj[:, 14, :])
            pe.wait_ge(norm_lo, LO0[NORM["kv"]] + 1)
            pe.wait_ge(rope_ready, 1)
            with pe.Fori(0, 2) as i:
                for s in range(SLOTS):
                    h = i * 4 + s
                    chunk(i + QUAD["mla"], s)
                    for j in range(2):
                        tile(half(0, j), s, j * ROPE, 192, 4, cq_hi, cq_lo)
                    tile(half(1, 0), s, 768, 256, 2, ckv_hi, ckv_lo)
                    for tt in range(2):
                        o = ps[:, 1, T + tt * HD:T + (tt + 1) * HD]
                        for k in range(2):
                            c, t = slice(768 + k * 256 + P, 768 + k * 256 + 256), slice(tt * P, tt * P + P)
                            pe.matmul(o, ckv_hi[:, k, t], whi[:, s, c], start=k == 0, stop=False)
                            pe.matmul(o, ckv_hi[:, k, t], wlo[:, s, c], start=False, stop=False)
                            ins = pe.matmul(o, ckv_lo[:, k, t], whi[:, s, c], start=False, stop=k == 1)
                    ins.then_inc(chunk_used, 1)
                    pe.wait_ge(m_copied, h + 1)
                    rope(proj[:, 1, :])
                    pe.wait_ge(rope_ready, h + 2)
                    for qt in range(2):
                        o = ps[:, 3, 128 * qt:128 + 256 * qt]
                        t, keys = slice(qt * P, qt * P + P), slice(0, P + P * qt)
                        pe.matmul(o, proj[:, 0, t], proj[:, 2, keys], start=True, stop=False)
                        ins = pe.matmul(o, proj[0:ROPE, 4, t], k_rope[:, keys], start=False, stop=True)
                    ins.then_inc(m_score, 1)
                    pe.wait_ge(m_prob, h + 1)
                    sc = proj[:, 5:7, :].rearrange("p a t -> p (a t)")
                    for b in range(3):
                        ins = pe.transpose(ps[:, 4, b * P:(b + 1) * P], sc[:, b * P:(b + 1) * P], ccol("ident"))
                    ins.then_inc(m_turned, 1)
                    pe.wait_ge(m_pt, h + 1)
                    pt = proj[:, 7:9, :].rearrange("p a t -> p (a t)")
                    pe.matmul(ps[:, 5, 0:128], proj[:, 3, 0:HD], pt[:, 0:128], start=True, stop=True)
                    pe.matmul(ps[:, 5, 128:256], proj[:, 3, 0:HD], pt[:, 128:256], start=True, stop=False)
                    pe.matmul(ps[:, 5, 128:256], proj[:, 3, HD:2 * HD], pt[:, 256:384], start=False, stop=True).then_inc(m_out, 1)
            norm("mla", scratch[:, 0:8, :])
            pe.wait_ge(norm_lo, LO0[NORM["mla"]] + 2)
            for b in range(4):
                n = BLOCK["out2"] + b
                quad_block(QUAD["out2"] + b, n % 2, n + 1)
            norm("ffn2", resid)

            q0, b0, h0, n = QUAD["ffn"], BLOCK["ffn"], HIDDEN["ffn"], FF2 // HID

            def up(g, quad, x_ready=None):
                for i in range(2):
                    quad_block(quad + i, i, g * 2 + (b0 + i + 1), x_ready if i == 0 else None)
            up(0, q0, (norm_lo, LO0[NORM["ffn2"]]))
            with pe.Fori(0, n - 1) as g:
                up(g + 1, g * 3 + (q0 + 2))
                down(g * 3 + (q0 + 4), g * 4 + 4 * h0, g + (h0 + 1))
            down(q0 + 3 * n - 1, 4 * (h0 + n - 1), h0 + n)
            norm("final", resid)


def shape_constants():
    import numpy as np
    t = np.zeros((P, N_CONST), np.float32)

    def put(name, a):
        t[:a.shape[0], CONST[name]:CONST[name] + a.shape[1]] = a
    put("ident", np.eye(P))
    far = 1e37
    lag = np.arange(T)[:, None] - np.arange(T)[None, :]
    for g, (window, dil) in enumerate(((128, 1), (512, 4), (2048, 16))):
        ok = (lag >= 0) & (lag <= window) & (lag % dil == 0)
        d = np.where(ok, lag, far)
        t[:, CONST["dist"] + 384 * g:CONST["dist"] + 384 * g + 128] = d[:P, :P]
        t[:, CONST["dist"] + 384 * g + 128:CONST["dist"] + 384 * g + 384] = d[P:, :]
    c = np.where(lag >= 0, 0.0, -far)
    put("causal", np.concatenate([c[:P, :P], c[P:, :]], axis=1))
    n = N_GROUPS * N_HEADS
    put("slope", np.broadcast_to(-np.exp2(-8.0 * np.arange(1, n + 1) / n) / ATTN_SCALE, (P, n)))
    sel, rot, h = np.zeros((P, ROPE)), np.zeros((P, ROPE)), ROPE // 2
    for i in range(ROPE):
        sel[ROPE + i, i] = 1.0
    for i in range(h):
        rot[ROPE + h + i, i] = -1.0
        rot[ROPE + i, h + i] = 1.0
    put("sel", sel)
    put("rot", rot)
    put("count", np.broadcast_to(np.concatenate([1.0 / np.minimum(np.arange(1, PAD + 1), w) for w in POOL_WINDOWS]), (P, 4 * PAD)))
    f = 10000.0 ** (-np.arange(0, ROPE, 2) / ROPE)
    put("freq", np.concatenate([f, f])[:, None])
    t[:, CONST["ln_eps"]] = LN_EPS
    t[:, CONST["rms_eps"]] = RMS_EPS
    return t


def pack_weights(i):
    import numpy as np

    def columns(w, kts=DT):
        n = CW // kts
        return w.reshape(kts, P, -1, n).transpose(2, 1, 0, 3).reshape(-1, P, CW)

    def rows(w):
        return w.reshape(-1, 4, P, w.shape[1] // 512, 512).transpose(0, 3, 2, 1, 4).reshape(-1, P, CW)

    def mlp(up, down):
        u, d = columns(up).reshape(-1, 4, P, CW), rows(down).reshape(-1, 4, P, CW)
        parts = [u[0]]
        for g in range(len(u) - 1):
            parts += [u[g + 1], d[g]]
        return np.concatenate(parts + [d[-1]])

    def ffn(up, down):
        u, d = columns(up).reshape(2, -1, 4, P, CW), rows(down).reshape(-1, 4, P, CW)
        n = len(d)
        parts = [u[0, 0], u[1, 0]]
        for g in range(n - 1):
            parts += [u[0, g + 1], u[1, g + 1], d[g]]
        return np.concatenate(parts + [d[-1]])
    parts = [columns(i["pool_w_in"][0]).reshape(4, 4, P, CW)[::-1].reshape(-1, P, CW),
             np.concatenate([rows(i["pool_w_group"][0, 3 - g]) for g in range(4)]),
             columns(i["pool_w_out"][0]), mlp(i["mlp_w_up"][0], i["mlp_w_down"][0])]
    qkv = columns(i["attn_w_qkv"][0]).reshape(3, N_GROUPS, N_HEADS, P, CW).transpose(2, 1, 0, 3, 4)
    attn = np.zeros((N_HEADS, N_GROUPS, 4, P, CW), np.float32)
    attn[:, :, 0:3] = qkv
    parts += [attn.reshape(-1, P, CW), columns(i["attn_w_out"][0], 8), mlp(i["mlp_w_up"][1], i["mlp_w_down"][1])]
    w = i["w_in_2"][0]
    parts += [columns(w[:, 0:1792]), columns(w[:, 1728:1856]), np.zeros((1, P, CW), np.float32), columns(i["ssm_w_glu_2"][0], 8)]
    mla = np.zeros((N_HEADS, P, CW), np.float32)
    mla[:, :, 0:768] = i["mla_w_uq_2"][0].reshape(4, P, N_HEADS, 192).transpose(2, 1, 0, 3).reshape(N_HEADS, P, 768)
    mla[:, :, 768:1280] = i["mla_w_ukv_2"][0].reshape(2, P, N_HEADS, 256).transpose(2, 1, 0, 3).reshape(N_HEADS, P, 512)
    parts += [mla, columns(i["w_out_2"][0]), ffn(i["ffn_w_up_2"][0], i["ffn_w_down_2"][0])]
    return np.concatenate(parts)


def pack_ssm(i):
    import numpy as np
    t = np.zeros((2, 2, 4, P, 2, 4, P), np.float32)
    for r, part in enumerate(("re", "im")):
        b, c = i[f"ssm_b_{part}_2"][0], i[f"ssm_c_{part}_2"][0]
        for g in range(64):
            hf, ci, st, h = g // 32, (g // 8) % 4, (g // 2) % 4, g % 2
            ch, state = slice(g % 8 * 16, g % 8 * 16 + 16), slice(64 * h, 64 * h + 64)
            t[hf, 0, ci, ch, r, st, state] = b[g].T
            t[hf, 1, ci, state, r, st, ch] = c[g].T
    return t.reshape(16, P, 1024)


def kernel(**inputs):
    import numpy as np
    import concourse.bacc as bacc
    from concourse.bass_utils import run_bass_kernel_spmd as run

    i = {k: np.asarray(v) for k, v in inputs.items()}
    lam = np.stack([i["ssm_lambda_re_2"].reshape(32, P), i["ssm_lambda_im_2"].reshape(32, P),
                    np.repeat(i["ssm_log_dt_2"].reshape(64), 64).reshape(32, P)])
    arrays = {
        "x_t": i["x"][0].T,
        "weights": pack_weights(i),
        "ssm_blocks": pack_ssm(i),
        "features": np.concatenate([i[n].reshape(-1, P) for n, _ in FEATURES]).T,
        "consts": shape_constants(),
        "ssm_lam": lam.transpose(2, 0, 1),
        "positions": i["positions_2"].reshape(T),
    }
    arrays = {k: np.ascontiguousarray(v) for k, v in arrays.items()}
    nc = bacc.Bacc("TRN2", target_bir_lowering=False, num_devices=1)
    args = [nc.dram_tensor(k, v.shape, mybir.dt.from_np(v.dtype), kind="ExternalInput").ap() for k, v in arrays.items()]
    out = nc.dram_tensor("out", (D, T), F32, kind="ExternalOutput").ap()
    build(nc, *args, out)
    r = run(nc, [arrays], core_ids=[0])
    return np.ascontiguousarray(r.results[0]["out"].T)[None]
```

```python
from contextlib import ExitStack

import concourse.bass as bass
from concourse import mybir

F32 = mybir.dt.float32
F32R = mybir.dt.float32r
I32 = mybir.dt.int32
ALU = mybir.AluOpType
ACT = mybir.ActivationFunctionType
AX = mybir.AxisListType

P = 128
T = 256
D = 2048
DT = D // P
FF = 4 * D
FF2 = 5632
HID = 512
SLOTS = 4
CW = 2048
N_HEADS = 8
N_GROUPS = 3
HD = 128
ROPE = 64
ALPHA = 4.0 ** 0.25
LN_EPS = 1e-5
RMS_EPS = 1e-6
ATTN_SCALE = HD ** -0.5
MLA_SCALE = (HD + ROPE) ** -0.5
POOL_WINDOWS = (2, 4, 8, 16)
PAD = 16
SCAN = 16
SCAN_DVE = 12

STAGES = (("pool_in", 4), ("pool_group", 1), ("pool_out", 4), ("mlp0", 32), ("attn", 24), ("attn_out", 2),
          ("mlp1", 32), ("proj", 4), ("glu", 1), ("mla", 2), ("out2", 4), ("ffn", 33))
QUAD, N_QUADS = {}, 0
for _name, _n in STAGES:
    QUAD[_name] = N_QUADS
    N_QUADS += _n

BLOCK, _b = {}, 0
for _name, _n in (("pool_in", 4), ("pool_group", 4), ("pool_out", 4), ("mlp0", 16), ("attn_out", 4), ("mlp1", 16),
                  ("proj", 4), ("glu", 2), ("out2", 4), ("ffn", 22)):
    BLOCK[_name] = _b
    _b += _n
HIDDEN = {"mlp0": 0, "mlp1": FF // HID, "ffn": 2 * FF // HID}

FEATURES = (("pool_scale", DT), ("ln_mix_g", 2 * DT), ("ln_mix_b", 2 * DT), ("ln_mlp_g", 2 * DT), ("ln_mlp_b", 2 * DT),
            ("attn_norm_w_2", DT), ("ffn_norm_w_2", DT), ("final_norm_w_2", DT), ("ssm_d_2", 8), ("ssm_b_glu_2", 8),
            ("mla_q_norm_w_2", 4), ("mla_kv_norm_w_2", 2), ("ssm_out_norm_w_2", 8), ("mla_out_norm_w_2", 8),
            ("ffn_conv_w_2", 3 * 2 * FF2 // P), ("ffn_conv_b_2", 2 * FF2 // P))
FEAT, N_FEAT = {}, 0
for _name, _n in FEATURES:
    FEAT[_name] = N_FEAT
    N_FEAT += _n

CONSTS = (("ident", P), ("dist", 3 * 384), ("causal", 384), ("slope", 24), ("sel", ROPE), ("rot", ROPE),
          ("count", 4 * PAD), ("freq", 1), ("ln_eps", 1), ("rms_eps", 1))
CONST, N_CONST = {}, 0
for _name, _n in CONSTS:
    CONST[_name] = N_CONST
    N_CONST += _n

NORMS = (("mix0", 16, True), ("mlp0", 16, True), ("mix1", 16, True), ("mlp1", 16, True), ("attn2", 16, False),
         ("q", 4, False), ("kv", 2, False), ("ssm", 8, False), ("mla", 8, False), ("ffn2", 16, False), ("final", 16, False))
NORM = {n: i for i, (n, _, _) in enumerate(NORMS)}
NORM_TILES = {n: t for n, t, _ in NORMS}
PIECES = [max(1, t // 4) for _, t, _ in NORMS]
PIECE0 = [sum(PIECES[:i]) for i in range(len(PIECES))]
LO0 = [sum(p for (n, _, _), p in zip(NORMS[:i], PIECES) if n not in ("mlp1", "final")) for i in range(len(NORMS))]
ATTN_WIDTHS = (CW, CW, CW, 16)


class Steps:

    def __init__(self, eng, sem):
        self.eng, self.sem, self.n, self.it, self.per = eng, sem, 0, None, 0

    def __call__(self, ins):
        ins.then_inc(self.sem, 1)
        self.n += 1

    def settle(self):
        if self.it is None:
            self.eng.wait_ge(self.sem, self.n)
        else:
            self.eng.wait_ge(self.sem, self.it * self.per + self.n)

    def enter(self, it, per):
        self.it, self.per, self.start = it, per, self.n

    def leave(self, times):
        assert self.n - self.start == self.per, (self.n - self.start, self.per)
        self.it = None
        self.n = self.start + self.per * times


def build(nc, x_t, weights, ssm_blocks, features, consts, ssm_lam, positions, out):
    with ExitStack() as ctx:
        def sem(name):
            return ctx.enter_context(nc.semaphore(name))

        def sb(name, shape, dt=F32, scope=ctx):
            return scope.enter_context(nc.sbuf_tensor(name, shape, dt))

        raw = sb("raw", [P, SLOTS, CW])
        whi = sb("whi", [P, SLOTS, CW], F32R)
        wlo = sb("wlo", [P, SLOTS, CW], F32R)
        resid = sb("resid", [P, DT, T])
        feat = sb("feat", [P, N_FEAT])
        const = sb("const", [P, N_CONST])
        ones = sb("ones", [P, P])
        ones_mean = sb("ones_mean", [P, P])
        std = sb("std", [P, T])
        rstd = sb("rstd", [P, T])
        lam = sb("lam", [P, 3, 32])
        par = sb("par", [P, 13, 32])
        pow_re = sb("pow_re", [P, 32, SCAN])
        pow_im = sb("pow_im", [P, 32, SCAN])
        rope_cos = sb("rope_cos", [ROPE, T])
        rope_sin = sb("rope_sin", [ROPE, T])
        pos_i = rope_cos[:].bitcast(I32)

        with ExitStack() as s:
            xhi = sb("xhi", [P, DT, T], F32R, s)
            xlo = sb("xlo", [P, DT, T], F32R, s)
        state = sb("state", [P, 2, 16, T])

        with ExitStack() as s:
            pool_hi = sb("pool_hi", [P, 2, 4, T], F32R, s)
            pool_lo = sb("pool_lo", [P, 2, 4, T], F32R, s)
        with ExitStack() as s:
            heads_hi = sb("heads_hi", [P, N_HEADS, T], F32R, s)
            heads_lo = sb("heads_lo", [P, N_HEADS, T], F32R, s)
        with ExitStack() as s:
            blocks = sb("blocks", [P, 4, 1024], F32, s)
        scratch = sb("scratch", [P, DT, T])

        with ExitStack() as s:
            u_pad = sb("u_pad", [P, 4, 4, PAD + T], F32, s)
            win_a = sb("win_a", [P, 4, PAD + T], F32, s)
            win_b = sb("win_b", [P, 4, PAD + T], F32, s)
        with ExitStack() as s:
            hid = sb("hid", [P, 4, T], F32, s)
            hid_hi = sb("hid_hi", [P, 4, T], F32R, s)
            hid_lo = sb("hid_lo", [P, 4, T], F32R, s)
            with ExitStack() as s2:
                last_hi = sb("last_hi", [P, 4, T], F32R, s2)
                last_lo = sb("last_lo", [P, 4, T], F32R, s2)
            conv = sb("conv", [P, 8, T], F32, s)
            gate_sig = sb("gate_sig", [P, 4, T], F32, s)
        with ExitStack() as s:
            qkv_t = sb("qkv_t", [P, N_GROUPS, 3, T], F32, s)
            v_rows = sb("v_rows", [P, 2, N_GROUPS, 2, HD], F32, s)
            score = sb("score", [P, N_GROUPS, 384], F32, s)
            prob_t = sb("prob_t", [P, N_GROUPS, 384], F32, s)
            row_max = sb("row_max", [P, 2], F32, s)
            row_den = sb("row_den", [P, 2], F32, s)
        with ExitStack() as s:
            proj = sb("proj", [P, 15, T], F32, s)
            with ExitStack() as s2:
                scan_a = sb("scan_a", [P, 2, 16, 16], F32, s2)
                scan_b = sb("scan_b", [P, 2, 16, 16], F32, s2)
                bu_tmp = sb("bu_tmp", [P, 4, 2, T], F32, s2)
            with ExitStack() as s2:
                cq_hi = sb("cq_hi", [P, 4, T], F32R, s2)
                cq_lo = sb("cq_lo", [P, 4, T], F32R, s2)
                ckv_hi = sb("ckv_hi", [P, 2, T], F32R, s2)
                ckv_lo = sb("ckv_lo", [P, 2, T], F32R, s2)
                m_max = sb("m_max", [P, 2], F32, s2)
                m_den = sb("m_den", [P, 2], F32, s2)

        ps = ctx.enter_context(nc.psum_tensor("ps", [P, 8, 512], F32))

        def half(bank, h):
            return ps[:, bank, h * T:(h + 1) * T]

        def block_ps(b):
            return ps[:, 2 * b:2 * b + 2, :].rearrange("p b (h t) -> p (b h) t", t=T)

        def wait_used(eng, q, s=SLOTS - 1):
            eng.wait_ge(chunk_used, q * SLOTS + (SLOTS + s + 1))

        def up_quad(q0, g, per):
            return q0 if isinstance(g, int) and g == 0 else g * per + (q0 - 1)

        def gelu_tmp(hf):
            return bu_tmp[:].rearrange("p a b t -> p (a b) t")[:, 4 * hf:4 * hf + 4, :]

        def m_buf(slot, a, b):
            return state[:, slot % 2, 8 + a:8 + b, :].rearrange("p a t -> p (a t)")
        hop_re = [pow_re[:, :, SCAN - 1], par[:, 0, :], par[:, 1, :], par[:, 2, :]]
        hop_im = [pow_im[:, :, SCAN - 1], par[:, 3, :], par[:, 6, :], par[:, 10, :]]
        hop_nim = [lam[:, 0, :], lam[:, 1, :], lam[:, 2, :], par[:, 12, :]]
        scan_tmp = bu_tmp[:].rearrange("p a b t -> p (a b t)").rearrange("p (k n) -> p k n", k=2)
        k_rope, rope_a = state[0:ROPE, 0, 15, :], state[0:ROPE, 1, 15, :]
        m_prob_buf = state[:, 0, 13:15, :].rearrange("p a t -> p (a t)")
        m_turned_buf = state[:, 1, 13:15, :].rearrange("p a t -> p (a t)")

        def fcol(name, i):
            return feat[:, bass.ds(FEAT[name] + i, 1)]

        def ccol(name, a=0, n=None, rows=P):
            n = dict(CONSTS)[name] - a if n is None else n
            return const[0:rows, CONST[name] + a:CONST[name] + a + n]

        landed = [sem(f"landed{i}") for i in range(SLOTS)]
        hi_ready, lo_ready, chunk_used = sem("hi_ready"), sem("lo_ready"), sem("chunk_used")
        x_landed = [sem(f"x_landed{i}") for i in range(4)]
        table_landed, lam_landed, out_landed = sem("table_landed"), sem("lam_landed"), sem("out_landed")
        ones_ready = sem("ones_ready")
        x_hi_ready, x_lo_ready, resid_ready = sem("x_hi_ready"), sem("x_lo_ready"), sem("resid_ready")
        block_free = sem("block_free")
        down_free = sem("down_free")
        hidden_ready, hidden_hi, hidden_lo = sem("hidden_ready"), sem("hidden_hi"), sem("hidden_lo")
        conv_start, conv_done, sig_ready = sem("conv_start"), sem("conv_done"), sem("sig_ready")
        pad_ready, summed, pooled, pooled_hi, pooled_lo = (sem(n) for n in ("pad_ready", "summed", "pooled", "pooled_hi", "pooled_lo"))
        y_scaled, y_hi, y_lo = sem("y_scaled"), sem("y_hi"), sem("y_lo")
        norm_mean, norm_xc, norm_sq, norm_var, norm_std, norm_scaled, norm_y, norm_hi, norm_lo = (
            sem(n) for n in ("norm_mean", "norm_xc", "norm_sq", "norm_var", "norm_std", "norm_scaled", "norm_y", "norm_hi", "norm_lo"))
        qkv_copied, v_turned, v_ready = sem("qkv_copied"), sem("v_turned"), sem("v_ready")
        scores_done, shift_ready, exp_done, prob_ready = sem("scores_done"), sem("shift_ready"), sem("exp_done"), sem("prob_ready")
        turned, turned_copied, head_done, head_hi, head_lo = (sem(n) for n in ("turned", "turned_copied", "head_done", "head_hi", "head_lo"))
        blocks_landed = [sem(f"blocks_landed{i}") for i in range(4)]
        angles_ready, trig_ready, table_ready = sem("angles_ready"), sem("trig_ready"), sem("table_ready")
        proj_copied, bu_done, bu_part, bu_ready, scan_done, scan_rest_done, y_done, y_ready = (
            sem(n) for n in ("proj_copied", "bu_done", "bu_part", "bu_ready", "scan_done", "scan_rest_done", "y_done", "y_ready"))
        gelu_sq, gelu_arg, gelu_sig, gelu_ready, gelu_hi, gelu_lo, glu_sig = (
            sem(n) for n in ("gelu_sq", "gelu_arg", "gelu_sig", "gelu_ready", "gelu_hi", "gelu_lo", "glu_sig"))
        m_q, m_q_copied, m_kv_copied, rope_done, rope_ready, m_score, m_shift, m_exp, m_prob, m_turned, m_pt, m_out, m_out_copied = (
            sem(n) for n in ("m_q", "m_q_copied", "m_kv_copied", "rope_done", "rope_ready", "m_score", "m_shift", "m_exp", "m_prob",
                             "m_turned", "m_pt", "m_out", "m_out_copied"))
        act_steps, dve_steps, pool_steps = sem("act_steps"), sem("dve_steps"), sem("pool_steps")

        def after_blocks(stage):
            return [(block_free, 2 + BLOCK[stage] + p + 1) for p in range(4)]

        def after_down(stage, groups):
            return [(down_free, 2 + 4 * (HIDDEN[stage] + groups - 1) + p + 1) for p in range(4)]
        source = {"mix0": after_blocks("pool_out"), "mlp0": after_down("mlp0", FF // HID),
                  "mix1": after_blocks("attn_out"), "mlp1": after_down("mlp1", FF // HID),
                  "attn2": [(norm_y, PIECE0[NORM["mlp1"]] + p + 1) for p in range(4)],
                  "q": [(gelu_ready, 2)], "kv": [(gelu_ready, 2)], "ssm": after_blocks("glu")[0:2],
                  "mla": [(m_out_copied, 4 * p + 4) for p in range(2)],
                  "ffn2": after_blocks("out2"), "final": after_down("ffn", FF2 // HID)}

        def norm_tmp(name):
            if name == "mla":
                return bu_tmp[:].rearrange("p a b t -> p (a b) t")
            return scratch[:, DT - NORM_TILES[name]:DT, :]

        def norm_ps(name):
            b = 2 if name in ("mlp0", "mlp1", "final") else 4 if name == "mla" else 6
            return half(b, 0), half(b + 1, 0)

        block = ctx.enter_context(nc.Block())

        def scan_tiles(eng, step, hf, first, n, at_once, unroll, tmp_a, tmp_b, done):
            own = slice(first, first + n)
            cols = slice(16 * hf + first, 16 * hf + first + n)
            sv = state[:, :, own, :].rearrange("p r s (b j) -> p r s b j", j=SCAN)
            a, b = scan_a[:, :, own, :], scan_b[:, :, own, :]

            def along(col, m):
                return col[:, cols].unsqueeze(2).to_broadcast([P, n, m])

            def both(col, m):
                return col[:, cols].unsqueeze(1).unsqueeze(3).to_broadcast([P, 2, n, m])

            def hop(prev, cur, re, im, nim, m):
                step(eng.tensor_tensor(a[:, :, :, 0:m], prev, both(re, m), ALU.mult))
                step(eng.tensor_tensor(b[:, 0, :, 0:m], prev[:, 1], along(nim, m), ALU.mult))
                step(eng.tensor_tensor(b[:, 1, :, 0:m], prev[:, 0], along(im, m), ALU.mult))
                step.settle()
                step(eng.tensor_tensor(a[:, :, :, 0:m], a[:, :, :, 0:m], b[:, :, :, 0:m], ALU.add))
                step.settle()
                step(eng.tensor_tensor(cur, cur, a[:, :, :, 0:m], ALU.add))
                step.settle()
            with eng.Fori(0, (SCAN - 1) // unroll) as j:
                step.enter(j, 5 * unroll)
                for k in range(unroll):
                    token = j if unroll == 1 else j * unroll + k
                    hop(sv[:, :, :, :, bass.ds(token, 1)].rearrange("p r s b a -> p r s (b a)"),
                        sv[:, :, :, :, bass.ds(token + 1, 1)].rearrange("p r s b a -> p r s (b a)"),
                        par[:, 4, :], par[:, 5, :], par[:, 11, :], SCAN)
                step.leave((SCAN - 1) // unroll)
            ends = sv[:, :, :, :, SCAN - 1]
            for level in range(4):
                d = 1 << level
                hop(ends[:, :, :, 0:SCAN - d], ends[:, :, :, d:SCAN], hop_re[level], hop_im[level], hop_nim[level], SCAN - d)
            m = SCAN - 1
            for s0 in range(0, n, at_once):
                ss, tt = slice(s0, s0 + at_once), slice(16 * hf + first + s0, 16 * hf + first + s0 + at_once)
                shape = [P, at_once, m, m]
                fa, fb = (t[:, 0:at_once * m * m].rearrange("p (s b j) -> p s b j", b=m, j=m) for t in (tmp_a, tmp_b))
                for r, (pa, pb, o) in enumerate(((pow_re, pow_im, ALU.subtract), (pow_im, pow_re, ALU.add))):
                    tgt = sv[:, r, ss, 1:SCAN, 0:m]
                    step(eng.tensor_tensor(fa, pa[:, tt, 0:m].unsqueeze(2).to_broadcast(shape),
                                           ends[:, 0, ss, 0:m].unsqueeze(3).to_broadcast(shape), ALU.mult))
                    step(eng.tensor_tensor(fb, pb[:, tt, 0:m].unsqueeze(2).to_broadcast(shape),
                                           ends[:, 1, ss, 0:m].unsqueeze(3).to_broadcast(shape), ALU.mult))
                    step.settle()
                    step(eng.tensor_tensor(tgt, tgt, fa, ALU.add))
                    step.settle()
                    step(eng.tensor_tensor(tgt, tgt, fb, o))
                    step.settle()
                eng.sem_inc(done, 1)

        @block.sync
        def _(sp):
            def load(q, s, width=CW):
                sp.wait_ge(lo_ready, q * SLOTS + (s + 1))
                sp.dma_start(raw[:, s, 0:width],
                             weights[bass.ds(q * SLOTS + s, 1), :, 0:width].rearrange("a p c -> p (a c)")).then_inc(landed[s], 16)

            xv = x_t.rearrange("(n p) t -> p n t", p=P)
            for p in range(4):
                sp.dma_start(resid[:, 4 * p:4 * p + 4, :], xv[:, 4 * p:4 * p + 4, :]).then_inc(x_landed[p], 16)
            with sp.Fori(0, QUAD["attn"]) as q:
                for s in range(SLOTS):
                    load(q, s)
            with sp.Fori(QUAD["attn"], QUAD["attn_out"]) as q:
                for s in range(SLOTS):
                    load(q, s, CW if s < 3 else 16)
            with sp.Fori(QUAD["attn_out"], N_QUADS) as q:
                for s in range(SLOTS):
                    load(q, s)
            for p in range(4):
                sp.wait_ge(norm_y, PIECE0[NORM["final"]] + p + 1)
                sp.dma_start(out.rearrange("(n p) t -> p n t", p=P)[:, 4 * p:4 * p + 4, :],
                             scratch[:, 4 * p:4 * p + 4, :]).then_inc(out_landed, 16)
            sp.wait_ge(out_landed, 64)

        @block.scalar
        def _(act):
            step = Steps(act, act_steps)

            def hi1(q, s, width=CW):
                act.wait_ge(landed[s], q * 16 + 16)
                act.wait_ge(chunk_used, q * SLOTS + (s + 1))
                act.activation(whi[:, s, 0:width], raw[:, s, 0:width], ACT.Copy).then_inc(hi_ready, 1)

            def hi4(q, widths=(CW,) * 4):
                for s in range(SLOTS):
                    hi1(q, s, widths[s])

            def norm_square(name, src, p):
                k = NORM[name]
                mean, t0, w = NORMS[k][2], PIECE0[k], min(4, NORMS[k][1])
                if mean:
                    act.wait_ge(norm_xc, t0 + p + 1)
                else:
                    act.wait_ge(*source[name][p])
                act.activation(norm_tmp(name)[:, p * w:p * w + w, :], src[:, p * w:p * w + w, :],
                               ACT.Square).then_inc(norm_sq, 1)

            def norm_squares(name, src):
                k = NORM[name]
                if LO0[k] and name != "mla":
                    act.wait_ge(norm_lo, LO0[k])
                for p in range(PIECES[k]):
                    norm_square(name, src, p)

            def norm_finish(name, src, dst_hi=None, scale_resid=False, bias=None, then=None):
                k = NORM[name]
                n, mean, t0 = NORMS[k][1], NORMS[k][2], PIECE0[k]
                w = min(4, n)
                if LO0[k]:
                    act.wait_ge(norm_lo, LO0[k])
                act.wait_ge(norm_var, k + 1)
                act.activation(std[:], norm_ps(name)[0], ACT.Sqrt, scale=1.0 / (n * P),
                               bias=ccol("ln_eps" if mean else "rms_eps")).then_inc(norm_std, 1)
                y = src if mean else norm_tmp(name)
                for p in range(PIECES[k]):
                    if mean:
                        act.wait_ge(norm_scaled, t0 + p + 1)
                        for i in range(p * w, p * w + w):
                            ins = act.activation(y[:, i, :], y[:, i, :], ACT.Identity, bias=fcol(bias[0], bias[1] + i))
                        ins.then_inc(norm_y, 1)
                    if then is not None:
                        norm_square(then, src, p)
                    if dst_hi is not None:
                        act.wait_ge(norm_y, t0 + p + 1)
                        act.activation(dst_hi[:, p * w:p * w + w, :], y[:, p * w:p * w + w, :], ACT.Copy).then_inc(norm_hi, 1)
                if scale_resid:
                    for p in range(PIECES[k]):
                        act.wait_ge(norm_lo, LO0[k] + p + 1)
                        act.mul(resid[:, 4 * p:4 * p + 4, :], resid[:, 4 * p:4 * p + 4, :], ALPHA).then_inc(resid_ready, 1)

            def norm(name, src, *args, **named):
                norm_squares(name, src)
                norm_finish(name, src, *args, **named)

            def mlp(name, next_quad, next_widths=(CW,) * 4):
                q0, b0, h0 = QUAD[name], BLOCK[name], HIDDEN[name]
                n = FF // HID

                def activate(g):
                    wait_used(act, up_quad(q0, g, 2))
                    if not (isinstance(g, int) and g + h0 == 0):
                        act.wait_ge(hidden_lo, g + h0)
                    act.activation(hid[:], block_ps(0), ACT.Relu).then_inc(block_free, 1)
                    act.wait_ge(block_free, g + (b0 + 3))
                    act.activation(hid[:], hid[:], ACT.Square).then_inc(hidden_ready, 1)

                def split(g, last=False):
                    act.wait_ge(hidden_ready, g + (h0 + 1))
                    if not last and not (isinstance(g, int) and g == 0):
                        wait_used(act, g * 2 + q0)
                    act.activation(last_hi[:] if last else hid_hi[:], hid[:], ACT.Copy).then_inc(hidden_hi, 1)

                hi4(q0 + 1)
                activate(0)
                split(0)
                with act.Fori(0, n - 2) as g:
                    hi4(g * 2 + (q0 + 2))
                    activate(g + 1)
                    hi4(g * 2 + (q0 + 3))
                    split(g + 1)
                hi4(q0 + 2 * n - 2)
                activate(n - 1)
                split(n - 1, True)
                hi4(q0 + 2 * n - 1)
                hi4(next_quad, next_widths)

            act.dma_start(lam[:], ssm_lam).then_inc(lam_landed, 16)
            act.dma_start(pos_i, positions.partition_broadcast(ROPE)).then_inc(lam_landed, 16)
            act.wait_ge(lam_landed, 32)
            act.activation(par[:, 0, :], lam[:, 2, :], ACT.Exp).then_inc(trig_ready, 1)
            act.wait_ge(angles_ready, 1)
            act.activation(par[:, 1, :], par[:, 1, :], ACT.Exp).then_inc(trig_ready, 1)
            for p in range(4):
                act.wait_ge(x_landed[p], 16)
                act.activation(xhi[:, 4 * p:4 * p + 4, :], resid[:, 4 * p:4 * p + 4, :], ACT.Copy).then_inc(x_hi_ready, 1)
            act.dma_start(const[:], consts).then_inc(table_landed, 16)
            act.dma_start(feat[:], features).then_inc(table_landed, 16)
            hi4(0)
            act.wait_ge(angles_ready, 3)
            act.activation(par[:, 2, :], par[:, 2, :], ACT.Sin)
            act.activation(par[:, 3, :], par[:, 3, :], ACT.Sin).then_inc(trig_ready, 1)
            for p in range(4):
                act.wait_ge(x_lo_ready, p + 1)
                act.mul(resid[:, 4 * p:4 * p + 4, :], resid[:, 4 * p:4 * p + 4, :], ALPHA).then_inc(resid_ready, 1)

            act.wait_ge(pad_ready, 1)

            def copy_u(b):
                wait_used(act, b)
                act.activation(u_pad[:, bass.ds(b, 1), :, PAD:PAD + T].rearrange("p a n t -> p (a n) t"),
                               block_ps(b % 2), ACT.Copy).then_inc(block_free, 1)

            def pooled_high(g):
                act.wait_ge(pooled, g + 1)
                if g >= 2:
                    wait_used(act, QUAD["pool_group"], g - 2)
                act.activation(pool_hi[:, g % 2], win_a[:, :, PAD:PAD + T] if (4 - g) % 2 else win_b[:, :, PAD:PAD + T],
                               ACT.Copy).then_inc(pooled_hi, 1)

            def mixed_high(g):
                grp = 3 - g
                act.wait_ge(y_scaled, g + 1)
                act.activation(xhi[:, 4 * grp:4 * grp + 4, :], u_pad[:, g, :, PAD:PAD + T], ACT.Copy).then_inc(y_hi, 1)
                hi1(QUAD["pool_out"], g)
            hi4(1)
            copy_u(0)
            hi4(2)
            copy_u(1)
            pooled_high(0)
            act.wait_ge(angles_ready, 5)
            act.activation(rope_sin[:], rope_sin[:], ACT.Sin)
            act.activation(rope_cos[:], rope_cos[:], ACT.Sin).then_inc(trig_ready, 1)
            hi4(3)
            copy_u(2)
            pooled_high(1)
            hi4(QUAD["pool_group"])
            copy_u(3)
            mixed_high(0)
            pooled_high(2)
            mixed_high(1)
            pooled_high(3)
            mixed_high(2)
            mixed_high(3)
            for b in range(1, 4):
                hi4(QUAD["pool_out"] + b)
            hi4(QUAD["mlp0"])
            act.wait_ge(table_landed, 32)
            norm("mix0", resid, xhi, True, ("ln_mix_b", 0))
            mlp("mlp0", QUAD["attn"], ATTN_WIDTHS)
            norm("mlp0", resid, xhi, True, ("ln_mlp_b", 0))

            def copy_qkv(h, odd, g):
                wait_used(act, h * 3 + (g + QUAD["attn"]))
                b = 2 * ((odd + g) % 2)
                act.activation(qkv_t[:, g].rearrange("p a t -> p (a t)"),
                               ps[:, b:b + 2, :].rearrange("p b c -> p (b c)")[:, 0:3 * T], ACT.Copy).then_inc(qkv_copied, 1)

            def copy_v(h, odd, g):
                act.wait_ge(v_turned, h * 3 + (g + 1))
                act.activation(v_rows[:, odd, g].rearrange("p a t -> p (a t)"), half(2 * ((odd + g) % 2) + 1, 1),
                               ACT.Copy).then_inc(v_ready, 1)

            def copy_turned(h):
                act.wait_ge(turned, h + 1)
                act.activation(prob_t[:], ps[:, 4:7, 0:384], ACT.Copy).then_inc(turned_copied, 1)

            def copy_head(h):
                act.wait_ge(head_done, h + 1)
                act.activation(heads_hi[:, bass.ds(h, 1), :].rearrange("p a t -> p (a t)"), half(7, 0), ACT.Copy).then_inc(head_hi, 1)

            def exps(h):
                act.wait_ge(shift_ready, h + 1)
                act.activation(score[:, :, 0:128], score[:, :, 0:128], ACT.Exp, bias=row_max[:, 0:1], scale=ATTN_SCALE,
                               accum_out=row_den[:, 0:1])
                act.activation(score[:, :, 128:384], score[:, :, 128:384], ACT.Exp, bias=row_max[:, 1:2], scale=ATTN_SCALE,
                               accum_out=row_den[:, 1:2]).then_inc(exp_done, 1)

            def attn_head(h, odd, first, last):
                q = h * 3 + QUAD["attn"]
                hi1(q + 1, 0)
                if not first:
                    copy_v(h - 1, 1 - odd, 2)
                hi1(q + 1, 1)
                if not first:
                    exps(h - 1)
                copy_qkv(h, odd, 0)
                hi1(q + 1, 2)
                hi1(q + 1, 3, ATTN_WIDTHS[3])
                hi1(q + 2, 0)
                copy_v(h, odd, 0)
                if not first:
                    copy_turned(h - 1)
                hi1(q + 2, 1)
                copy_qkv(h, odd, 1)
                hi1(q + 2, 2)
                hi1(q + 2, 3, ATTN_WIDTHS[3])
                hi1(q + 3, 0)
                if not first:
                    copy_head(h - 1)
                copy_v(h, odd, 1)
                hi1(q + 3, 1)
                copy_qkv(h, odd, 2)
                hi1(q + 3, 2)
                hi1(q + 3, 3, CW if last else ATTN_WIDTHS[3])
            attn_head(0, 0, True, False)
            with act.Fori(0, N_HEADS // 2 - 1) as i:
                attn_head(i * 2 + 1, 1, False, False)
                attn_head(i * 2 + 2, 0, False, False)
            attn_head(N_HEADS - 1, 1, False, True)
            copy_v(N_HEADS - 1, 1, 2)
            exps(N_HEADS - 1)
            copy_turned(N_HEADS - 1)
            copy_head(N_HEADS - 1)
            hi4(QUAD["attn_out"] + 1)
            hi4(QUAD["mlp1"])
            norm("mix1", resid, xhi, True, ("ln_mix_b", DT))
            mlp("mlp1", QUAD["proj"])
            norm("mlp1", resid, bias=("ln_mlp_b", DT), then="attn2")
            norm_finish("attn2", resid, xhi)

            hi4(QUAD["proj"] + 1)
            for b in range(4):
                if b:
                    hi4(QUAD["proj"] + b + 1)
                wait_used(act, QUAD["proj"] + b)
                n = min(4, 15 - 4 * b)
                act.activation(proj[:, 4 * b:4 * b + n, :], block_ps(b % 2)[:, 0:n, :], ACT.Copy).then_inc(block_free, 1)

            for hf in range(2):
                for ci in range(4):
                    c = 4 * hf + ci
                    act.wait_ge(bu_done, c + 1)
                    if c == 0:
                        act.wait_ge(table_ready, 1)
                    if c >= 1:
                        act.wait_ge(bu_ready, c)
                    for st in range(4):
                        tile = 4 * c + st
                        src = ps[:, 4 * ((ci + hf) % 2) + st, :].rearrange("p (r t) -> p r t", r=2)
                        act.activation(bu_tmp[:, st, 0, :], src[:, 1, :], ACT.Copy, scale=par[:, 9, tile:tile + 1])
                        act.activation(bu_tmp[:, st, 1, :], src[:, 0, :], ACT.Copy, scale=par[:, 8, tile:tile + 1]).then_inc(bu_part, 1)
            act.wait_ge(y_ready, 2)
            for hf in range(2):
                act.activation(gelu_tmp(hf), proj[:, 4 * hf:4 * hf + 4, :], ACT.Square).then_inc(gelu_sq, 1)
            for hf in range(2):
                act.wait_ge(gelu_arg, hf + 1)
                act.activation(gelu_tmp(hf), gelu_tmp(hf), ACT.Sigmoid).then_inc(gelu_sig, 1)
            for hf in range(2):
                act.wait_ge(gelu_ready, hf + 1)
                act.activation(xhi[:, 4 * hf:4 * hf + 4, :], proj[:, 4 * hf:4 * hf + 4, :], ACT.Copy).then_inc(gelu_hi, 1)
            norm("q", proj[:, 8:12, :], cq_hi)
            norm("kv", proj[:, 12:14, :], ckv_hi)

            def glu_gate(b):
                wait_used(act, QUAD["glu"], 2 * b + 1)
                for nt in range(4):
                    ins = act.activation(scratch[:, 4 * b + nt, :], block_ps(b)[:, nt, :], ACT.Sigmoid,
                                         bias=fcol("ssm_b_glu_2", 4 * b + nt))
                ins.then_inc(glu_sig, 1)
            glu_gate(0)
            hi1(QUAD["mla"], 0)
            hi1(QUAD["mla"], 1)
            glu_gate(1)
            hi1(QUAD["mla"], 2)
            norm_squares("ssm", proj[:, 0:8, :])
            hi1(QUAD["mla"], 3)

            def copy_q(h, s):
                act.wait_ge(m_q, h + 1)
                act.activation(m_buf(s, 0, 2), ps[:, 0, :], ACT.Copy).then_inc(m_q_copied, 1)

            def copy_kv(h, q, s):
                wait_used(act, q, s)
                act.activation(m_buf(s, 2, 4), ps[:, 1, :], ACT.Copy).then_inc(m_kv_copied, 1)

            def mla_head(h, q, s):
                if s < SLOTS - 1:
                    copy_q(h + 1, s + 1)
                hi1(q + 1, s)
                act.wait_ge(m_shift, h + 1)
                act.activation(m_prob_buf[:, 0:128], m_prob_buf[:, 0:128], ACT.Exp, bias=m_max[:, 0:1], scale=MLA_SCALE,
                               accum_out=m_den[:, 0:1])
                act.activation(m_prob_buf[:, 128:384], m_prob_buf[:, 128:384], ACT.Exp, bias=m_max[:, 1:2], scale=MLA_SCALE,
                               accum_out=m_den[:, 1:2]).then_inc(m_exp, 1)
                if s < SLOTS - 1:
                    copy_kv(h + 1, q, s + 1)
                act.wait_ge(m_turned, h + 1)
                act.activation(m_turned_buf[:, 0:384], ps[:, 4, 0:384], ACT.Copy).then_inc(m_pt, 1)
                act.wait_ge(m_out, h + 1)
                act.activation(scratch[:, bass.ds(h, 1), :].rearrange("p a t -> p (a t)"), half(5, 0), ACT.Copy).then_inc(m_out_copied, 1)
            with act.Fori(0, 2) as i:
                copy_q(i * 4, 0)
                copy_kv(i * 4, i + QUAD["mla"], 0)
                for s in range(SLOTS):
                    mla_head(i * 4 + s, i + QUAD["mla"], s)
            norm_squares("mla", scratch[:, 0:8, :])
            norm_finish("ssm", proj[:, 0:8, :], xhi)
            norm_finish("mla", scratch[:, 0:8, :], xhi[:, 8:16, :])
            for b in range(1, 4):
                hi4(QUAD["out2"] + b)
            hi4(QUAD["ffn"])
            norm("ffn2", resid, xhi)

            q0, b0, h0, n = QUAD["ffn"], BLOCK["ffn"], HIDDEN["ffn"], FF2 // HID

            def conv_first(g, half_):
                wait_used(act, up_quad(q0, g, 3) + half_)
                if not (isinstance(g, int) and g == 0):
                    act.wait_ge(hidden_ready, g + h0)
                for nt in range(4):
                    i = g * 4 + (half_ * (FF2 // P) + nt)
                    ins = act.activation(conv[:, 4 * half_ + nt, :], block_ps(half_)[:, nt, :], ACT.Identity,
                                         scale=fcol("ffn_conv_w_2", i + 2 * (2 * FF2 // P)), bias=fcol("ffn_conv_b_2", i))
                ins.then_inc(conv_start, 1)

            def gate(g):
                act.wait_ge(conv_done, g * 2 + 1)
                act.activation(gate_sig[:], conv[:, 0:4, :], ACT.Sigmoid).then_inc(sig_ready, 1)

            def ffn_split(g):
                act.wait_ge(hidden_ready, g + (h0 + 1))
                if not (isinstance(g, int) and g == 0):
                    wait_used(act, g * 3 + (q0 + 1))
                act.activation(hid_hi[:], hid[:], ACT.Copy).then_inc(hidden_hi, 1)

            def group(g, q):
                conv_first(g, 0)
                hi1(q, 0)
                gate(g)
                for s in range(1, SLOTS):
                    hi1(q, s)
                conv_first(g, 1)
                hi4(q + 1)
                ffn_split(g)
            hi4(q0 + 1)
            group(0, q0 + 2)
            with act.Fori(0, n - 2) as g:
                group(g + 1, g * 3 + (q0 + 4))
                hi4(g * 3 + (q0 + 6))
            group(n - 1, q0 + 3 * n - 2)
            norm("final", resid)

        @block.vector
        def _(dve):
            step = Steps(dve, dve_steps)

            def lo1(q, s, width=CW):
                dve.wait_ge(hi_ready, q * SLOTS + (s + 1))
                dve.tensor_tensor(wlo[:, s, 0:width], raw[:, s, 0:width], whi[:, s, 0:width].bitcast(F32),
                                  ALU.subtract).then_inc(lo_ready, 1)

            def lo4(q, widths=(CW,) * 4):
                for s in range(SLOTS):
                    lo1(q, s, widths[s])

            def lo4_add(q, q_down, widths=(CW,) * 4):
                for s in range(SLOTS):
                    lo1(q, s, widths[s])
                    add_down(q_down, s)

            def norm(name, src, gain, dst_hi=None, dst_lo=None):
                k = NORM[name]
                n, mean, t0 = NORMS[k][1], NORMS[k][2], PIECE0[k]
                w = min(4, n)
                pieces = range(PIECES[k])
                y = src if mean else norm_tmp(name)
                if mean:
                    dve.wait_ge(norm_mean, k + 1)
                    for p in pieces:
                        s = src[:, p * w:p * w + w, :]
                        dve.tensor_tensor(s, s, norm_ps(name)[1].unsqueeze(1).to_broadcast([P, w, T]), ALU.subtract).then_inc(norm_xc, 1)
                dve.wait_ge(norm_std, k + 1)
                step(dve.reciprocal(rstd[:], std[:]))
                step.settle()

                def lo(p):
                    dve.wait_ge(norm_hi, LO0[k] + p + 1)
                    a = slice(p * w, p * w + w)
                    dve.tensor_tensor(dst_lo[:, a, :], y[:, a, :], dst_hi[:, a, :].bitcast(F32), ALU.subtract).then_inc(norm_lo, 1)
                for p in pieces:
                    for i in range(p * w, p * w + w):
                        ins = dve.scalar_tensor_tensor(out=y[:, i, :], in0=src[:, i, :], scalar=fcol(gain[0], gain[1] + i),
                                                       in1=rstd[:], op0=ALU.mult, op1=ALU.mult)
                    ins.then_inc(norm_scaled if mean else norm_y, 1)
                    if dst_lo is not None and p >= 1:
                        lo(p - 1)
                if dst_lo is not None:
                    lo(PIECES[k] - 1)

            def add_down(q, nb):
                wait_used(dve, q, nb)
                r = resid[:, 4 * nb:4 * nb + 4, :]
                return dve.tensor_tensor(r, r, block_ps(2 + nb % 2), ALU.add).then_inc(down_free, 1)

            def mlp(name, next_quad, next_widths=(CW,) * 4):
                q0, h0 = QUAD[name], HIDDEN[name]
                n = FF // HID

                def split(g, hi=hid_hi, lo=hid_lo):
                    dve.wait_ge(hidden_hi, g + (h0 + 1))
                    dve.tensor_tensor(lo[:], hid[:], hi[:].bitcast(F32), ALU.subtract).then_inc(hidden_lo, 1)

                lo4(q0 + 1)
                split(0)
                with dve.Fori(0, n - 2) as g:
                    lo4(g * 2 + (q0 + 2))
                    lo4_add(g * 2 + (q0 + 3), g * 2 + (q0 + 2))
                    split(g + 1)
                lo4(q0 + 2 * n - 2)
                split(n - 1, last_hi, last_lo)
                lo4_add(q0 + 2 * n - 1, q0 + 2 * n - 2)
                lo4_add(next_quad, q0 + 2 * n - 1, next_widths)

            def add_block(b, nb, q, s=SLOTS - 1):
                wait_used(dve, q, s)
                r = resid[:, 4 * nb:4 * nb + 4, :]
                dve.tensor_tensor(r, r, block_ps(b % 2), ALU.add).then_inc(block_free, 1)

            dve.sem_inc(lo_ready, SLOTS)
            dve.memset(ones[:], 1.0)
            dve.memset(ones_mean[:], 1.0 / D).then_inc(ones_ready, 1)
            dve.memset(win_a[:, :, 0:PAD], 0.0)
            dve.memset(win_b[:, :, 0:PAD], 0.0)
            dve.memset(u_pad[:, :, :, 0:PAD].rearrange("p a n t -> p (a n) t"), 0.0).then_inc(pad_ready, 1)
            def op(out_, a, b_, o):
                step(dve.tensor_tensor(out_, a, b_, o))
                step.settle()

            def reduce_angle(out_, angle, tmp, quarter):
                def ts(o, a, s1, s2, o1, o2=ALU.bypass):
                    step(dve.tensor_scalar(o, a, s1, s2, o1, o2) if s2 is not None else dve.tensor_scalar(o, a, s1, None, o1))
                    step.settle()
                two_pi = 6.283185307179586
                c1 = 6.28125
                c2 = 0.0019350051879882812
                c3 = two_pi - c1 - c2
                magic = 12582912.0
                ts(tmp, angle, 1.0 / two_pi, 0.25 if quarter else 0.0, ALU.mult, ALU.add)
                ts(tmp, tmp, magic, None, ALU.add)
                ts(tmp, tmp, magic, None, ALU.subtract)
                for n, c in enumerate((c1, c2, c3)):
                    step(dve.scalar_tensor_tensor(out=out_, in0=tmp, scalar=-c, in1=angle if n == 0 else out_, op0=ALU.mult, op1=ALU.add))
                    step.settle()
                ts(out_, out_, two_pi / 4 if quarter else 0.0, 3.1415925, ALU.add, ALU.min)
                ts(out_, out_, -3.1415925, None, ALU.max)

            dve.wait_ge(lam_landed, 32)
            lr, li = lam[:, 0, :], lam[:, 1, :]
            dve.wait_ge(trig_ready, 1)
            dt = par[:, 0, :]
            op(par[:, 1, :], lr, dt, ALU.mult)
            dve.sem_inc(angles_ready, 1)
            op(par[:, 4, :], li, dt, ALU.mult)
            for p in range(4):
                a = slice(4 * p, 4 * p + 4)
                dve.wait_ge(x_hi_ready, p + 1)
                dve.tensor_tensor(xlo[:, a, :], resid[:, a, :], xhi[:, a, :].bitcast(F32), ALU.subtract).then_inc(x_lo_ready, 1)

            lo4(0)
            reduce_angle(par[:, 2, :], par[:, 4, :], par[:, 5, :], False)
            dve.sem_inc(angles_ready, 1)
            reduce_angle(par[:, 3, :], par[:, 4, :], par[:, 5, :], True)
            dve.sem_inc(angles_ready, 1)
            dve.wait_ge(trig_ready, 3)
            a_re, a_im, n_re, den, z_re, z_im, nz_im, na_im = (par[:, i, :] for i in (4, 5, 6, 10, 7, 8, 9, 11))
            tmp = par[:, 12, :]
            op(a_re, par[:, 1, :], par[:, 3, :], ALU.mult)
            op(a_im, par[:, 1, :], par[:, 2, :], ALU.mult)
            step(dve.tensor_scalar(n_re, a_re, 1.0, None, ALU.subtract))
            step.settle()
            op(den, lr, lr, ALU.mult)
            op(tmp, li, li, ALU.mult)
            op(den, den, tmp, ALU.add)
            op(z_re, n_re, lr, ALU.mult)
            op(tmp, a_im, li, ALU.mult)
            op(z_re, z_re, tmp, ALU.add)
            op(z_im, a_im, lr, ALU.mult)
            op(tmp, n_re, li, ALU.mult)
            op(z_im, z_im, tmp, ALU.subtract)
            step(dve.reciprocal(den, den))
            step.settle()
            op(z_re, z_re, den, ALU.mult)
            op(z_im, z_im, den, ALU.mult)
            step(dve.tensor_scalar(nz_im, z_im, -1.0, None, ALU.mult))
            step(dve.tensor_scalar(na_im, a_im, -1.0, None, ALU.mult))
            step(dve.tensor_copy(pow_re[:, :, 0], a_re))
            step(dve.tensor_copy(pow_im[:, :, 0], a_im))
            step.settle()

            def rope_tables():
                rope_tmp, rope_angle = std[0:ROPE, :], rstd[0:ROPE, :]
                step(dve.tensor_copy(rope_angle, pos_i))
                step.settle()
                dve.wait_ge(table_landed, 32)
                step(dve.tensor_scalar(rope_angle, rope_angle, ccol("freq", rows=ROPE), None, ALU.mult))
                step.settle()
                reduce_angle(rope_sin[:], rope_angle, rope_tmp, False)
                dve.sem_inc(angles_ready, 1)
                reduce_angle(rope_cos[:], rope_angle, rope_tmp, True)
                dve.sem_inc(angles_ready, 1)

            def hop_powers():
                for n in range(4):
                    if n:
                        re, im = hop_re[n - 1], hop_im[n - 1]
                        op(hop_re[n], re, re, ALU.mult)
                        op(hop_im[n], im, im, ALU.mult)
                        op(hop_re[n], hop_re[n], hop_im[n], ALU.subtract)
                        op(hop_im[n], re, im, ALU.mult)
                        op(hop_im[n], hop_im[n], hop_im[n], ALU.add)
                    step(dve.tensor_scalar(hop_nim[n], hop_im[n], -1.0, None, ALU.mult))
                    step.settle()

            def powers(j0, j1):
                for j in range(j0, j1):
                    op(pow_re[:, :, j], pow_re[:, :, j - 1], a_re, ALU.mult)
                    op(tmp, pow_im[:, :, j - 1], a_im, ALU.mult)
                    op(pow_re[:, :, j], pow_re[:, :, j], tmp, ALU.subtract)
                    op(pow_im[:, :, j], pow_im[:, :, j - 1], a_re, ALU.mult)
                    op(tmp, pow_re[:, :, j - 1], a_im, ALU.mult)
                    op(pow_im[:, :, j], pow_im[:, :, j], tmp, ALU.add)

            def pooled_mean(g):
                dve.wait_ge(summed, g + 1)
                res = (win_a if (4 - g) % 2 else win_b)[:, :, PAD:PAD + T]
                dve.scalar_tensor_tensor(out=res, in0=res, scalar=1.0 / POOL_WINDOWS[3 - g], in1=u_pad[:, g, :, PAD:PAD + T],
                                         op0=ALU.mult, op1=ALU.subtract).then_inc(pooled, 1)

            def pooled_low(g):
                dve.wait_ge(pooled_hi, g + 1)
                res = win_a if (4 - g) % 2 else win_b
                dve.tensor_tensor(pool_lo[:, g % 2], res[:, :, PAD:PAD + T], pool_hi[:, g % 2].bitcast(F32),
                                  ALU.subtract).then_inc(pooled_lo, 1)

            def mixed_low(g):
                grp = 3 - g
                b = BLOCK["pool_group"] + g
                wait_used(dve, QUAD["pool_group"], g)
                for nt in range(4):
                    ins = dve.tensor_scalar(u_pad[:, g, nt, PAD:PAD + T], block_ps(b % 2)[:, nt, :],
                                            fcol("pool_scale", 4 * grp + nt), None, ALU.mult)
                    if nt == 3:
                        ins.then_inc(y_scaled, 1)
                dve.wait_ge(y_hi, g + 1)
                dve.tensor_tensor(xlo[:, 4 * grp:4 * grp + 4, :], u_pad[:, g, :, PAD:PAD + T],
                                  xhi[:, 4 * grp:4 * grp + 4, :].bitcast(F32), ALU.subtract).then_inc(y_lo, 1)
                dve.sem_inc(block_free, 1)
                lo1(QUAD["pool_out"], g)
            lo4(1)
            rope_tables()
            powers(1, 6)
            lo4(2)
            pooled_mean(0)
            pooled_low(0)
            powers(6, 11)
            lo4(3)
            pooled_mean(1)
            pooled_low(1)
            powers(11, SCAN)
            hop_powers()
            dve.sem_inc(table_ready, 1)
            lo4(QUAD["pool_group"])
            dve.wait_ge(table_landed, 32)
            pooled_mean(2)
            mixed_low(0)
            pooled_low(2)
            pooled_mean(3)
            mixed_low(1)
            pooled_low(3)
            mixed_low(2)
            mixed_low(3)
            dve.wait_ge(resid_ready, 4)
            for b in range(4):
                lo4(QUAD["pool_out"] + b + 1)
                add_block(BLOCK["pool_out"] + b, b, QUAD["pool_out"] + b)
            norm("mix0", resid, ("ln_mix_g", 0), xhi, xlo)
            dve.wait_ge(resid_ready, 8)
            mlp("mlp0", QUAD["attn"], ATTN_WIDTHS)
            norm("mlp0", resid, ("ln_mlp_g", 0), xhi, xlo)

            def shift(h):
                dve.wait_ge(scores_done, h + 1)
                for g in range(N_GROUPS):
                    step(dve.scalar_tensor_tensor(
                        out=score[:, g, :], in0=ccol("dist", 384 * g, 384),
                        scalar=const[:, bass.ds(h + (CONST["slope"] + g * N_HEADS), 1)],
                        in1=ps[:, 4 + g, 0:384], op0=ALU.mult, op1=ALU.add))
                step.settle()
                step(dve.tensor_reduce(row_max[:, 0:1], score[:, :, 0:128], AX.XY, ALU.max))
                step(dve.tensor_reduce(row_max[:, 1:2], score[:, :, 128:384], AX.XY, ALU.max))
                step.settle()
                dve.tensor_scalar(row_max[:], row_max[:], -ATTN_SCALE, None, ALU.mult).then_inc(shift_ready, 1)

            def probs(h):
                dve.wait_ge(exp_done, h + 1)
                step(dve.reciprocal(row_den[:], row_den[:]))
                step.settle()
                dve.tensor_scalar(score[:, :, 0:128], score[:, :, 0:128], row_den[:, 0:1], None, ALU.mult)
                dve.tensor_scalar(score[:, :, 128:384], score[:, :, 128:384], row_den[:, 1:2], None, ALU.mult).then_inc(prob_ready, 1)

            def head_low(h):
                dve.wait_ge(head_hi, h + 1)
                dve.tensor_tensor(heads_lo[:, bass.ds(h, 1), :].rearrange("p a t -> p (a t)"), half(7, 0),
                                  heads_hi[:, bass.ds(h, 1), :].rearrange("p a t -> p (a t)").bitcast(F32), ALU.subtract).then_inc(head_lo, 1)

            def attn_head(h, first, last):
                q = h * 3 + QUAD["attn"]
                lo1(q + 1, 0)
                if not first:
                    shift(h - 1)
                lo1(q + 1, 1)
                if not first:
                    probs(h - 1)
                lo1(q + 1, 2)
                lo1(q + 1, 3, ATTN_WIDTHS[3])
                lo4(q + 2, ATTN_WIDTHS)
                lo1(q + 3, 0)
                if not first:
                    head_low(h - 1)
                lo1(q + 3, 1)
                lo1(q + 3, 2)
                lo1(q + 3, 3, CW if last else ATTN_WIDTHS[3])
            attn_head(0, True, False)
            with dve.Fori(0, N_HEADS // 2 - 1) as i:
                step.enter(i, 12)
                attn_head(i * 2 + 1, False, False)
                attn_head(i * 2 + 2, False, False)
                step.leave(N_HEADS // 2 - 1)
            attn_head(N_HEADS - 1, False, True)
            shift(N_HEADS - 1)
            probs(N_HEADS - 1)
            head_low(N_HEADS - 1)
            lo4(QUAD["attn_out"] + 1)
            dve.wait_ge(resid_ready, 12)
            b = BLOCK["attn_out"]
            add_block(b, 0, QUAD["attn_out"], 1)
            add_block(b + 1, 1, QUAD["attn_out"], 3)
            lo4(QUAD["mlp1"])
            add_block(b + 2, 2, QUAD["attn_out"] + 1, 1)
            add_block(b + 3, 3, QUAD["attn_out"] + 1, 3)
            norm("mix1", resid, ("ln_mix_g", DT), xhi, xlo)
            dve.wait_ge(resid_ready, 16)
            mlp("mlp1", QUAD["proj"])
            norm("mlp1", resid, ("ln_mlp_g", DT))
            norm("attn2", resid, ("attn_norm_w_2", 0), xhi, xlo)

            lo4(QUAD["proj"] + 1)
            for b in range(1, 4):
                lo4(QUAD["proj"] + b + 1)

            for hf in range(2):
                for ci in range(4):
                    c = 4 * hf + ci
                    for st in range(4):
                        tile = 4 * c + st
                        dve.wait_ge(bu_part, 4 * c + st + 1)
                        src = ps[:, 4 * ((ci + hf) % 2) + st, :].rearrange("p (r t) -> p r t", r=2)
                        zr = par[:, 7, tile:tile + 1]
                        dve.scalar_tensor_tensor(out=state[:, 0, 4 * ci + st, :], in0=src[:, 0, :], scalar=zr,
                                                 in1=bu_tmp[:, st, 0, :], op0=ALU.mult, op1=ALU.add)
                        ins = dve.scalar_tensor_tensor(out=state[:, 1, 4 * ci + st, :], in0=src[:, 1, :], scalar=zr,
                                                       in1=bu_tmp[:, st, 1, :], op0=ALU.mult, op1=ALU.add)
                    ins.then_inc(bu_ready, 1)
                dve.wait_ge(bu_ready, 4 * hf + 4)
                scan_tiles(dve, step, hf, 0, SCAN_DVE, 4, 3, scan_tmp[:, 0], scan_tmp[:, 1], scan_done)
                for ci in range(4):
                    c = 4 * hf + ci
                    dve.wait_ge(y_done, c + 1)
                    step(dve.scalar_tensor_tensor(out=proj[:, c, :], in0=proj[:, c, :], scalar=fcol("ssm_d_2", c),
                                                  in1=half(ci, 0), op0=ALU.mult, op1=ALU.add))
                    step.settle()
                    step(dve.tensor_tensor(proj[:, c, :], proj[:, c, :], half(ci, 1), ALU.subtract))
                step.settle()
                dve.sem_inc(y_ready, 1)
            k = 2.0 * (2.0 / 3.141592653589793) ** 0.5
            for hf in range(2):
                dve.wait_ge(gelu_sq, hf + 1)
                step(dve.tensor_scalar(gelu_tmp(hf), gelu_tmp(hf), 0.044715 * k, k, ALU.mult, ALU.add))
                step.settle()
                dve.tensor_tensor(gelu_tmp(hf), gelu_tmp(hf), proj[:, 4 * hf:4 * hf + 4, :], ALU.mult).then_inc(gelu_arg, 1)
            for hf in range(2):
                u = proj[:, 4 * hf:4 * hf + 4, :]
                dve.wait_ge(gelu_sig, hf + 1)
                dve.tensor_tensor(u, u, gelu_tmp(hf), ALU.mult).then_inc(gelu_ready, 1)
            for hf in range(2):
                a = slice(4 * hf, 4 * hf + 4)
                dve.wait_ge(gelu_hi, hf + 1)
                dve.tensor_tensor(xlo[:, a, :], proj[:, a, :], xhi[:, a, :].bitcast(F32), ALU.subtract).then_inc(gelu_lo, 1)
            norm("q", proj[:, 8:12, :], ("mla_q_norm_w_2", 0), cq_hi, cq_lo)
            norm("kv", proj[:, 12:14, :], ("mla_kv_norm_w_2", 0), ckv_hi, ckv_lo)

            def rope(n, dst):
                dve.wait_ge(rope_done, n + 1)
                step(dve.tensor_tensor(rope_a, ps[0:ROPE, 7, 0:T], rope_cos[:], ALU.mult))
                step(dve.tensor_tensor(dst, ps[0:ROPE, 7, T:2 * T], rope_sin[:], ALU.mult))
                step.settle()
                dve.tensor_tensor(dst, dst, rope_a, ALU.add).then_inc(rope_ready, 1)

            dve.wait_ge(trig_ready, 4)
            rope(0, k_rope)

            def glu(b):
                a = slice(4 * b, 4 * b + 4)
                dve.wait_ge(glu_sig, b + 1)
                dve.tensor_tensor(proj[:, a, :], proj[:, a, :], scratch[:, a, :], ALU.mult).then_inc(block_free, 1)
            glu(0)
            lo1(QUAD["mla"], 0)
            lo1(QUAD["mla"], 1)
            glu(1)
            lo1(QUAD["mla"], 2)
            lo1(QUAD["mla"], 3)

            def mla_head(h, q, s):
                dve.wait_ge(m_score, h + 1)
                step(dve.tensor_tensor(m_prob_buf[:, 0:384], ps[:, 3, 0:384], ccol("causal"), ALU.add))
                step.settle()
                step(dve.tensor_reduce(m_max[:, 0:1], m_prob_buf[:, 0:128], AX.X, ALU.max))
                step(dve.tensor_reduce(m_max[:, 1:2], m_prob_buf[:, 128:384], AX.X, ALU.max))
                step.settle()
                dve.tensor_scalar(m_max[:], m_max[:], -MLA_SCALE, None, ALU.mult).then_inc(m_shift, 1)
                if s < SLOTS - 1:
                    rope(h + 2, m_buf(s + 1, 4, 5)[0:ROPE, :])
                dve.wait_ge(m_exp, h + 1)
                step(dve.reciprocal(m_den[:], m_den[:]))
                step.settle()
                dve.tensor_scalar(m_prob_buf[:, 0:128], m_prob_buf[:, 0:128], m_den[:, 0:1], None, ALU.mult)
                dve.tensor_scalar(m_prob_buf[:, 128:384], m_prob_buf[:, 128:384], m_den[:, 1:2], None, ALU.mult).then_inc(m_prob, 1)
                lo1(q + 1, s)
            with dve.Fori(0, 2) as i:
                step.enter(i, SLOTS * 6)
                rope(i * 4 + 1, m_buf(0, 4, 5)[0:ROPE, :])
                for s in range(SLOTS):
                    mla_head(i * 4 + s, i + QUAD["mla"], s)
                step.leave(2)
            norm("ssm", proj[:, 0:8, :], ("ssm_out_norm_w_2", 0), xhi, xlo)
            norm("mla", scratch[:, 0:8, :], ("mla_out_norm_w_2", 0), xhi[:, 8:16, :], xlo[:, 8:16, :])
            for b in range(4):
                lo4(QUAD["out2"] + b + 1)
                add_block(BLOCK["out2"] + b, b, QUAD["out2"] + b)
            norm("ffn2", resid, ("ffn_norm_w_2", 0), xhi, xlo)

            q0, h0, n = QUAD["ffn"], HIDDEN["ffn"], FF2 // HID

            def conv_rest(g, half_):
                dve.wait_ge(conv_start, g * 2 + (half_ + 1))
                for lag, tap in ((1, 1), (2, 0)):
                    for nt in range(4):
                        i = g * 4 + (half_ * (FF2 // P) + nt)
                        o = conv[:, 4 * half_ + nt, lag:T]
                        ins = dve.scalar_tensor_tensor(out=o, in0=block_ps(half_)[:, nt, 0:T - lag],
                                                       scalar=fcol("ffn_conv_w_2", i + tap * (2 * FF2 // P)), in1=o,
                                                       op0=ALU.mult, op1=ALU.add)
                        if lag == 1:
                            step(ins)
                    if lag == 1:
                        step.settle()
                ins.then_inc(conv_done, 1)
                dve.wait_ge(conv_done, g * 2 + (half_ + 1))
                dve.sem_inc(block_free, 1)

            def group(g, q, adds):
                conv_rest(g, 0)
                lo1(q, 0)
                dve.wait_ge(sig_ready, g + 1)
                if not (isinstance(g, int) and g == 0):
                    dve.wait_ge(hidden_lo, g + h0)
                step(dve.tensor_tensor(hid[:], conv[:, 0:4, :], gate_sig[:], ALU.mult))
                for s in range(1, SLOTS):
                    lo1(q, s)
                conv_rest(g, 1)
                for s in range(SLOTS):
                    lo1(q + 1, s)
                    if adds:
                        add_down(q, s)
                    if s == 0:
                        step.settle()
                        dve.tensor_tensor(hid[:], hid[:], conv[:, 4:8, :], ALU.mult).then_inc(hidden_ready, 1)
                dve.wait_ge(hidden_hi, g + (h0 + 1))
                dve.tensor_tensor(hid_lo[:], hid[:], hid_hi[:].bitcast(F32), ALU.subtract).then_inc(hidden_lo, 1)
            lo4(q0 + 1)
            group(0, q0 + 2, False)
            with dve.Fori(0, n - 2) as g:
                step.enter(g, 9)
                group(g + 1, g * 3 + (q0 + 4), True)
                lo4(g * 3 + (q0 + 6))
                step.leave(n - 2)
            group(n - 1, q0 + 3 * n - 2, True)
            for nb in range(4):
                add_down(q0 + 3 * n - 1, nb)
            norm("final", resid, ("final_norm_w_2", 0))

        @block.gpsimd
        def _(pool):
            step = Steps(pool, pool_steps)
            pool.wait_ge(pad_ready, 1)
            pool.wait_ge(table_landed, 32)
            for g in range(4):
                grp = 3 - g
                w = POOL_WINDOWS[grp]
                pool.wait_ge(block_free, 2 + g + 1)
                src, shift = u_pad[:, g], 1
                bufs = (win_a, win_b)
                if g >= 1:
                    pool.wait_ge(pooled_lo, g)
                n = 0
                while shift < w:
                    dst = bufs[n % 2]
                    step(pool.tensor_tensor(dst[:, :, PAD:PAD + T], src[:, :, PAD:PAD + T],
                                            src[:, :, PAD - shift:PAD - shift + T], ALU.add))
                    step.settle()
                    src, shift, n = dst, shift * 2, n + 1
                assert (src is win_a) == ((4 - g) % 2 == 1)
                head = src[:, :, PAD:2 * PAD]
                pool.tensor_tensor(head, head, ccol("count", PAD * grp, PAD).unsqueeze(1).to_broadcast([P, 4, PAD]),
                                   ALU.mult).then_inc(summed, 1)
            for n in range(16):
                hf, kind, ci = n // 8, (n // 4) % 2, n % 4
                if n == 0:
                    pool.wait_ge(norm_lo, LO0[NORM["attn2"]] + 4)
                elif kind == 1:
                    pool.wait_ge(bu_done, 4 * hf + ci + 1)
                elif n >= 8:
                    pool.wait_ge(y_done, ci + 1)
                pool.dma_start(blocks[:, ci, :], ssm_blocks[n]).then_inc(blocks_landed[ci], 16)
                if n % 8 == 7:
                    pool.wait_ge(bu_ready, 4 * hf + 4)
                    scan_tiles(pool, step, hf, SCAN_DVE, 16 - SCAN_DVE, 1, 1, std, rstd, scan_rest_done)

        @block.tensor
        def _(pe):
            pe.sem_inc(chunk_used, SLOTS)
            pe.sem_inc(block_free, 2)
            pe.sem_inc(down_free, 2)
            pe.sem_inc(head_lo, 1)

            def chunk(q, s):
                pe.wait_ge(lo_ready, q * SLOTS + (SLOTS + s + 1))

            def three(o, w_hi, w_lo, x_hi, x_lo, first, last):
                pe.matmul(o, w_hi, x_hi, start=first, stop=False)
                pe.matmul(o, w_hi, x_lo, start=False, stop=False)
                return pe.matmul(o, w_lo, x_hi, start=False, stop=last)

            def tile(o, s, off, stride, kts, xh, xl, x_ready=None):
                for k in range(kts):
                    if x_ready is not None and k % 4 == 0:
                        pe.wait_ge(x_ready[0], x_ready[1] + k // 4 + 1)
                    c = slice(off + k * stride, off + k * stride + P)
                    ins = three(o, whi[:, s, c], wlo[:, s, c], xh[:, k, :], xl[:, k, :], k == 0, k == kts - 1)
                return ins

            def quad_block(q, set_, free, x_ready=None, tiles=4, order=range(DT)):
                pe.wait_ge(block_free, free)
                for s in range(tiles):
                    chunk(q, s if s < tiles - 1 else SLOTS - 1)
                    o = block_ps(set_)[:, s, :]
                    for n, k in enumerate(order):
                        if s == 0 and x_ready is not None and n % 4 == 0:
                            pe.wait_ge(x_ready[0], x_ready[1] + n // 4 + 1)
                        c = slice(k * P, k * P + P)
                        ins = three(o, whi[:, s, c], wlo[:, s, c], xhi[:, k, :], xlo[:, k, :], n == 0, n == DT - 1)
                    if s < tiles - 1:
                        ins.then_inc(chunk_used, 1)
                ins.then_inc(chunk_used, 1 + SLOTS - tiles)

            def norm(name, src):
                k = NORM[name]
                n, mean, t0 = NORMS[k][1], NORMS[k][2], PIECE0[k]
                w = min(4, n)
                if mean:
                    for i in range(n):
                        if i % w == 0:
                            pe.wait_ge(*source[name][i // w])
                        ins = pe.matmul(norm_ps(name)[1], ones_mean[:], src[:, i, :], start=i == 0, stop=i == n - 1)
                    ins.then_inc(norm_mean, 1)
                for p in range(PIECES[k]):
                    pe.wait_ge(norm_sq, t0 + p + 1)
                    for i in range(p * w, p * w + w):
                        ins = pe.matmul(norm_ps(name)[0], ones[:], norm_tmp(name)[:, i, :], start=i == 0, stop=i == n - 1)
                ins.then_inc(norm_var, 1)

            def down(q, m, hidden, hi=hid_hi, lo=hid_lo):
                pe.wait_ge(hidden_lo, hidden)
                for s in range(SLOTS):
                    chunk(q, s)
                    pe.wait_ge(down_free, m + (s + 1))
                    for nt in range(4):
                        ins = tile(block_ps(2 + s % 2)[:, nt, :], s, nt * P, 512, 4, hi, lo)
                    ins.then_inc(chunk_used, 1)

            def mlp(name):
                q0, b0, h0, n = QUAD[name], BLOCK[name], HIDDEN[name], FF // HID

                def up(g, x_ready=None):
                    quad_block(q0 if isinstance(g, int) else g * 2 + (q0 - 1), 0, g + (b0 + 2), x_ready)
                up(0, (norm_lo, LO0[NORM["mix" + name[-1]]]))
                with pe.Fori(0, n - 1) as g:
                    up(g + 1)
                    down(g * 2 + (q0 + 2), g * 4 + 4 * h0, g + (h0 + 1))
                down(q0 + 2 * n - 1, 4 * (h0 + n - 1), h0 + n, last_hi, last_lo)

            pe.wait_ge(ones_ready, 1)
            for b in range(4):
                quad_block(b, b % 2, b + 1, (x_lo_ready, 0) if b == 0 else None)
            for g in range(4):
                b = BLOCK["pool_group"] + g
                pe.wait_ge(pooled_lo, g + 1)
                pe.wait_ge(block_free, b + 1)
                chunk(QUAD["pool_group"], g)
                for nt in range(4):
                    ins = tile(block_ps(b % 2)[:, nt, :], g, nt * P, 512, 4, pool_hi[:, g % 2], pool_lo[:, g % 2])
                ins.then_inc(chunk_used, 1)
            for b in range(4):
                n = BLOCK["pool_out"] + b
                quad_block(QUAD["pool_out"] + b, n % 2, n + 1, (y_lo, 0) if b == 0 else None,
                           order=[4 * grp + i for grp in (3, 2, 1, 0) for i in range(4)])
            norm("mix0", resid)
            mlp("mlp0")
            norm("mlp0", resid)


            pe.wait_ge(table_landed, 32)

            def qkv(h, odd, g, part):
                n = h * 3 + g
                q = n + QUAD["attn"]
                b = 2 * ((odd + g) % 2)
                if part == 0 and not (isinstance(h, int) and n < 2):
                    pe.wait_ge(qkv_copied, n - 1)
                if part == 2 and not (isinstance(h, int) and n < 2):
                    pe.wait_ge(v_ready, n - 1)
                chunk(q, part if part < 2 else 3)
                first = isinstance(h, int) and n + part == 0
                tile(half(b + part // 2, part % 2), part, 0, P, DT, xhi, xlo,
                     (norm_lo, LO0[NORM["mlp0"]]) if first else None).then_inc(chunk_used, 1 if part < 2 else 2)

            def turn_v(h, odd, g):
                pe.wait_ge(qkv_copied, h * 3 + (g + 1))
                b = 2 * ((odd + g) % 2)
                for kt in range(2):
                    ins = pe.transpose(ps[:, b + 1, T + kt * P:T + kt * P + P], qkv_t[:, g, 2, kt * P:kt * P + P], ccol("ident"))
                ins.then_inc(v_turned, 1)

            def scores(h):
                pe.wait_ge(qkv_copied, h * 3 + 3)
                for g in range(N_GROUPS):
                    pe.matmul(ps[:, 4 + g, 0:128], qkv_t[:, g, 0, 0:128], qkv_t[:, g, 1, 0:128], start=True, stop=True)
                    ins = pe.matmul(ps[:, 4 + g, 128:384], qkv_t[:, g, 0, 128:256], qkv_t[:, g, 1, :], start=True, stop=True)
                ins.then_inc(scores_done, 1)

            def turn(h):
                pe.wait_ge(prob_ready, h + 1)
                for g in range(N_GROUPS):
                    for b in range(3):
                        ins = pe.transpose(ps[:, 4 + g, b * P:(b + 1) * P], score[:, g, b * P:(b + 1) * P], ccol("ident"))
                ins.then_inc(turned, 1)

            def mix(h, odd):
                pe.wait_ge(turned_copied, h + 1)
                pe.wait_ge(v_ready, h * 3 + 3)
                pe.wait_ge(head_lo, h + 1)
                for g in range(N_GROUPS):
                    pe.matmul(ps[:, 7, 0:128], v_rows[:, odd, g, 0], prob_t[:, g, 0:128], start=g == 0, stop=g == 2)
                for g in range(N_GROUPS):
                    for kt in range(2):
                        ins = pe.matmul(ps[:, 7, 128:256], v_rows[:, odd, g, kt], prob_t[:, g, 128 + 128 * kt:256 + 128 * kt],
                                        start=g + kt == 0, stop=g + kt == 3)
                ins.then_inc(head_done, 1)

            def attn_head(h, odd, first):
                qkv(h, odd, 0, 0)
                if not first:
                    turn_v(h - 1, 1 - odd, 2)
                    scores(h - 1)
                qkv(h, odd, 0, 1)
                qkv(h, odd, 0, 2)
                qkv(h, odd, 1, 0)
                turn_v(h, odd, 0)
                if not first:
                    turn(h - 1)
                qkv(h, odd, 1, 1)
                qkv(h, odd, 1, 2)
                qkv(h, odd, 2, 0)
                if not first:
                    mix(h - 1, 1 - odd)
                turn_v(h, odd, 1)
                qkv(h, odd, 2, 1)
                qkv(h, odd, 2, 2)
            attn_head(0, 0, True)
            with pe.Fori(0, N_HEADS // 2 - 1) as i:
                attn_head(i * 2 + 1, 1, False)
                attn_head(i * 2 + 2, 0, False)
            attn_head(N_HEADS - 1, 1, False)
            turn_v(N_HEADS - 1, 1, 2)
            scores(N_HEADS - 1)
            turn(N_HEADS - 1)
            mix(N_HEADS - 1, 1)
            pe.wait_ge(head_lo, 1 + N_HEADS)
            for b in range(4):
                n = BLOCK["attn_out"] + b
                q = QUAD["attn_out"] + b // 2
                pe.wait_ge(block_free, n + 1)
                for s2 in range(2):
                    s = 2 * (b % 2) + s2
                    chunk(q, s)
                    for j in range(2):
                        ins = tile(block_ps(n % 2)[:, 2 * s2 + j, :], s, j * P, 256, 8, heads_hi, heads_lo)
                    ins.then_inc(chunk_used, 1)
            norm("mix1", resid)
            mlp("mlp1")
            norm("mlp1", resid)
            norm("attn2", resid)

            for b in range(4):
                n = BLOCK["proj"] + b
                quad_block(QUAD["proj"] + b, n % 2, n + 1, (norm_lo, LO0[NORM["attn2"]]) if b == 0 else None, 3 if b == 3 else 4)
            for hf in range(2):
                pe.wait_ge(block_free, 2 + BLOCK["proj"] + 4)
                for ci in range(4):
                    c = 4 * hf + ci
                    pe.wait_ge(blocks_landed[ci], 32 * hf + 16)
                    if c >= 2:
                        pe.wait_ge(bu_ready, c - 1 if c != 4 else 4)
                    if hf and ci == 1:
                        pe.wait_ge(y_ready, 1)
                    for st in range(4):
                        for r in range(2):
                            ins = pe.matmul(half(4 * ((ci + hf) % 2) + st, r), blocks[:, ci, r * 512 + st * P:r * 512 + st * P + P],
                                            proj[:, c, :], start=True, stop=True)
                    ins.then_inc(bu_done, 1)
                for ci in range(4):
                    pe.wait_ge(blocks_landed[ci], 32 * hf + 32)
                    if ci < SCAN_DVE // 4:
                        pe.wait_ge(scan_done, SCAN_DVE // 4 * hf + ci + 1)
                    else:
                        pe.wait_ge(scan_rest_done, (16 - SCAN_DVE) * (hf + 1))
                    for r in range(2):
                        for st in range(4):
                            ins = pe.matmul(half(ci, r), blocks[:, ci, r * 512 + st * P:r * 512 + st * P + P],
                                            state[:, r, 4 * ci + st, :], start=st == 0, stop=st == 3)
                    ins.then_inc(y_done, 1)
            def rope(src):
                pe.matmul(ps[0:ROPE, 7, 0:T], ccol("sel"), src, start=True, stop=True)
                pe.matmul(ps[0:ROPE, 7, T:2 * T], ccol("rot"), src, start=True, stop=True).then_inc(rope_done, 1)

            pe.wait_ge(gelu_lo, 2)
            for s in range(SLOTS):
                chunk(QUAD["glu"], s)
                for j in range(2):
                    ins = tile(block_ps(s // 2)[:, 2 * (s % 2) + j, :], s, j * P, 256, 8, xhi, xlo)
                ins.then_inc(chunk_used, 1)
                if s == 0:
                    norm("q", proj[:, 8:12, :])
                if s == 2:
                    norm("kv", proj[:, 12:14, :])
                    rope(proj[:, 14, :])

            def project_q(i, s):
                chunk(i + QUAD["mla"], s)
                for j in range(2):
                    ins = tile(half(0, j), s, j * ROPE, 192, 4, cq_hi, cq_lo)
                ins.then_inc(m_q, 1)

            def project_kv(s):
                tile(half(1, 0), s, 768, 256, 2, ckv_hi, ckv_lo)
                for tt in range(2):
                    o = ps[:, 1, T + tt * HD:T + (tt + 1) * HD]
                    for k in range(2):
                        c, t = slice(768 + k * 256 + P, 768 + k * 256 + 256), slice(tt * P, tt * P + P)
                        pe.matmul(o, ckv_hi[:, k, t], whi[:, s, c], start=k == 0, stop=False)
                        pe.matmul(o, ckv_hi[:, k, t], wlo[:, s, c], start=False, stop=False)
                        ins = pe.matmul(o, ckv_lo[:, k, t], whi[:, s, c], start=False, stop=k == 1)
                ins.then_inc(chunk_used, 1)

            def rope_q(h, s):
                pe.wait_ge(m_q_copied, h + 1)
                rope(m_buf(s, 1, 2))

            def mla_scores(h, s):
                pe.wait_ge(m_kv_copied, h + 1)
                pe.wait_ge(rope_ready, h + 2)
                q, k, turned_q = m_buf(s, 0, 1), m_buf(s, 2, 3), m_buf(s, 4, 5)
                for qt in range(2):
                    o = ps[:, 3, 128 * qt:128 + 256 * qt]
                    t, keys = slice(qt * P, qt * P + P), slice(0, P + P * qt)
                    pe.matmul(o, q[:, t], k[:, keys], start=True, stop=False)
                    ins = pe.matmul(o, turned_q[0:ROPE, t], k_rope[:, keys], start=False, stop=True)
                ins.then_inc(m_score, 1)

            def mla_mix(h, s):
                pe.wait_ge(m_prob, h + 1)
                for b in range(3):
                    ins = pe.transpose(ps[:, 4, b * P:(b + 1) * P], m_prob_buf[:, b * P:(b + 1) * P], ccol("ident"))
                ins.then_inc(m_turned, 1)
                pe.wait_ge(m_pt, h + 1)
                pt, v = m_turned_buf, m_buf(s, 3, 4)
                pe.matmul(ps[:, 5, 0:128], v[:, 0:HD], pt[:, 0:128], start=True, stop=True)
                pe.matmul(ps[:, 5, 128:256], v[:, 0:HD], pt[:, 128:256], start=True, stop=False)
                pe.matmul(ps[:, 5, 128:256], v[:, HD:2 * HD], pt[:, 256:384], start=False, stop=True).then_inc(m_out, 1)
            pe.wait_ge(norm_lo, LO0[NORM["kv"]] + 1)
            pe.wait_ge(rope_ready, 1)
            with pe.Fori(0, 2) as i:
                project_q(i, 0)
                project_kv(0)
                rope_q(i * 4, 0)
                for s in range(SLOTS):
                    h = i * 4 + s
                    if s < SLOTS - 1:
                        project_q(i, s + 1)
                    mla_scores(h, s)
                    if s < SLOTS - 1:
                        project_kv(s + 1)
                        rope_q(h + 1, s + 1)
                    mla_mix(h, s)
            norm("ssm", proj[:, 0:8, :])
            norm("mla", scratch[:, 0:8, :])
            for b in range(4):
                n = BLOCK["out2"] + b
                quad_block(QUAD["out2"] + b, n % 2, n + 1, (norm_lo, LO0[NORM["ssm"]]) if b == 0 else None)
            norm("ffn2", resid)

            q0, b0, h0, n = QUAD["ffn"], BLOCK["ffn"], HIDDEN["ffn"], FF2 // HID

            def up(g, quad, x_ready=None):
                for i in range(2):
                    quad_block(quad + i, i, g * 2 + (b0 + i + 1), x_ready if i == 0 else None)
            up(0, q0, (norm_lo, LO0[NORM["ffn2"]]))
            with pe.Fori(0, n - 1) as g:
                up(g + 1, g * 3 + (q0 + 2))
                down(g * 3 + (q0 + 4), g * 4 + 4 * h0, g + (h0 + 1))
            down(q0 + 3 * n - 1, 4 * (h0 + n - 1), h0 + n)
            norm("final", resid)


def shape_constants():
    import numpy as np
    t = np.zeros((P, N_CONST), np.float32)

    def put(name, a):
        t[:a.shape[0], CONST[name]:CONST[name] + a.shape[1]] = a
    put("ident", np.eye(P))
    far = 1e37
    lag = np.arange(T)[:, None] - np.arange(T)[None, :]
    for g, (window, dil) in enumerate(((128, 1), (512, 4), (2048, 16))):
        ok = (lag >= 0) & (lag <= window) & (lag % dil == 0)
        d = np.where(ok, lag, far)
        t[:, CONST["dist"] + 384 * g:CONST["dist"] + 384 * g + 128] = d[:P, :P]
        t[:, CONST["dist"] + 384 * g + 128:CONST["dist"] + 384 * g + 384] = d[P:, :]
    c = np.where(lag >= 0, 0.0, -far)
    put("causal", np.concatenate([c[:P, :P], c[P:, :]], axis=1))
    n = N_GROUPS * N_HEADS
    put("slope", np.broadcast_to(-np.exp2(-8.0 * np.arange(1, n + 1) / n) / ATTN_SCALE, (P, n)))
    sel, rot, h = np.zeros((P, ROPE)), np.zeros((P, ROPE)), ROPE // 2
    for i in range(ROPE):
        sel[ROPE + i, i] = 1.0
    for i in range(h):
        rot[ROPE + h + i, i] = -1.0
        rot[ROPE + i, h + i] = 1.0
    put("sel", sel)
    put("rot", rot)
    put("count", np.broadcast_to(np.concatenate([w / np.minimum(np.arange(1, PAD + 1), w) for w in POOL_WINDOWS]), (P, 4 * PAD)))
    f = 10000.0 ** (-np.arange(0, ROPE, 2) / ROPE)
    put("freq", np.concatenate([f, f])[:, None])
    t[:, CONST["ln_eps"]] = LN_EPS
    t[:, CONST["rms_eps"]] = RMS_EPS
    return t


def pack_weights(i):
    import numpy as np

    def columns(w, kts=DT):
        n = CW // kts
        return w.reshape(kts, P, -1, n).transpose(2, 1, 0, 3).reshape(-1, P, CW)

    def rows(w):
        return w.reshape(-1, 4, P, w.shape[1] // 512, 512).transpose(0, 3, 2, 1, 4).reshape(-1, P, CW)

    def mlp(up, down):
        u, d = columns(up).reshape(-1, 4, P, CW), rows(down).reshape(-1, 4, P, CW)
        parts = [u[0]]
        for g in range(len(u) - 1):
            parts += [u[g + 1], d[g]]
        return np.concatenate(parts + [d[-1]])

    def ffn(up, down):
        u, d = columns(up).reshape(2, -1, 4, P, CW), rows(down).reshape(-1, 4, P, CW)
        n = len(d)
        parts = [u[0, 0], u[1, 0]]
        for g in range(n - 1):
            parts += [u[0, g + 1], u[1, g + 1], d[g]]
        return np.concatenate(parts + [d[-1]])
    parts = [columns(i["pool_w_in"][0]).reshape(4, 4, P, CW)[::-1].reshape(-1, P, CW),
             np.concatenate([rows(i["pool_w_group"][0, 3 - g]) for g in range(4)]),
             columns(i["pool_w_out"][0]), mlp(i["mlp_w_up"][0], i["mlp_w_down"][0])]
    qkv = columns(i["attn_w_qkv"][0]).reshape(3, N_GROUPS, N_HEADS, P, CW).transpose(2, 1, 0, 3, 4)
    attn = np.zeros((N_HEADS, N_GROUPS, 4, P, CW), np.float32)
    attn[:, :, 0:3] = qkv
    parts += [attn.reshape(-1, P, CW), columns(i["attn_w_out"][0], 8), mlp(i["mlp_w_up"][1], i["mlp_w_down"][1])]
    w = i["w_in_2"][0]
    parts += [columns(w[:, 0:1792]), columns(w[:, 1728:1856]), np.zeros((1, P, CW), np.float32), columns(i["ssm_w_glu_2"][0], 8)]
    mla = np.zeros((N_HEADS, P, CW), np.float32)
    mla[:, :, 0:768] = i["mla_w_uq_2"][0].reshape(4, P, N_HEADS, 192).transpose(2, 1, 0, 3).reshape(N_HEADS, P, 768)
    mla[:, :, 768:1280] = i["mla_w_ukv_2"][0].reshape(2, P, N_HEADS, 256).transpose(2, 1, 0, 3).reshape(N_HEADS, P, 512)
    parts += [mla, columns(i["w_out_2"][0]), ffn(i["ffn_w_up_2"][0], i["ffn_w_down_2"][0])]
    return np.concatenate(parts)


def pack_ssm(i):
    import numpy as np
    t = np.zeros((2, 2, 4, P, 2, 4, P), np.float32)
    for r, part in enumerate(("re", "im")):
        b, c = i[f"ssm_b_{part}_2"][0], i[f"ssm_c_{part}_2"][0]
        for g in range(64):
            hf, ci, st, h = g // 32, (g // 8) % 4, (g // 2) % 4, g % 2
            ch, state = slice(g % 8 * 16, g % 8 * 16 + 16), slice(64 * h, 64 * h + 64)
            t[hf, 0, ci, ch, r, st, state] = b[g].T
            t[hf, 1, ci, state, r, st, ch] = c[g].T
    return t.reshape(16, P, 1024)


def kernel(**inputs):
    import numpy as np
    import concourse.bacc as bacc
    from concourse.bass_utils import run_bass_kernel_spmd as run

    i = {k: np.asarray(v) for k, v in inputs.items()}
    lam = np.stack([i["ssm_lambda_re_2"].reshape(32, P), i["ssm_lambda_im_2"].reshape(32, P),
                    np.repeat(i["ssm_log_dt_2"].reshape(64), 64).reshape(32, P)])
    arrays = {
        "x_t": i["x"][0].T,
        "weights": pack_weights(i),
        "ssm_blocks": pack_ssm(i),
        "features": np.concatenate([i[n].reshape(-1, P) for n, _ in FEATURES]).T,
        "consts": shape_constants(),
        "ssm_lam": lam.transpose(2, 0, 1),
        "positions": i["positions_2"].reshape(T),
    }
    arrays = {k: np.ascontiguousarray(v) for k, v in arrays.items()}
    nc = bacc.Bacc("TRN2", target_bir_lowering=False, num_devices=1)
    args = [nc.dram_tensor(k, v.shape, mybir.dt.from_np(v.dtype), kind="ExternalInput").ap() for k, v in arrays.items()]
    out = nc.dram_tensor("out", (D, T), F32, kind="ExternalOutput").ap()
    build(nc, *args, out)
    r = run(nc, [arrays], core_ids=[0])
    return np.ascontiguousarray(r.results[0]["out"].T)[None]
```
